# Optimizing a Trainium2 kernel written in Bass

```python
import math
import jax, jax.numpy as jnp
from jax import lax
import numpy as np

D_MODEL = 1024
BATCH = 1
SEQ = 256
DEPTH = 1

N_META = 16
BLOCK_Q = 128
EPS = 1e-6

MLA_HEADS = 8
MLA_Q_RANK = 256
MLA_KV_RANK = 256
MLA_NOPE_DIM = 64
MLA_ROPE_DIM = 32
MLA_V_DIM = 64
MLA_QK_DIM = MLA_NOPE_DIM + MLA_ROPE_DIM
ROPE_THETA = 10000.0

DIFF_HEADS = 4
DIFF_HEAD_DIM = 64
DIFF_V_DIM = 2 * DIFF_HEAD_DIM
DIFF_QK_WIDTH = DIFF_HEADS * 2 * DIFF_HEAD_DIM
DIFF_V_WIDTH = DIFF_HEADS * DIFF_V_DIM

NUM_BUCKETS = 32
MAX_DISTANCE = 128

_S1 = MLA_Q_RANK
_S2 = _S1 + MLA_KV_RANK
_S3 = _S2 + MLA_ROPE_DIM
_S4 = _S3 + DIFF_QK_WIDTH
_S5 = _S4 + DIFF_QK_WIDTH
IN_WIDTH = _S5 + DIFF_V_WIDTH
IN_SPLITS = (_S1, _S2, _S3, _S4, _S5)
MIX_WIDTH = MLA_HEADS * MLA_V_DIM + DIFF_V_WIDTH

PEER_HEADS = 8
PEER_N_KEYS = 128
PEER_N_EXPERTS = PEER_N_KEYS * PEER_N_KEYS
PEER_TOPK = 16
PEER_QUERY_DIM = 256
PEER_SUBKEY_DIM = PEER_QUERY_DIM // 2
PEER_CHUNK = 128


def _rms_norm(x, gain):
    xf = x.astype(jnp.float32)
    y = xf * lax.rsqrt(jnp.mean(xf * xf, axis=-1, keepdims=True) + EPS)
    return (y * gain.astype(jnp.float32)).astype(x.dtype)

def _rope(t, pos):
    half = t.shape[-1] // 2
    inv_freq = ROPE_THETA ** (-jnp.arange(half, dtype=jnp.float32) / half)
    ang = pos.astype(jnp.float32)[:, None] * inv_freq[None, :]
    cos = jnp.cos(ang)[:, None, :].astype(t.dtype)
    sin = jnp.sin(ang)[:, None, :].astype(t.dtype)
    t1, t2 = t[..., :half], t[..., half:]
    return jnp.concatenate([t1 * cos - t2 * sin, t1 * sin + t2 * cos], axis=-1)

def _t5_bucket(dist):
    n = jnp.maximum(dist, 0)
    max_exact = NUM_BUCKETS // 2
    nf = jnp.maximum(n, 1).astype(jnp.float32)
    large = max_exact + (jnp.log(nf / max_exact) / math.log(MAX_DISTANCE / max_exact)
                         * (NUM_BUCKETS - max_exact)).astype(jnp.int32)
    large = jnp.minimum(large, NUM_BUCKETS - 1)
    return jnp.where(n < max_exact, n, large)

def _causal_softmax(logits, q_pos, k_pos):
    mask = k_pos[None, :] <= q_pos[:, None]
    logits = jnp.where(mask, logits.astype(jnp.float32), -1e30)
    return jax.nn.softmax(logits, axis=-1)

def _to_blocks(t):
    b, l = t.shape[0], t.shape[1]
    t = t.reshape((b, l // BLOCK_Q, BLOCK_Q) + t.shape[2:])
    return jnp.moveaxis(t, 1, 0)

def _from_blocks(t):
    t = jnp.moveaxis(t, 0, 1)
    return t.reshape((t.shape[0], t.shape[1] * t.shape[2]) + t.shape[3:])

def _mla(c_q, c_kv, k_rope, q_norm, w_uq, kv_norm, w_ukv, qk_norm_q, qk_norm_k, pos):
    b, l, _ = c_q.shape
    q = (_rms_norm(c_q, q_norm) @ w_uq).reshape(b, l, MLA_HEADS, MLA_QK_DIM)
    kv = (_rms_norm(c_kv, kv_norm) @ w_ukv).reshape(b, l, MLA_HEADS, MLA_NOPE_DIM + MLA_V_DIM)
    k_nope, v = kv[..., :MLA_NOPE_DIM], kv[..., MLA_NOPE_DIM:]
    k_r = jnp.broadcast_to(k_rope[:, :, None, :], (b, l, MLA_HEADS, MLA_ROPE_DIM))
    k = jnp.concatenate([k_nope, k_r], axis=-1)
    q = _rms_norm(q, qk_norm_q)
    k = _rms_norm(k, qk_norm_k)
    q = jnp.concatenate([q[..., :MLA_NOPE_DIM], _rope(q[..., MLA_NOPE_DIM:], pos)], axis=-1)
    k = jnp.concatenate([k[..., :MLA_NOPE_DIM], _rope(k[..., MLA_NOPE_DIM:], pos)], axis=-1)
    scale = MLA_QK_DIM ** -0.5

    def block(args):
        q_start, qb = args
        q_pos = q_start + jnp.arange(BLOCK_Q, dtype=jnp.int32)
        s = jnp.einsum('bqhd,bkhd->bhqk', qb, k) * scale
        p = _causal_softmax(s, q_pos, pos)
        return jnp.einsum('bhqk,bkhd->bqhd', p.astype(v.dtype), v)

    starts = jnp.arange(l // BLOCK_Q, dtype=jnp.int32) * BLOCK_Q
    out = _from_blocks(lax.map(block, (starts, _to_blocks(q))))
    return out.reshape(b, l, MLA_HEADS * MLA_V_DIM)

def _diff_attn(q, k, v, q_norm, k_norm, lam_q1, lam_k1, lam_q2, lam_k2, subln, rel_bias, pos, lambda_init):
    b, l, _ = q.shape
    q = _rms_norm(q.reshape(b, l, DIFF_HEADS, 2, DIFF_HEAD_DIM), q_norm)
    k = _rms_norm(k.reshape(b, l, DIFF_HEADS, 2, DIFF_HEAD_DIM), k_norm)
    v = v.reshape(b, l, DIFF_HEADS, DIFF_V_DIM)
    lam = (jnp.exp(jnp.sum(lam_q1.astype(jnp.float32) * lam_k1.astype(jnp.float32)))
           - jnp.exp(jnp.sum(lam_q2.astype(jnp.float32) * lam_k2.astype(jnp.float32)))
           + lambda_init)
    k1, k2 = k[..., 0, :], k[..., 1, :]
    bias_table = rel_bias.astype(jnp.float32)
    scale = DIFF_HEAD_DIM ** -0.5

    def block(args):
        q_start, qb = args
        q_pos = q_start + jnp.arange(BLOCK_Q, dtype=jnp.int32)
        bias = bias_table[_t5_bucket(q_pos[:, None] - pos[None, :])]
        bias = jnp.transpose(bias, (2, 0, 1))[None]
        s1 = jnp.einsum('bqhd,bkhd->bhqk', qb[..., 0, :], k1).astype(jnp.float32) * scale + bias
        s2 = jnp.einsum('bqhd,bkhd->bhqk', qb[..., 1, :], k2).astype(jnp.float32) * scale + bias
        a = _causal_softmax(s1, q_pos, pos) - lam * _causal_softmax(s2, q_pos, pos)
        return jnp.einsum('bhqk,bkhd->bqhd', a.astype(v.dtype), v)

    starts = jnp.arange(l // BLOCK_Q, dtype=jnp.int32) * BLOCK_Q
    out = _from_blocks(lax.map(block, (starts, _to_blocks(q))))
    out = _rms_norm(out, subln) * (1.0 - lambda_init)
    return out.reshape(b, l, DIFF_V_WIDTH)

def _peer(h, w_query, sub_keys, u, v):
    b, l, d = h.shape
    tokens = h.reshape(b * l // PEER_CHUNK, PEER_CHUNK, d)

    def chunk(xc):
        q = (xc @ w_query).reshape(PEER_CHUNK, PEER_HEADS, 2, PEER_SUBKEY_DIM)
        s = jnp.einsum('chpd,hpnd->chpn', q, sub_keys).astype(jnp.float32)
        s1, i1 = lax.top_k(s[:, :, 0], PEER_TOPK)
        s2, i2 = lax.top_k(s[:, :, 1], PEER_TOPK)
        cand = (s1[..., :, None] + s2[..., None, :]).reshape(PEER_CHUNK, PEER_HEADS, PEER_TOPK * PEER_TOPK)
        best, flat = lax.top_k(cand, PEER_TOPK)
        e1 = jnp.take_along_axis(i1, flat // PEER_TOPK, axis=-1)
        e2 = jnp.take_along_axis(i2, flat % PEER_TOPK, axis=-1)
        experts = e1 * PEER_N_KEYS + e2
        g = jax.nn.softmax(best, axis=-1)
        u_sel = jnp.take(u, experts, axis=0)
        act = jax.nn.gelu(jnp.einsum('cd,chkd->chk', xc, u_sel).astype(jnp.float32), approximate=False)
        v_sel = jnp.take(v, experts, axis=0)
        return jnp.einsum('chk,chkd->cd', (g * act).astype(v.dtype), v_sel)

    return lax.map(chunk, tokens).reshape(b, l, d)

def first_inputs(seed: int = 0) -> dict:
    key = jax.random.key(seed)
    ks = jax.random.split(key, 24)
    f32 = jnp.float32

    def nrm(k, shape, scale):
        return jax.random.normal(k, shape, f32) * scale

    def gain(k, shape):
        return 1.0 + 0.02 * jax.random.normal(k, shape, f32)

    return {
        "x": nrm(ks[0], (BATCH, SEQ, D_MODEL), 1.0),
        "meta_tokens": nrm(ks[1], (N_META, D_MODEL), 1.0),
        "rel_bias": nrm(ks[2], (NUM_BUCKETS, DIFF_HEADS), 0.5),
        "attn_norm": gain(ks[3], (DEPTH, D_MODEL)),
        "w_in": nrm(ks[4], (DEPTH, D_MODEL, IN_WIDTH), D_MODEL ** -0.5),
        "mla_q_norm": gain(ks[5], (DEPTH, MLA_Q_RANK)),
        "mla_w_uq": nrm(ks[6], (DEPTH, MLA_Q_RANK, MLA_HEADS * MLA_QK_DIM), MLA_Q_RANK ** -0.5),
        "mla_kv_norm": gain(ks[7], (DEPTH, MLA_KV_RANK)),
        "mla_w_ukv": nrm(ks[8], (DEPTH, MLA_KV_RANK, MLA_HEADS * (MLA_NOPE_DIM + MLA_V_DIM)), MLA_KV_RANK ** -0.5),
        "mla_qk_norm_q": gain(ks[9], (DEPTH, MLA_QK_DIM)),
        "mla_qk_norm_k": gain(ks[10], (DEPTH, MLA_QK_DIM)),
        "diff_q_norm": gain(ks[11], (DEPTH, DIFF_HEAD_DIM)),
        "diff_k_norm": gain(ks[12], (DEPTH, DIFF_HEAD_DIM)),
        "diff_lambda_q1": nrm(ks[13], (DEPTH, DIFF_HEAD_DIM), 0.1),
        "diff_lambda_k1": nrm(ks[14], (DEPTH, DIFF_HEAD_DIM), 0.1),
        "diff_lambda_q2": nrm(ks[15], (DEPTH, DIFF_HEAD_DIM), 0.1),
        "diff_lambda_k2": nrm(ks[16], (DEPTH, DIFF_HEAD_DIM), 0.1),
        "diff_subln": gain(ks[17], (DEPTH, DIFF_V_DIM)),
        "w_out": nrm(ks[18], (DEPTH, MIX_WIDTH, D_MODEL), MIX_WIDTH ** -0.5),
        "ffn_norm": gain(ks[19], (DEPTH, D_MODEL)),
        "peer_w_query": nrm(ks[20], (DEPTH, D_MODEL, PEER_HEADS * PEER_QUERY_DIM), D_MODEL ** -0.5),
        "peer_sub_keys": nrm(ks[21], (DEPTH, PEER_HEADS, 2, PEER_N_KEYS, PEER_SUBKEY_DIM), PEER_SUBKEY_DIM ** -0.5),
        "peer_u": nrm(ks[22], (DEPTH, PEER_N_EXPERTS, D_MODEL), D_MODEL ** -0.5),
        "peer_v": nrm(ks[23], (DEPTH, PEER_N_EXPERTS, D_MODEL), PEER_HEADS ** -0.5),
    }

def first_block(x, meta_tokens, rel_bias, attn_norm, w_in, mla_q_norm, mla_w_uq, mla_kv_norm, mla_w_ukv,
              mla_qk_norm_q, mla_qk_norm_k, diff_q_norm, diff_k_norm, diff_lambda_q1, diff_lambda_k1,
              diff_lambda_q2, diff_lambda_k2, diff_subln, w_out, ffn_norm, peer_w_query, peer_sub_keys,
              peer_u, peer_v):
    b, s, d = x.shape
    l_real = N_META + s
    l_pad = -(-l_real // BLOCK_Q) * BLOCK_Q
    meta = jnp.broadcast_to(meta_tokens[None].astype(x.dtype), (b, N_META, d))
    h = jnp.concatenate([meta, x, jnp.zeros((b, l_pad - l_real, d), x.dtype)], axis=1)
    pos = jnp.arange(l_pad, dtype=jnp.int32)
    for layer in range(DEPTH):
        lambda_init = 0.8 - 0.6 * math.exp(-0.3 * layer)
        n = _rms_norm(h, attn_norm[layer])
        proj = n @ w_in[layer]
        c_q, c_kv, k_rope, dq, dk, dv = jnp.split(proj, IN_SPLITS, axis=-1)
        y_mla = _mla(c_q, c_kv, k_rope, mla_q_norm[layer], mla_w_uq[layer], mla_kv_norm[layer],
                     mla_w_ukv[layer], mla_qk_norm_q[layer], mla_qk_norm_k[layer], pos)
        y_diff = _diff_attn(dq, dk, dv, diff_q_norm[layer], diff_k_norm[layer], diff_lambda_q1[layer],
                            diff_lambda_k1[layer], diff_lambda_q2[layer], diff_lambda_k2[layer],
                            diff_subln[layer], rel_bias, pos, lambda_init)
        h = h + jnp.concatenate([y_mla, y_diff], axis=-1) @ w_out[layer]
        h = h + _peer(_rms_norm(h, ffn_norm[layer]), peer_w_query[layer], peer_sub_keys[layer],
                      peer_u[layer], peer_v[layer])
    return h[:, N_META:l_real]


N_ATTN_HEADS = 8
HEAD_DIM = 64
ATTN_WIDTH = N_ATTN_HEADS * HEAD_DIM
N_CONV_GROUPS = 8
CONV_GROUP_DIM = 64
CONV_WIDTH = N_CONV_GROUPS * CONV_GROUP_DIM
CONV_KSIZE = 3
D_FF = 2816
Q_BLOCK = 128
N_SUBLAYERS = 3
N_MOD = 3
FFN_RES_WEIGHT = 0.5
MIX_IN_WIDTH = 3 * CONV_WIDTH + 3 * ATTN_WIDTH + 2 * D_MODEL


def rmsnorm(x, g):
    xf = x.astype(jnp.float32)
    inv = lax.rsqrt(jnp.mean(xf * xf, axis=-1, keepdims=True) + EPS)
    return (xf * inv).astype(x.dtype) * g

def modulate(x, shift, scale):
    return x * (1 + scale[:, None, :]) + shift[:, None, :]

def swiglu(x, w_gu, w_down):
    g, u = jnp.split(x @ w_gu, 2, axis=-1)
    return (jax.nn.silu(g) * u) @ w_down

def short_conv(b_gate, c_gate, xin, conv_w):
    v = c_gate * xin
    S = v.shape[1]
    vp = jnp.pad(v, ((0, 0), (CONV_KSIZE - 1, 0), (0, 0)))
    y = conv_w[0] * vp[:, 0:S, :]
    for k in range(1, CONV_KSIZE):
        y = y + conv_w[k] * vp[:, k:k + S, :]
    return b_gate * y

def stick_breaking_attention(q, k, v):
    S = q.shape[2]
    scale = HEAD_DIM ** -0.5
    qf = q.astype(jnp.float32)
    kf = k.astype(jnp.float32)
    vf = v.astype(jnp.float32)
    outs = []
    for i in range(S // Q_BLOCK):
        start = i * Q_BLOCK
        end = start + Q_BLOCK
        q_blk = qf[:, :, start:end, :]
        k_c = kf[:, :, :end, :]
        v_c = vf[:, :, :end, :]
        z = jnp.einsum('bhqd,bhkd->bhqk', q_blk, k_c) * scale
        t_pos = start + jnp.arange(Q_BLOCK)
        s_pos = jnp.arange(end)
        valid = s_pos[None, :] < t_pos[:, None]
        sp = jnp.where(valid, jax.nn.softplus(z), 0.0)
        rem = lax.cumsum(sp, axis=3, reverse=True) - sp
        log_a = jax.nn.log_sigmoid(z) - rem
        a = jnp.where(valid, jnp.exp(log_a), 0.0)
        outs.append(jnp.einsum('bhqk,bhkd->bhqd', a, v_c))
    return jnp.concatenate(outs, axis=2).astype(q.dtype)

def mixer(u, w_mix_in, b_merge, conv_w, w_conv_out, w_attn_out, w_out):
    B, S, _ = u.shape
    proj = u @ w_mix_in
    idx = [CONV_WIDTH, 2 * CONV_WIDTH, 3 * CONV_WIDTH,
           3 * CONV_WIDTH + ATTN_WIDTH, 3 * CONV_WIDTH + 2 * ATTN_WIDTH,
           3 * CONV_WIDTH + 3 * ATTN_WIDTH, 3 * CONV_WIDTH + 3 * ATTN_WIDTH + D_MODEL]
    cb, cc, cx, q, k, v, ga, gb = jnp.split(proj, idx, axis=-1)
    ya = short_conv(cb, cc, cx, conv_w) @ w_conv_out
    def heads(t):
        return t.reshape(B, S, N_ATTN_HEADS, HEAD_DIM).transpose(0, 2, 1, 3)
    o = stick_breaking_attention(heads(q), heads(k), heads(v))
    o = o.transpose(0, 2, 1, 3).reshape(B, S, ATTN_WIDTH)
    yb = o @ w_attn_out
    merged = jax.nn.sigmoid(ga + b_merge[0]) * ya + jax.nn.sigmoid(gb + b_merge[1]) * yb
    return merged @ w_out

def second_inputs(seed: int = 0) -> dict:
    key = jax.random.key(seed)
    ks = jax.random.split(key, 24)
    f32 = jnp.float32
    L, D = DEPTH, D_MODEL

    def nrm(k, shape, s):
        return jax.random.normal(k, shape, f32) * s

    return {
        "x": nrm(ks[0], (BATCH, SEQ, D), 1.0),
        "c": nrm(ks[1], (BATCH, D), 1.0),
        "w_ada": nrm(ks[2], (L, D, N_SUBLAYERS * N_MOD * D), 0.5 * D ** -0.5),
        "b_ada": nrm(ks[3], (L, N_SUBLAYERS * N_MOD * D), 0.02),
        "norm1_g": 1.0 + nrm(ks[4], (L, D), 0.02),
        "ffn1_w_gu": nrm(ks[5], (L, D, 2 * D_FF), D ** -0.5),
        "ffn1_w_down": nrm(ks[6], (L, D_FF, D), D_FF ** -0.5),
        "norm2_g": 1.0 + nrm(ks[7], (L, D), 0.02),
        "w_mix_in": nrm(ks[8], (L, D, MIX_IN_WIDTH), D ** -0.5),
        "b_merge": nrm(ks[9], (L, 2, D), 0.02),
        "conv_w": nrm(ks[10], (L, CONV_KSIZE, CONV_WIDTH), CONV_KSIZE ** -0.5),
        "w_conv_out": nrm(ks[11], (L, CONV_WIDTH, D), CONV_WIDTH ** -0.5),
        "w_attn_out": nrm(ks[12], (L, ATTN_WIDTH, D), ATTN_WIDTH ** -0.5),
        "w_out": nrm(ks[13], (L, D, D), D ** -0.5),
        "norm3_g": 1.0 + nrm(ks[14], (L, D), 0.02),
        "ffn2_w_gu": nrm(ks[15], (L, D, 2 * D_FF), D ** -0.5),
        "ffn2_w_down": nrm(ks[16], (L, D_FF, D), D_FF ** -0.5),
        "final_g": 1.0 + nrm(ks[17], (D,), 0.02),
    }

def second_block(x, c, w_ada, b_ada, norm1_g, ffn1_w_gu, ffn1_w_down, norm2_g,
              w_mix_in, b_merge, conv_w, w_conv_out, w_attn_out, w_out,
              norm3_g, ffn2_w_gu, ffn2_w_down, final_g):
    B = x.shape[0]
    c_act = jax.nn.silu(c)
    h = x
    for l in range(DEPTH):
        mod = (c_act @ w_ada[l] + b_ada[l]).reshape(B, N_SUBLAYERS, N_MOD, D_MODEL)
        u = modulate(rmsnorm(h, norm1_g[l]), mod[:, 0, 0], mod[:, 0, 1])
        h = h + FFN_RES_WEIGHT * mod[:, 0, 2][:, None, :] * swiglu(u, ffn1_w_gu[l], ffn1_w_down[l])
        u = modulate(rmsnorm(h, norm2_g[l]), mod[:, 1, 0], mod[:, 1, 1])
        y = mixer(u, w_mix_in[l], b_merge[l], conv_w[l], w_conv_out[l], w_attn_out[l], w_out[l])
        h = h + mod[:, 1, 2][:, None, :] * y
        u = modulate(rmsnorm(h, norm3_g[l]), mod[:, 2, 0], mod[:, 2, 1])
        h = h + FFN_RES_WEIGHT * mod[:, 2, 2][:, None, :] * swiglu(u, ffn2_w_gu[l], ffn2_w_down[l])
    return rmsnorm(h, final_g)


def setup_inputs(seed=0):
    out = dict(first_inputs(seed))
    for name, value in second_inputs(seed + 1).items():
        if name != "x":
            out[name + "_2"] = value
    return out


def reference(
    x, meta_tokens, rel_bias, attn_norm, w_in, mla_q_norm, mla_w_uq, mla_kv_norm, mla_w_ukv,
    mla_qk_norm_q, mla_qk_norm_k, diff_q_norm, diff_k_norm, diff_lambda_q1, diff_lambda_k1,
    diff_lambda_q2, diff_lambda_k2, diff_subln, w_out, ffn_norm, peer_w_query, peer_sub_keys,
    peer_u, peer_v, c_2, w_ada_2, b_ada_2, norm1_g_2, ffn1_w_gu_2, ffn1_w_down_2, norm2_g_2,
    w_mix_in_2, b_merge_2, conv_w_2, w_conv_out_2, w_attn_out_2, w_out_2, norm3_g_2,
    ffn2_w_gu_2, ffn2_w_down_2, final_g_2,
):
    x = first_block(
        x, meta_tokens, rel_bias, attn_norm, w_in, mla_q_norm, mla_w_uq, mla_kv_norm, mla_w_ukv,
        mla_qk_norm_q, mla_qk_norm_k, diff_q_norm, diff_k_norm, diff_lambda_q1, diff_lambda_k1,
        diff_lambda_q2, diff_lambda_k2, diff_subln, w_out, ffn_norm, peer_w_query,
        peer_sub_keys, peer_u, peer_v,
    )
    return second_block(
        x, c_2, w_ada_2, b_ada_2, norm1_g_2, ffn1_w_gu_2, ffn1_w_down_2, norm2_g_2, w_mix_in_2,
        b_merge_2, conv_w_2, w_conv_out_2, w_attn_out_2, w_out_2, norm3_g_2, ffn2_w_gu_2,
        ffn2_w_down_2, final_g_2,
    )


_drawn_inputs = setup_inputs


def setup_inputs(seed=0):
    import zlib

    import numpy as np

    out = dict(_drawn_inputs(seed))
    spreads = {}
    factors = {'mla_q_norm': 6.59,
     'mla_kv_norm': 6.169,
     'mla_qk_norm_q': 6.63,
     'mla_qk_norm_k': 6.446,
     'diff_q_norm': 2.882,
     'diff_k_norm': 3.148,
     'diff_subln': 7.587,
     'b_ada_2': 2.935,
     'norm1_g_2': 8.0,
     'norm2_g_2': 8.0,
     'b_merge_2': 22.513,
     'norm3_g_2': 64.0,
     'final_g_2': 7.941,
     'ffn_norm': 3.338,
     'w_attn_out_2': 3.8}
    for name, (base, spread) in spreads.items():
        noise = np.random.default_rng([zlib.crc32(name.encode()), seed]).standard_normal(out[name].shape)
        drawn = base * np.exp(spread * noise) if base else spread * noise
        out[name] = __import__('jax').numpy.asarray(drawn.astype(out[name].dtype))
    for name, factor in factors.items():
        out[name] = (out[name] * factor).astype(out[name].dtype)
    return out
```

```python
import math
from contextlib import ExitStack

import numpy as np

import concourse.bass as bass
from concourse import mybir

F32 = mybir.dt.float32
U32 = mybir.dt.uint32
ACT = mybir.ActivationFunctionType
ALU = mybir.AluOpType
AX = mybir.AxisListType.X

P = 128
D = 1024
KD = D // P
SEQ, META = 256, 16
KEYS = META + SEQ
ROWS = (P, P, META)
COL0 = (META, META + P, 0)
QT = 2
EPS = 1e-6
NEG = -1e30
MH, MQR, MKVR, NOPE, ROPE, MV = 8, 256, 256, 64, 32, 64
QK = NOPE + ROPE
HALF = ROPE // 2
DH, DD = 4, 64
DV = 2 * DD
LAMBDA_INIT = 0.8 - 0.6 * math.exp(0.0)
BUCKETS, MAX_DIST = 32, 128
C_C, C_ROPE = 0, MQR + MKVR
C_DQ = C_ROPE + ROPE
C_DK = C_DQ + DH * 2 * DD
C_DV = C_DK + DH * 2 * DD
IN_W = C_DV + DH * DV
PH, NK, TOPK, PQ = 8, 128, 16, 256
SLOTS = PH * TOPK
FF = 2816
FT = FF // P
SH, SD = 8, 64
CW = 512
ADA = 9 * D


class Signal:

    def __init__(self, sem):
        self.sem, self.sent = sem, 0

    def mark(self, ins):
        self.sent += 1
        ins.then_inc(self.sem, 1)

    def step(self, eng, ins):
        self.mark(ins)
        eng.wait_ge(self.sem, self.sent)


def bucket_one_hot():
    dist = KEYS - 1 - np.arange(KEYS + SEQ)
    n = np.maximum(dist, 0)
    exact = BUCKETS // 2
    large = exact + (np.log(np.maximum(n, 1).astype(np.float32) / np.float32(exact))
                     / np.float32(math.log(MAX_DIST / exact)) * np.float32(BUCKETS - exact)).astype(np.int32)
    bucket = np.where(n < exact, n, np.minimum(large, BUCKETS - 1))
    return ((bucket[None] == np.arange(BUCKETS)[:, None]) & (dist >= 0)[None]).astype(np.float32)


def rope_table():
    inv = np.float32(10000.0) ** (-np.arange(HALF, dtype=np.float32) / np.float32(HALF))
    ang = np.arange(KEYS, dtype=np.float32)[:, None] * inv[None]
    return np.concatenate([np.cos(ang), np.sin(ang)], 1).astype(np.float32)


def spread(ap, *shape):
    while len(ap.shape) < len(shape):
        ap = ap.unsqueeze(len(ap.shape))
    return ap.to_broadcast(list(shape))


def program(nc, t, out):
    ctx = ExitStack()
    with ctx:
        def sb(name, cols, dt=F32, rows=P):
            return ctx.enter_context(nc.sbuf_tensor(name, [rows, cols], dt))

        def sem(name):
            return ctx.enter_context(nc.semaphore(name))

        def signal(name):
            return Signal(sem(name))

        RING, SLOT = 6, 2048
        hx = sb("hx", QT * D)[:].rearrange("p (t d) -> p t d", t=QT)
        ident = sb("ident", P)[:]
        ones = sb("ones", P)[:]
        eps = sb("eps", 1)[:]
        ring = sb("ring", RING * SLOT)
        arena = sb("arena", 34816)
        stats = sb("stats", 128)[:]
        rstd = sb("rstd", 128)[:]
        gain_rows = sb("gain_rows", P)[:]
        gains = sb("gains", P)[:]
        rope = sb("rope", 3 * ROPE)[:].rearrange("p (t c) -> p t c", t=3)
        lam_in = sb("lam_in", 4 * DD)[:].rearrange("p (v d) -> p v d", v=4)
        lam = sb("lam", 4)[:]
        rel = sb("rel", 4, rows=BUCKETS)[:]
        small = sb("small", 256)[:]

        def area(tensor, at, cols):
            assert at + cols <= tensor.shape[1]
            return tensor[:, at:at + cols]

        W0, W1, W2, WR = 0, 4096, 8192, 12288
        w_slot = [area(arena, o, 4096).rearrange("p (k n) -> p k n", k=KD) for o in (W0, W1, W2)]
        w_rope = area(arena, WR, KD * ROPE).rearrange("p (k n) -> p k n", k=KD)
        N0 = WR + KD * ROPE
        nT = area(arena, N0, KD * KEYS).rearrange("p (k n) -> p k n", k=KD)
        dqT = area(arena, N0, DH * SEQ).rearrange("p (h n) -> p h n", h=DH)
        dkT = area(arena, N0 + DH * SEQ, DH * KEYS).rearrange("p (h n) -> p h n", h=DH)
        R0 = N0 + KD * KEYS
        pr = area(arena, R0, 3 * IN_W).rearrange("p (t n) -> p t n", t=3)
        U0 = R0 + 3 * IN_W
        w_uq = area(arena, U0, 2 * MH * QK).rearrange("p (k n) -> p k n", k=2)
        w_ukv = area(arena, U0 + 2 * MH * QK, 2 * 1024).rearrange("p (k n) -> p k n", k=2)
        C0 = U0 + 2 * MH * QK + 2048
        hm = area(arena, C0, D)[0:META]
        cT = area(arena, C0, 4 * KEYS).rearrange("p (k n) -> p k n", k=4)
        B0 = C0 + 4 * KEYS
        bias = area(arena, B0, DH * QT * KEYS).rearrange("p (h t n) -> p h t n", h=DH, t=QT)
        mask = area(arena, B0 + DH * QT * KEYS, QT * KEYS).rearrange("p (t n) -> p t n", t=QT)
        G0 = B0 + (DH + 1) * QT * KEYS
        g_rope = area(arena, G0, 2 * ROPE).rearrange("p (w c) -> p w c", w=2)
        K0 = G0 + 2 * ROPE
        qT = area(arena, K0, MH * SEQ).rearrange("p (h n) -> p h n", h=MH)
        kT = area(arena, K0 + MH * SEQ, MH * KEYS).rearrange("p (h n) -> p h n", h=MH)
        q_row = area(arena, W1, 2 * MH * QK).rearrange("p (t n) -> p t n", t=2)
        k_row = area(arena, W1 + 2 * MH * QK, 3 * MH * QK).rearrange("p (t n) -> p t n", t=3)
        v_row = area(arena, W2, 3 * MH * MV).rearrange("p (t n) -> p t n", t=3)
        rot = area(arena, W2 + 3 * MH * MV, 3 * MH * ROPE).rearrange("p (s h c) -> p s h c", s=3, h=MH)
        wo_half = [w_slot[0], area(arena, U0, 4096).rearrange("p (k n) -> p k n", k=KD)]
        xn = area(ring, 0, 3 * D).rearrange("p (t d) -> p t d", t=3)
        fill = area(ring, 3072, KEYS + SEQ)[0:4]
        onehot = area(ring, 3616, KEYS + SEQ)[0:BUCKETS]
        tmp = area(ring, 4352, 1024)
        NM = 4
        sc = [area(ring, i * NM * KEYS, NM * KEYS).rearrange("p (m n) -> p m n", m=NM) for i in range(2)]
        pb = [area(ring, (2 + i) * NM * KEYS, NM * KEYS).rearrange("p (m n) -> p m n", m=NM) for i in range(2)]
        Y0 = 4 * NM * KEYS
        pT = area(ring, Y0, 4 * 3 * P).rearrange("p (s b n) -> p s b n", s=4, b=3)
        y = area(ring, Y0 + 1536, QT * D).rearrange("p (t d) -> p t d", t=QT)
        yT = area(ring, Y0 + 1536 + QT * D, KD * SEQ).rearrange("p (k n) -> p k n", k=KD)

        wq_chunk = [area(arena, o, 4096).rearrange("p (k n) -> p k n", k=KD) for o in (W1, W2, N0, N0 + 4096)]
        hn = area(arena, W0, QT * D).rearrange("p (t d) -> p t d", t=QT)
        hnT = area(arena, B0, KD * SEQ).rearrange("p (k n) -> p k n", k=KD)
        keysT = area(arena, B0 + 2048, 2 * PH * NK).rearrange("p (s n) -> p s n", s=2 * PH)
        keys = area(arena, B0 + 4096, 2 * PH * P).rearrange("p (s d) -> p s d", s=2 * PH)
        g_ffn = area(arena, B0 + 6144, D)
        pqT = area(arena, U0, 2 * PH * SEQ).rearrange("p (s n) -> p s n", s=2 * PH)
        ps = [area(arena, o, 2 * PH * NK).rearrange("p (s n) -> p s n", s=2 * PH) for o in (W0 + 2048, B0 + 4096)]
        wide = [area(arena, U0 + 2048 * i, 2048).rearrange("p (h a b) -> p h a b", h=PH, a=TOPK) for i in range(2)]

        def table(n, dt=F32, cols=SLOTS):
            tab = area(arena, W1 + P * n, cols)
            return tab if dt == F32 else tab.bitcast(dt)

        top_v, top_i, top_f = (table(2 * i, dt, 256).rearrange("p (s k) -> p s k", k=TOPK) for i, dt in enumerate((F32, U32, F32)))
        best, flat, half_i, half_f = table(6), table(7, U32), table(8, U32), table(9)
        e_hi, e_lo, iota16 = table(10), table(11), table(12)
        gate = [table(13), table(14)]
        expert = [table(15, U32), table(16, U32)]
        dots = [table(17), table(18)]
        slot8 = table(19)
        expert8 = table(20, U32)
        GB = 8
        rows = area(arena, N0, GB * D).rearrange("p (b d) -> p b d", b=GB)
        prod = area(arena, W2, 2 * D).rearrange("p (b d) -> p b d", b=2)
        gates = area(arena, B0, 3 * D).rearrange("p (s d) -> p s d", s=3)
        b_ada = sb("b_ada", 512, rows=ADA // 512)[:]
        c_act = sb("c_act", KD)[:]
        mod_row = sb("mod_row", 512, rows=2)[:]
        mod = sb("mod", 3 * 2 * KD)[:].rearrange("p (s m k) -> p s m k", s=3, m=2)
        ada_chunk = [area(ring, 4096 * i, 4096).rearrange("p (k n) -> p k n", k=KD) for i in range(RING // 2)]

        uT = area(arena, 0, KD * SEQ).rearrange("p (k n) -> p k n", k=KD)
        nrm = area(arena, 2048, QT * D).rearrange("p (t d) -> p t d", t=QT)
        silu = area(arena, 4096, 2 * SEQ).rearrange("p (b n) -> p b n", b=2)
        hT = area(arena, 4608, 4 * SEQ).rearrange("p (b n) -> p b n", b=4)
        part = area(arena, 5632, D)
        g_final = area(arena, 6656, D)
        at = [7680]

        def mix(cols, *dims):
            piece = area(arena, at[0], cols)
            at[0] += cols
            return piece.rearrange("p (a n) -> p a n", a=dims[0]) if dims else piece

        PAD = SEQ + 2
        cbT, ccT, cxT, convT, vT = mix(4 * SEQ, 4), mix(4 * SEQ, 4), mix(4 * SEQ, 4), mix(4 * SEQ, 4), mix(4 * PAD, 4)
        sqT, skT, sv_row = mix(4 * SEQ, 4), mix(4 * SEQ, 4), mix(QT * CW, QT)
        sgaT, sgbT, oT = mix(KD * SEQ, KD), mix(KD * SEQ, KD), mix(4 * SEQ, 4)
        ZW = SEQ + P
        zx, zlog, zsp = (mix(4 * ZW, 4) for _ in range(3))
        assert at[0] <= B0
        later = sb("later", P)[:]
        seen = sb("seen", P)[:]
        w_slots = [ring[:, SLOT * i:SLOT * (i + 1)] for i in range(RING)]

        psum = [ctx.enter_context(nc.psum_tensor(f"bank{i}", [P, 512], F32)) for i in range(8)]
        LB = 4
        lane_d, lane_a = psum[:LB], psum[LB:]
        d_full, d_free = signal("d_full"), signal("d_free")
        a_full, a_free = signal("a_full"), signal("a_free")

        fill_dram = nc.dram_tensor("bias_by_distance", [4, KEYS + SEQ], F32, kind="Internal")
        SKEW = P * (KEYS + SEQ + 1)
        skew_dram = nc.dram_tensor("bias_by_distance_skewed", [DH, SKEW], F32, kind="Internal")
        onehot_dram = nc.inline_tensor(bucket_one_hot(), "bucket_one_hot")
        rope_dram = nc.inline_tensor(rope_table(), "rope_table")

        GAIN, n_gain = {}, 0
        gain_src = [("attn_norm", KD), ("mla_q_norm", 2), ("mla_kv_norm", 2), ("diff_subln", 1), ("norm1_g_2", KD),
                    ("norm2_g_2", KD), ("norm3_g_2", KD), ("b_merge_2", 2 * KD), ("c_2", KD)]
        for name, n in gain_src:
            GAIN[name], n_gain = n_gain, n_gain + n
        conv_row = n_gain
        n_gain += 12
        for name in ("diff_q_norm", "diff_k_norm", "mla_qk_norm_q", "mla_qk_norm_k"):
            GAIN[name], n_gain = n_gain, n_gain + 1
        assert n_gain <= P

        ld_x = [sem(f"ld_x{i}") for i in range(3)]
        ld_gain, ld_small, ld_rope_w = sem("ld_gain"), sem("ld_small"), sem("ld_rope_w")
        ld_c, ld_dk, ld_dq, ld_dv, ld_up, ld_wo = (sem(n) for n in ("ld_c", "ld_dk", "ld_dq", "ld_dv", "ld_up", "ld_wo"))
        ld_hot, st_fill, st_skew, ld_bias = (sem(n) for n in ("ld_hot", "st_fill", "st_skew", "ld_bias"))
        consts, bias_ready = signal("consts"), signal("bias_ready")
        sums, roots = signal("sums"), signal("roots")
        dve, act = signal("dve"), signal("act")
        gains_ready, fill_ready = signal("gains_ready"), signal("fill_ready")
        xn_ready, c_row_ready = signal("xn_ready"), signal("c_row_ready")
        m_ready, p_ready = signal("m_ready"), signal("p_ready")
        a_ready, y_ready = signal("a_ready"), signal("y_ready")
        h1_ready, dk_ready, dq_ready = signal("h1_ready"), signal("dk_ready"), signal("dq_ready")
        head_ready = signal("head_ready")
        lam_sums, lam_exps = signal("lam_sums"), signal("lam_exps")
        stored = sem("stored")
        ld_wq = [sem(f"ld_wq{i}") for i in range(4)]
        ld_keys, ld_gffn, ld_bada = sem("ld_keys"), sem("ld_gffn"), sem("ld_bada")
        slot_ld = [sem(f"slot_ld{i}") for i in range(RING)]
        slot_used = signal("slot_used")
        hn_ready, c_ready, ada_row = signal("hn_ready"), signal("c_ready"), signal("ada_row")
        bests, softs, routed = signal("bests"), signal("softs"), signal("routed")
        rows_ld = [sem(f"rows_ld{i}") for i in range(GB)]
        rows_free = sem("rows_free")
        gather_go = sem("gather_go")
        expert8_ready = signal("expert8_ready")
        mod_ready, n_ready = signal("mod_ready"), signal("n_ready")
        u_even, u_odd = signal("u_even"), signal("u_odd")
        flipped = signal("flipped")
        b_sums, b_roots = signal("b_sums"), signal("b_roots")
        w_ld = [sem(f"w_ld{i}") for i in range(RING)]
        gu_full, silu_ready, h_ready, down_done = (signal(n) for n in ("gu_full", "silu_ready", "h_ready", "down_done"))
        ffn_out = signal("ffn_out")
        x_full, x_act, x_dve = signal("x_full"), signal("x_act"), signal("x_dve")
        z_full, z_free, e_ready, sp_ready, prob_ready = (signal(n) for n in ("z_full", "z_free", "e_ready", "sp_ready", "prob_ready"))
        masked = signal("masked")
        log_ready, min_ready, conv_ready, merged_ready = (signal(n) for n in ("log_ready", "min_ready", "conv_ready", "merged_ready"))
        ld_final, out_ready = sem("ld_final"), signal("out_ready")
        dots_ready, acts_ready, h2_ready = signal("dots_ready"), signal("acts_ready"), signal("h2_ready")


        STEPS = [(tt, g) for tt in range(QT) for g in range(4)]
        def maps(g):
            return range(4) if g < 2 else range(0, 4, 2)

        d_jobs = ["gains", ("fill", 0), ("fill", 1)]
        d_jobs += [("nT", tt, b) for tt in range(3) for b in range(2)] + [("cT", tt) for tt in range(3)]
        for i in range(len(STEPS) + 1):
            if i < len(STEPS):
                d_jobs += [("s", i, m) for m in range(4)]
            if i:
                d_jobs.append(("o", i - 1))
        d_jobs += [("yT", tt, b) for tt in range(QT) for b in range(2)]
        d_jobs += [("wo", n, tt) for n in range(2) for tt in range(QT)]
        a_jobs = [("c", tt) for tt in range(3)] + [("rope", tt) for tt in range(3)] + [("dk", tt) for tt in range(3)]
        a_jobs += [("dq", tt) for tt in range(QT)]
        for tt in range(3):
            a_jobs += [("q", tt, n) for n in range(2) if tt < QT] + [("kv", tt, n) for n in range(2)]
        a_jobs += [("dv", tt) for tt in range(3)] + [("dkT", tt) for tt in range(3)] + [("dqT", tt) for tt in range(QT)]
        for tt in range(3):
            a_jobs += [("qT", tt, n) for n in range(2) if tt < QT] + [("kT", tt, n) for n in range(2)]
        for i, (tt, g) in enumerate(STEPS):
            a_jobs += [("pT", i, m) for m in maps(g)]
        d_jobs += [("hnT", tt, b) for tt in range(QT) for b in range(2)]
        a_jobs += [("keysT", n) for n in range(4)] + [("pq", n) for n in range(8)]
        a_jobs += [("ps", tt, n) for tt in range(QT) for n in range(4)]
        for n in range(ADA // 512):
            a_jobs += [("ada", n)] + [("mod", n)] * (n % 6 < 4)
        d_at = {job: n for n, job in enumerate(d_jobs)}
        a_at = {job: n for n, job in enumerate(a_jobs)}

        def bank_of(job, at, lane):
            return lane[at[job] % LB]

        def open_bank(pe, job, at, lane, free):
            if at[job] >= LB:
                pe.wait_ge(free.sem, at[job] - LB + 1)
            return bank_of(job, at, lane)

        def full_bank(eng, job, at, lane, full):
            eng.wait_ge(full.sem, at[job] + 1)
            return bank_of(job, at, lane)

        norms, col = [], 0
        for names, n, width in ([[("x", tt) for tt in range(3)], 1, D], [[("c", tt) for tt in range(3)], 2, 256],
                                [[("dk", tt) for tt in range(3)] + [("dq", tt) for tt in range(QT)], 8, DD],
                                [[("q", 0), ("k", 0), ("q", 1), ("k", 1), ("k", 2)], MH, QK],
                                [["subln"], QT * DH, DV], [["h1"], QT, D]):
            for name in names:
                norms.append((name, col, n, width))
                col += n
        norm_at = {name: (k, slice(c, c + n), width) for k, (name, c, n, width) in enumerate(norms)}
        ROWS_OF = {("x", 2): META, ("c", 2): META, ("dk", 2): META, ("k", 2): META}

        BLOCKS = FT // 2
        MIX = [("in", n) for n in range(20)] + [("conv", n) for n in range(2)] + [("attn", n) for n in range(2)] + [("out", n) for n in range(4)]
        FIRST = (0, 3 * BLOCKS + len(MIX))
        MIX0 = 3 * BLOCKS
        MIX_COLS = [256 * n for n in (*range(6, 12), *range(0, 6), *range(12, 20))]
        x_jobs = [("in", n) for n in range(20)] + [("ya", n) for n in range(4)] + [("yb", n) for n in range(4)] + [("wo", n) for n in range(4)]
        x_at = {job: n for n, job in enumerate(x_jobs)}
        z_jobs = []
        for r in range(2):
            z_jobs += [("z", r, h) for h in range(4)] + [("rem", r, h) for h in range(4)] + [("o", r)]
        z_at = {job: n for n, job in enumerate(z_jobs)}

        def each_tile(eng, body):
            for j in range(4):
                body(j, j)
            with eng.Fori(1, 5) as i:
                for c in range(4):
                    body(i * 4 + c, c)
            for j in (20, 21):
                body(j, j % 4)

        block = ctx.enter_context(nc.Block())

        @block.sync
        def _(sp):
            for i, (dst, src) in enumerate(((hx[:, 0], t["x"][0, 0:P]), (hx[:, 1], t["x"][0, P:SEQ]), (hm, t["meta_tokens"]))):
                sp.dma_start(dst, src).then_inc(ld_x[i], 16)
            sp.wait_ge(consts.sem, 1)
            for name, n in gain_src:
                src = t[name].rearrange("a b -> (a b)") if len(t[name].shape) == 2 else t[name].rearrange("a b c -> (a b c)")
                sp.dma_start(gain_rows[GAIN[name]:GAIN[name] + n], src.rearrange("(k p) -> k p", p=P)).then_inc(ld_gain, 16)
            sp.dma_start(gain_rows[conv_row:conv_row + 12], t["conv_w_2"][0].rearrange("a (k p) -> (a k) p", p=P)).then_inc(ld_gain, 16)
            for name in ("diff_q_norm", "diff_k_norm"):
                for c in range(2):
                    sp.dma_start(gain_rows[GAIN[name]:GAIN[name] + 1, c * DD:(c + 1) * DD], t[name]).then_inc(ld_gain, 16)
            for name in ("mla_qk_norm_q", "mla_qk_norm_k"):
                sp.dma_start(gain_rows[GAIN[name]:GAIN[name] + 1, 0:NOPE], t[name][:, 0:NOPE]).then_inc(ld_gain, 16)
            w_in = t["w_in"][0].rearrange("(k p) n -> p k n", p=P)
            sp.dma_start(w_slot[0], w_in[:, :, C_C:C_C + 512]).then_inc(ld_c, 16)
            sp.dma_start(w_rope, w_in[:, :, C_ROPE:C_ROPE + ROPE]).then_inc(ld_rope_w, 16)
            sp.dma_start(w_slot[1], w_in[:, :, C_DK:C_DK + 512]).then_inc(ld_dk, 16)
            sp.dma_start(w_slot[2], w_in[:, :, C_DQ:C_DQ + 512]).then_inc(ld_dq, 16)
            sp.dma_start(w_uq, t["mla_w_uq"][0].rearrange("(k p) n -> p k n", p=P)).then_inc(ld_up, 16)
            sp.dma_start(w_ukv, t["mla_w_ukv"][0].rearrange("(k p) n -> p k n", p=P)).then_inc(ld_up, 16)
            sp.dma_start(onehot, onehot_dram.ap()).then_inc(ld_hot, 16)
            sp.dma_start(rel, t["rel_bias"]).then_inc(ld_hot, 16)
            for i in range(3):
                sp.dma_start(rope[0:ROWS[i], i], rope_dram.ap()[COL0[i]:COL0[i] + ROWS[i]]).then_inc(ld_small, 16)
            for i, name in enumerate(("diff_lambda_q1", "diff_lambda_k1", "diff_lambda_q2", "diff_lambda_k2")):
                sp.dma_start(lam_in[:, i], t[name].to_broadcast([P, DD])).then_inc(ld_small, 16)
            for i, name in enumerate(("mla_qk_norm_q", "mla_qk_norm_k")):
                sp.dma_start(g_rope[:, i], t[name][:, NOPE:QK].to_broadcast([P, ROPE])).then_inc(ld_small, 16)
            sp.wait_ge(a_full.sem, a_at["c", 2] + 1)
            sp.dma_start(w_slot[0], w_in[:, :, C_DV:C_DV + 512]).then_inc(ld_dv, 16)
            sp.wait_ge(fill_ready.sem, 1)
            sp.dma_start(fill_dram.ap(), fill).then_inc(st_fill, 16)
            sp.wait_ge(st_fill, 16)
            sp.dma_start(bass.AP(skew_dram, 0, [[KEYS + SEQ + 1, P], [SKEW, DH], [1, KEYS + SEQ]]),
                         bass.AP(fill_dram, 0, [[0, P], [KEYS + SEQ, DH], [1, KEYS + SEQ]])).then_inc(st_skew, 16)
            sp.wait_ge(st_skew, 16)
            for tt in range(QT):
                src = bass.AP(skew_dram, SEQ - 1 - P * tt, [[KEYS + SEQ, P], [SKEW, DH], [1, KEYS]])
                sp.dma_start(bias[:, :, tt], src).then_inc(ld_bias, 16)
            w_out = t["w_out"][0].rearrange("(k p) n -> p k n", p=P)
            sp.wait_ge(a_full.sem, a_at["dv", 2] + 1)
            for n in range(2):
                sp.dma_start(wo_half[n], w_out[:, :, n * 512:(n + 1) * 512]).then_inc(ld_wo, 16)
            sp.wait_ge(y_ready.sem, 1)
            w_query = t["peer_w_query"][0].rearrange("(k p) n -> p k n", p=P)
            sp.dma_start(g_ffn, t["ffn_norm"].to_broadcast([P, D])).then_inc(ld_gffn, 16)
            for n in range(4):
                sp.dma_start(wq_chunk[n], w_query[:, :, n * 512:(n + 1) * 512]).then_inc(ld_wq[n], 16)
                if n == 0:
                    sp.dma_start(keys, t["peer_sub_keys"][0].rearrange("h s n d -> n (h s) d")).then_inc(ld_keys, 16)
            sp.dma_start(b_ada, t["b_ada_2"][0].rearrange("(a n) -> a n", n=512)).then_inc(ld_bada, 16)
            w_ada = t["w_ada_2"][0].rearrange("(k p) n -> p k n", p=P)
            sp.wait_ge(d_full.sem, d_at["yT", QT - 1, 1] + 1)
            for n in range(ADA // 512):
                if n == 1:
                    sp.wait_ge(hn_ready.sem, QT)
                if n >= 3:
                    sp.wait_ge(a_full.sem, a_at["ada", n - 3] + 1)
                sp.dma_start(ada_chunk[n % 3], w_ada[:, :, n * 512:(n + 1) * 512]).then_inc(slot_ld[n % 3], 16)

            def ffn_loads(f):
                w_gu = t[f"ffn{f + 1}_w_gu_2"][0].rearrange("(k p) n -> p k n", p=P)
                w_down = t[f"ffn{f + 1}_w_down_2"][0].rearrange("(j p) n -> p j n", p=P)

                def block_loads(b, parity, waits):
                    for c in range(3):
                        slot = (FIRST[f] + 3 * parity + c) % RING
                        waits(b, parity, c)
                        dst = w_slots[slot].rearrange("p (k n) -> p k n", k=KD if c < 2 else 2)
                        src = w_gu[:, :, bass.ds(b * 256 + c * FF, 256)] if c < 2 else w_down[:, bass.ds(b * 2, 2), :]
                        sp.dma_start(dst, src).then_inc(w_ld[slot], 16)

                def first(b, parity, c):
                    n = 3 * b + c
                    if f == 0:
                        sp.wait_ge(a_full.sem, a_at["ada", ADA // 512 - 3 + n // 2] + 1)
                    else:
                        mix_slot_used(len(MIX) - RING + n)

                def steady(b, parity, c):
                    if c < 2:
                        sp.wait_ge(gu_full.sem, b * 2 + (f * FT - 2))
                    else:
                        sp.wait_ge(down_done.sem, b * 2 + (f * FT - 2))

                for b in range(2):
                    block_loads(b, b, first)
                with sp.Fori(1, 5) as i:
                    for c in range(2):
                        block_loads(i * 2 + c, c, steady)
                block_loads(10, 0, steady)

            def mix_slot_used(n):
                kind, m = MIX[n]
                job = {"in": ("in", m), "conv": ("ya", 2 * m + 1), "attn": ("yb", 2 * m + 1), "out": ("wo", m)}[kind]
                sp.wait_ge(x_full.sem, x_at[job] + 1)

            ffn_loads(0)
            w_mix = {"in": t["w_mix_in_2"], "conv": t["w_conv_out_2"], "attn": t["w_attn_out_2"], "out": t["w_out_2"]}
            for n, (kind, m) in enumerate(MIX):
                if n < RING:
                    k = 3 * BLOCKS - RING + n
                    done = (k // 3 + 1) * 2
                    sp.wait_ge((gu_full if k % 3 < 2 else down_done).sem, done)
                else:
                    mix_slot_used(n - RING)
                w = w_mix[kind][0].rearrange("(k p) n -> p k n", p=P)
                cols, width = (MIX_COLS[m], 256) if kind == "in" else (256 * m, 256) if kind == "out" else (512 * m, 512)
                slot = (MIX0 + n) % RING
                sp.dma_start(w_slots[slot].rearrange("p (k n) -> p k n", k=2048 // width), w[:, :, cols:cols + width]).then_inc(w_ld[slot], 16)
            ffn_loads(1)
            sp.dma_start(g_final, t["final_g_2"].unsqueeze(0).to_broadcast([P, D])).then_inc(ld_final, 16)
            for tt in range(QT):
                sp.wait_ge(out_ready.sem, tt + 1)
                sp.dma_start(out[0, tt * P:(tt + 1) * P], nrm[:, tt]).then_inc(stored, 16)
            sp.wait_ge(stored, 16 * QT)

        @block.gpsimd
        def _(pool):
            gp = nc.gpsimd
            consts.step(pool, gp.memset(gain_rows, 1.0))
            consts.step(pool, gp.memset(ident, 0.0))
            consts.step(pool, gp.affine_select(out=ident, in_=ident, compare_op=ALU.not_equal, fill=1.0, base=0,
                                               pattern=[[-1, P]], channel_multiplier=1))
            consts.step(pool, gp.memset(ones, 1.0))
            consts.step(pool, gp.memset(eps, EPS))
            consts.step(pool, gp.memset(later, 1.0))
            consts.step(pool, gp.affine_select(out=later, in_=later, compare_op=ALU.is_gt, fill=0.0, base=0,
                                               pattern=[[-1, P]], channel_multiplier=1))
            consts.step(pool, gp.memset(seen, 1.0))
            consts.step(pool, gp.affine_select(out=seen, in_=seen, compare_op=ALU.is_gt, fill=0.0, base=0,
                                               pattern=[[1, P]], channel_multiplier=-1))
            bias_ready.step(pool, gp.memset(mask, 0.0))
            for tt in range(QT):
                bias_ready.step(pool, gp.affine_select(out=mask[:, tt], in_=mask[:, tt], compare_op=ALU.is_ge, fill=NEG,
                                                       base=META + P * tt, pattern=[[-1, KEYS]], channel_multiplier=1))
            pool.wait_ge(ld_bias, 32)
            for tt in range(QT):
                bias_ready.step(pool, gp.affine_select(out=bias[:, :, tt], in_=bias[:, :, tt], compare_op=ALU.is_ge,
                                                       fill=NEG, base=META + P * tt, pattern=[[0, DH], [-1, KEYS]],
                                                       channel_multiplier=1))

            pool.wait_ge(routed.sem, 1)
            for phase, (src, tt) in enumerate((("peer_u", 0), ("peer_u", 1), ("peer_v", 0), ("peer_v", 1))):
                if tt:
                    pool.wait_ge(routed.sem, 2)
                weights = t[src][0]
                with gp.Fori(0, SLOTS // (2 * GB)) as i:
                    for half in range(2):
                        first = (i * 2 + (phase * (SLOTS // GB) + half)) * GB
                        pool.wait_ge(rows_free, first + 1)
                        idx = expert8[:, half * GB:(half + 1) * GB]
                        gp.tensor_copy(idx, expert[tt][:, bass.ds((i * 2 + half) * GB, GB)]).then_inc(expert8_ready.sem, 1)
                        pool.wait_ge(expert8_ready.sem, i * 2 + (phase * (SLOTS // GB) + half + 1))
                        for j in range(GB):
                            pool.wait_ge(rows_free, first + (j + 1))
                            pool.sem_inc(gather_go, 1)
                            gp.indirect_dma_start(out=rows[:, j], out_offset=None, in_=weights,
                                                  in_offset=bass.IndirectOffsetOnAxis(ap=idx[:, j:j + 1], axis=0)).then_inc(rows_ld[j], 16)

        @block.scalar
        def _(sc_e):
            ac = nc.scalar

            def root(name, rows=P):
                k, cols, width = norm_at[name]
                sc_e.wait_ge(sums.sem, k + 1)
                roots.mark(ac.activation(rstd[0:rows, cols], stats[0:rows, cols], ACT.Sqrt, bias=eps[0:rows], scale=1.0 / width))

            def evac(job, pairs, scale=1.0):
                bank = full_bank(sc_e, job, a_at, lane_a, a_full)
                for dst, src in pairs(bank):
                    last = ac.activation(dst, src, ACT.Copy, scale=scale)
                a_free.mark(last)

            sc_e.wait_ge(consts.sem, 9)
            for tt in range(3):
                root(("x", tt), ROWS[tt])
            for tt in range(3):
                evac(("c", tt), lambda b: [(pr[0:ROWS[tt], tt, C_C:C_C + 512], b[0:ROWS[tt], :])])
            for tt in range(3):
                evac(("rope", tt), lambda b: [(pr[0:ROWS[tt], tt, C_ROPE:C_ROPE + ROPE], b[0:ROWS[tt], 0:ROPE])])
            for tt in range(3):
                root(("c", tt), ROWS[tt])
            for tt in range(3):
                evac(("dk", tt), lambda b: [(pr[0:ROWS[tt], tt, C_DK:C_DK + 512], b[0:ROWS[tt], :])])
            for tt in range(QT):
                evac(("dq", tt), lambda b: [(pr[:, tt, C_DQ:C_DQ + 512], b[:, :])])
            for tt in range(3):
                root(("dk", tt), ROWS[tt])
            for tt in range(3):
                for n in range(2):
                    if tt < QT:
                        w = 512 if n == 0 else MH * QK - 512
                        evac(("q", tt, n), lambda b: [(q_row[:, tt, n * 512:n * 512 + w], b[:, 0:w])])
                for n in range(2):
                    def kv(b):
                        b = b[0:ROWS[tt], :].rearrange("p (h c) -> p h c", h=4)
                        k4 = k_row[0:ROWS[tt], tt].rearrange("p (h c) -> p h c", h=MH)[:, 4 * n:4 * n + 4, 0:NOPE]
                        v4 = v_row[0:ROWS[tt], tt].rearrange("p (h c) -> p h c", h=MH)[:, 4 * n:4 * n + 4]
                        return [(k4, b[:, :, 0:NOPE]), (v4, b[:, :, NOPE:])]
                    evac(("kv", tt, n), kv)
            for tt in range(QT):
                root(("dq", tt))
            for tt in range(3):
                evac(("dv", tt), lambda b: [(pr[0:ROWS[tt], tt, C_DV:C_DV + 512], b[0:ROWS[tt], :])])
            for tt in range(3):
                r = ROWS[tt]
                evac(("dkT", tt), lambda b: [(dkT[:, :, COL0[tt]:COL0[tt] + r], b[:, 0:4 * r].rearrange("p (h n) -> p h n", h=4))],
                     scale=gains[:, GAIN["diff_k_norm"]:GAIN["diff_k_norm"] + 1])
            for tt in range(QT):
                evac(("dqT", tt), lambda b: [(dqT[:, :, P * tt:P * tt + P], b[:, :].rearrange("p (h n) -> p h n", h=4))],
                     scale=gains[:, GAIN["diff_q_norm"]:GAIN["diff_q_norm"] + 1])
            for name in (("q", 0), ("k", 0), ("q", 1), ("k", 1), ("k", 2)):
                root(name, ROWS_OF.get(name, P))
            for tt in range(3):
                r = ROWS[tt]
                for n in range(2):
                    if tt < QT:
                        evac(("qT", tt, n), lambda b: [(qT[0:QK, 4 * n:4 * n + 4, P * tt:P * tt + P],
                                                        b[0:QK, :].rearrange("p (h n) -> p h n", h=4))],
                             scale=gains[0:QK, GAIN["mla_qk_norm_q"]:GAIN["mla_qk_norm_q"] + 1])
                for n in range(2):
                    evac(("kT", tt, n), lambda b: [(kT[0:QK, 4 * n:4 * n + 4, COL0[tt]:COL0[tt] + r],
                                                    b[0:QK, 0:4 * r].rearrange("p (h n) -> p h n", h=4))],
                         scale=gains[0:QK, GAIN["mla_qk_norm_k"]:GAIN["mla_qk_norm_k"] + 1])
            sc_e.wait_ge(lam_sums.sem, 1)
            lam_exps.mark(ac.activation(lam[:, 2:4], lam[:, 0:2], ACT.Exp))
            for i in range(len(STEPS) + 1):
                if i < len(STEPS):
                    tt, g = STEPS[i]
                    nk = META + P * (tt + 1)
                    sc_e.wait_ge(m_ready.sem, i + 1)
                    if i >= 2:
                        sc_e.wait_ge(a_full.sem, a_at["pT", i - 2, maps(STEPS[i - 2][1])[-1]] + 1)
                    for m in range(4):
                        last = ac.activation(pb[i % 2][:, m, 0:nk], sc[i % 2][:, m, 0:nk], ACT.Exp,
                                             bias=small[:, 16 * i + 4 + m:16 * i + 5 + m],
                                             accum_out=small[:, 16 * i + 8 + m:16 * i + 9 + m])
                    p_ready.mark(last)
                if i:
                    tt, g = STEPS[i - 1]
                    if i >= 2:
                        sc_e.wait_ge(d_full.sem, d_at["o", i - 2] + 1)
                    for m in maps(g):
                        s = m
                        evac(("pT", i - 1, m), lambda b: [(pT[0:META, s, 0], b[0:META, 0:P]),
                                                          (pT[:, s, 1:2 + tt], b[:, P:P * (2 + tt)].rearrange("p (k n) -> p k n", n=P))])
            root("subln")
            root("h1")
            for n in range(4):
                evac(("keysT", n), lambda b: [(keysT[:, 4 * n:4 * n + 4], b[:, :].rearrange("p (s n) -> p s n", s=4))])
            for n in range(8):
                evac(("pq", n), lambda b: [(pqT[:, 2 * n:2 * n + 2], b[:, :].rearrange("p (s n) -> p s n", s=2))])
            for tt in range(QT):
                for n in range(4):
                    evac(("ps", tt, n), lambda b: [(ps[tt][:, 4 * n:4 * n + 4], b[:, :].rearrange("p (s n) -> p s n", s=4))])
            c_ready.mark(ac.activation(c_act, gains[:, GAIN["c_2"]:GAIN["c_2"] + KD], ACT.Silu))

            def soft(tt):
                sc_e.wait_ge(bests.sem, tt + 1)
                softs.mark(ac.activation(gate[tt], gate[tt], ACT.Exp))

            for n in range(ADA // 512):
                s, m, half = n // 6, n % 6 // 2, n % 2
                if n == 2:
                    soft(0)
                if n == 8:
                    soft(1)
                if m == 2:
                    evac(("ada", n), lambda b: [(gates[:, s, half * 512:(half + 1) * 512], b[:, :])], scale=(0.5, 1.0, 0.5)[s])
                else:
                    bank = full_bank(sc_e, ("ada", n), a_at, lane_a, a_full)
                    a_free.mark(ac.activation(mod_row[0:1], bank[0:1, :], ACT.Copy))
                    evac(("mod", n), lambda b: [(mod[:, s, m, half * 4:half * 4 + 4], b[:, 0:4])])
            for tt in range(QT):
                sc_e.wait_ge(dots_ready.sem, tt + 1)
                acts_ready.mark(ac.activation(dots[tt], dots[tt], ACT.Gelu))

            def norm_part(s):
                b = slice(2 * s, 2 * s + 2)
                sc_e.wait_ge(b_sums.sem, s + 1)
                b_roots.mark(ac.activation(rstd[:, b], stats[:, b], ACT.Sqrt, bias=eps, scale=1.0 / D))
                if s == 3:
                    return
                sc_e.wait_ge(mod_ready.sem, 3)
                for j in (1, 3):
                    sc_e.wait_ge(flipped.sem, 4 * s + j + 1)
                    for k in (2 * j, 2 * j + 1):
                        u_odd.mark(ac.activation(uT[:, k], psum[j][:, (k % 2) * SEQ:(k % 2 + 1) * SEQ], ACT.Identity,
                                                 scale=mod[:, s, 1, k:k + 1], bias=mod[:, s, 0, k:k + 1]))

            def silu_part(f):
                def tile(j, c):
                    sc_e.wait_ge(gu_full.sem, j + (f * FT + 1))
                    if f or not isinstance(j, int) or j >= 2:
                        sc_e.wait_ge(h_ready.sem, j + (f * FT - 1))
                    ac.activation(silu[:, c % 2], psum[c][:, 0:SEQ], ACT.Silu).then_inc(silu_ready.sem, 1)
                each_tile(ac, tile)

            norm_part(0)
            silu_part(0)
            norm_part(1)

            def x_out(n):
                sc_e.wait_ge(x_full.sem, n + 1)
                bank = psum[4 + n % 4]
                two = bank[:, :].rearrange("p (a n) -> p a n", a=2)
                what, m = ("q", "k", "v", "cb", "cc", "cx", "ga", "ga", "gb", "gb")[n // 2], n % 2
                if what in ("q", "k"):
                    last = ac.activation((sqT if what == "q" else skT)[:, 2 * m:2 * m + 2], two, ACT.Copy)
                elif what == "v":
                    last = ac.activation(sv_row[:, :, 256 * m:256 * m + 256], two, ACT.Copy)
                elif what in ("cb", "cc", "cx"):
                    last = ac.activation({"cb": cbT, "cc": ccT, "cx": cxT}[what][:, 2 * m:2 * m + 2], two, ACT.Copy)
                else:
                    for j in range(2):
                        k = 2 * ((n - 12) % 4) + j
                        col = GAIN["b_merge_2"] + (0 if what == "ga" else KD) + k
                        last = ac.activation((sgaT if what == "ga" else sgbT)[:, k], two[:, j], ACT.Sigmoid, bias=gains[:, col:col + 1])
                x_act.mark(last)

            def soft_part(r):
                sc_e.wait_ge(min_ready.sem, r + 1)
                act.step(sc_e, ac.activation(zx, zx, ACT.Exp))
                e_ready.mark(ac.activation(zx, zx, ACT.Ln, bias=1.0))

            def prob_part(r):
                sc_e.wait_ge(log_ready.sem, r + 1)
                prob_ready.mark(ac.activation(zx, zlog, ACT.Exp))

            for n in range(6):
                x_out(n)
            soft_part(0)
            for n in range(6, 12):
                x_out(n)
            prob_part(0)
            soft_part(1)
            prob_part(1)
            for n in range(12, 20):
                x_out(n)
            norm_part(2)
            silu_part(1)
            norm_part(3)

        @block.tensor
        def _(pe):
            te = nc.tensor

            def d_bank(job):
                return open_bank(pe, job, d_at, lane_d, d_free)

            def a_bank(job):
                return open_bank(pe, job, a_at, lane_a, a_free)

            def flip(bank, at, src, rows, cols):
                return te.transpose(bank[0:cols, at:at + rows], src, ident[0:rows, 0:rows])

            pe.wait_ge(consts.sem, 9)
            pe.wait_ge(ld_gain, 16 * (len(gain_src) + 7))
            bank = d_bank("gains")
            d_full.mark(flip(bank, 0, gain_rows, P, P))
            pe.wait_ge(ld_hot, 32)
            for n in range(2):
                w = (512, KEYS + SEQ - 512)[n]
                bank = d_bank(("fill", n))
                d_full.mark(te.matmul(bank[0:4, 0:w], rel, onehot[:, n * 512:n * 512 + w], start=True, stop=True))
            for tt in range(3):
                pe.wait_ge(xn_ready.sem, tt + 1)
                for b in range(2):
                    bank = d_bank(("nT", tt, b))
                    for j in range(4):
                        k = 4 * b + j
                        last = flip(bank, j * ROWS[tt], xn[0:ROWS[tt], tt, k * P:(k + 1) * P], ROWS[tt], P)
                    d_full.mark(last)

            def chunk(name, rhs, width, tiles):
                for tt in tiles:
                    bank = a_bank((name, tt))
                    pe.wait_ge(d_free.sem, d_at["nT", tt, 1] + 1)
                    for k in range(KD):
                        last = te.matmul(bank[0:ROWS[tt], 0:width], nT[:, k, COL0[tt]:COL0[tt] + ROWS[tt]], rhs[:, k],
                                         start=(k == 0), stop=(k == KD - 1))
                    a_full.mark(last)

            pe.wait_ge(ld_c, 16)
            chunk("c", w_slot[0], 512, range(3))
            pe.wait_ge(ld_rope_w, 16)
            chunk("rope", w_rope, ROPE, range(3))
            pe.wait_ge(ld_dk, 16)
            chunk("dk", w_slot[1], 512, range(3))
            for tt in range(3):
                pe.wait_ge(c_row_ready.sem, tt + 1)
                bank = d_bank(("cT", tt))
                for j in range(4):
                    last = flip(bank, j * ROWS[tt], pr[0:ROWS[tt], tt, j * P:(j + 1) * P], ROWS[tt], P)
                d_full.mark(last)
            pe.wait_ge(ld_dq, 16)
            chunk("dq", w_slot[2], 512, range(QT))
            pe.wait_ge(ld_up, 32)
            for tt in range(3):
                pe.wait_ge(d_free.sem, d_at["cT", tt] + 1)
                cols = slice(COL0[tt], COL0[tt] + ROWS[tt])
                for n in range(2):
                    if tt < QT:
                        w = 512 if n == 0 else MH * QK - 512
                        bank = a_bank(("q", tt, n))
                        for k in range(2):
                            last = te.matmul(bank[:, 0:w], cT[:, k, cols], w_uq[:, k, n * 512:n * 512 + w], start=(k == 0), stop=(k == 1))
                        a_full.mark(last)
                for n in range(2):
                    bank = a_bank(("kv", tt, n))
                    for k in range(2):
                        last = te.matmul(bank[0:ROWS[tt], :], cT[:, 2 + k, cols], w_ukv[:, k, n * 512:(n + 1) * 512],
                                         start=(k == 0), stop=(k == 1))
                    a_full.mark(last)
            pe.wait_ge(ld_dv, 16)
            chunk("dv", w_slot[0], 512, range(3))
            for tt in range(3):
                pe.wait_ge(dk_ready.sem, tt + 1)
                bank = a_bank(("dkT", tt))
                for h in range(DH):
                    last = flip(bank, h * ROWS[tt], pr[0:ROWS[tt], tt, C_DK + h * P:C_DK + (h + 1) * P], ROWS[tt], P)
                a_full.mark(last)
            for tt in range(QT):
                pe.wait_ge(dq_ready.sem, tt + 1)
                bank = a_bank(("dqT", tt))
                for h in range(DH):
                    last = flip(bank, h * P, pr[:, tt, C_DQ + h * P:C_DQ + (h + 1) * P], P, P)
                a_full.mark(last)
            for tt in range(3):
                for which, row in (("q", q_row), ("k", k_row)):
                    if which == "q" and tt == 2:
                        continue
                    pe.wait_ge(head_ready.sem, {("q", 0): 1, ("k", 0): 2, ("q", 1): 3, ("k", 1): 4, ("k", 2): 5}[which, tt])
                    for n in range(2):
                        bank = a_bank((which + "T", tt, n))
                        for j in range(4):
                            h = 4 * n + j
                            last = flip(bank, j * ROWS[tt], row[0:ROWS[tt], tt, h * QK:(h + 1) * QK], ROWS[tt], QK)
                        a_full.mark(last)
            for i in range(len(STEPS) + 1):
                if i < len(STEPS):
                    tt, g = STEPS[i]
                    nk = META + P * (tt + 1)
                    if i == 0:
                        pe.wait_ge(a_free.sem, a_at["kT", 2, 1] + 1)
                    for m in range(4):
                        bank = d_bank(("s", i, m))
                        if g < 2:
                            h = 4 * g + m
                            ins = te.matmul(bank[:, 0:nk], qT[0:QK, h, P * tt:P * tt + P], kT[0:QK, h, 0:nk], start=True, stop=True)
                        else:
                            h, c = 2 * (g - 2) + m // 2, DD * (m % 2)
                            ins = te.matmul(bank[:, 0:nk], dqT[c:c + DD, h, P * tt:P * tt + P], dkT[c:c + DD, h, 0:nk], start=True, stop=True)
                        d_full.mark(ins)
                if i:
                    tt, g = STEPS[i - 1]
                    if g < 2:
                        pe.wait_ge(p_ready.sem, i)
                    else:
                        pe.wait_ge(a_ready.sem, 2 * tt + g - 1)
                    for m in maps(g):
                        bank = a_bank(("pT", i - 1, m))
                        src = pb[(i - 1) % 2][:, m]
                        flip(bank, 0, src[:, 0:META], P, META)
                        for k in range(tt + 1):
                            last = flip(bank, P * (k + 1), src[:, META + P * k:META + P * (k + 1)], P, P)
                        a_full.mark(last)
                    bank = d_bank(("o", i - 1))
                    for m in maps(g):
                        pe.wait_ge(a_free.sem, a_at["pT", i - 1, m] + 1)
                        if g < 2:
                            h, w = 4 * g + m, MV
                            dst, v = bank[:, m * MV:(m + 1) * MV], v_row
                            vc = slice(h * MV, (h + 1) * MV)
                        else:
                            h = 2 * (g - 2) + m // 2
                            dst, v = bank[:, (m // 2) * DV:(m // 2 + 1) * DV], pr
                            vc = slice(C_DV + h * DV, C_DV + (h + 1) * DV)
                        s = m
                        te.matmul(dst, pT[0:META, s, 0], v[0:META, 2, vc], start=True, stop=False)
                        for k in range(tt + 1):
                            last = te.matmul(dst, pT[:, s, 1 + k], v[:, k, vc], start=False, stop=(k == tt))
                    d_full.mark(last)
            for tt in range(QT):
                pe.wait_ge(y_ready.sem, 1)
                for b in range(2):
                    bank = d_bank(("yT", tt, b))
                    for j in range(4):
                        last = flip(bank, j * P, y[:, tt, (4 * b + j) * P:(4 * b + j + 1) * P], P, P)
                    d_full.mark(last)
            pe.wait_ge(ld_wo, 32)
            pe.wait_ge(d_free.sem, d_at["yT", QT - 1, 1] + 1)
            for n in range(2):
                for tt in range(QT):
                    bank = d_bank(("wo", n, tt))
                    for k in range(KD):
                        last = te.matmul(bank[:, :], yT[:, k, P * tt:P * tt + P], wo_half[n][:, k], start=(k == 0), stop=(k == KD - 1))
                    d_full.mark(last)

            pe.wait_ge(ld_keys, 16)
            for n in range(4):
                bank = a_bank(("keysT", n))
                for j in range(4):
                    last = flip(bank, j * P, keys[:, 4 * n + j], P, P)
                a_full.mark(last)
            for tt in range(QT):
                pe.wait_ge(hn_ready.sem, tt + 1)
                for b in range(2):
                    bank = d_bank(("hnT", tt, b))
                    for j in range(4):
                        last = flip(bank, j * P, hn[:, tt, (4 * b + j) * P:(4 * b + j + 1) * P], P, P)
                    d_full.mark(last)
            pe.wait_ge(d_free.sem, d_at["hnT", QT - 1, 1] + 1)
            for n in range(8):
                if n % 2 == 0:
                    pe.wait_ge(ld_wq[n // 2], 16)
                bank = a_bank(("pq", n))
                for j in range(2):
                    for k in range(KD):
                        last = te.matmul(bank[:, j * SEQ:(j + 1) * SEQ], wq_chunk[n // 2][:, k, (n % 2) * 256 + j * P:(n % 2) * 256 + (j + 1) * P],
                                         hnT[:, k], start=(k == 0), stop=(k == KD - 1))
                a_full.mark(last)
            pe.wait_ge(a_free.sem, a_at["pq", 7] + 1)
            for tt in range(QT):
                for n in range(4):
                    bank = a_bank(("ps", tt, n))
                    for j in range(4):
                        last = te.matmul(bank[:, j * NK:(j + 1) * NK], pqT[:, 4 * n + j, P * tt:P * tt + P], keysT[:, 4 * n + j], start=True, stop=True)
                    a_full.mark(last)
            pe.wait_ge(c_ready.sem, 1)
            pe.wait_ge(ld_bada, 16)
            for n in range(ADA // 512):
                bank = a_bank(("ada", n))
                pe.wait_ge(slot_ld[n % 3], 16 * (n // 3 + 1))
                te.matmul(bank[:, :], ident[0:ADA // 512, n:n + 1].to_broadcast([ADA // 512, P]), b_ada, start=True, stop=False)
                for k in range(KD):
                    last = te.matmul(bank[:, :], c_act[:, k:k + 1].to_broadcast([P, P]), ada_chunk[n % 3][:, k], start=False, stop=(k == KD - 1))
                a_full.mark(last)
                if n % 6 < 4:
                    pe.wait_ge(a_free.sem, a_at["ada", n] + 1)
                    bank = a_bank(("mod", n))
                    for j in range(4):
                        last = flip(bank, j, mod_row[0:1, j * P:(j + 1) * P], 1, P)
                    a_full.mark(last)

            def transposed_norm(s):
                for j in range(4):
                    for tt in range(QT):
                        if j == 0:
                            pe.wait_ge(n_ready.sem, QT * s + tt + 1)
                    for a in range(2):
                        for tt in range(QT):
                            last = flip(psum[j], a * SEQ + tt * P, nrm[:, tt, (2 * j + a) * P:(2 * j + a + 1) * P], P, P)
                    flipped.mark(last)
                pe.wait_ge(u_even.sem, 4 * (s + 1))
                pe.wait_ge(u_odd.sem, 4 * (s + 1))

            def ffn(f):
                def slot_of(parity, c):
                    return (FIRST[f] + 3 * parity + c) % RING

                def wait_slot(i, parity, c):
                    pe.wait_ge(w_ld[slot_of(parity, c)], i * 16 + 16 * ((FIRST[f] + 3 * parity + c) // RING + 1))

                def up(j, c, i):
                    if f or not isinstance(j, int) or j >= 4:
                        pe.wait_ge(h_ready.sem, j + (f * FT - 3))
                    parity = c // 2
                    for w in range(2):
                        if c % 2 == 0:
                            wait_slot(i, parity, w)
                        weight = w_slots[slot_of(parity, w)].rearrange("p (k n) -> p k n", k=KD)
                        for k in range(KD):
                            last = te.matmul(psum[c][:, w * SEQ:(w + 1) * SEQ], weight[:, k, (c % 2) * P:(c % 2 + 1) * P], uT[:, k],
                                             start=(k == 0), stop=(k == KD - 1), skip_group_check=True)
                    last.then_inc(gu_full.sem, 1)

                def down(j, c, i, first=False, final=False):
                    pe.wait_ge(h_ready.sem, j + (f * FT + 1))
                    parity = c // 2
                    if c % 2 == 0:
                        wait_slot(i, parity, 2)
                    weight = w_slots[slot_of(parity, 2)].rearrange("p (j n) -> p j n", j=2)
                    for tt in range(QT):
                        for n in range(2):
                            last = te.matmul(psum[4 + 2 * tt + n][:, :], hT[:, c, tt * P:(tt + 1) * P], weight[:, c % 2, n * 512:(n + 1) * 512],
                                             start=first, stop=final, skip_group_check=True)
                    last.then_inc(down_done.sem, 1)

                for j in range(4):
                    up(j, j, 0)
                    if j:
                        down(j - 1, j - 1, 0, first=(j == 1))
                with te.Fori(1, 5) as i:
                    for c in range(4):
                        up(i * 4 + c, c, i)
                        if c:
                            down(i * 4 + (c - 1), c - 1, i)
                        else:
                            down(i * 4 - 1, 3, i - 1)
                for j in (20, 21):
                    up(j, j % 4, 5)
                    down(j - 1, (j - 1) % 4, (j - 1) // 4)
                down(21, 1, 5, final=True)

            transposed_norm(0)
            ffn(0)
            pe.wait_ge(ffn_out.sem, 1)
            transposed_norm(1)

            def x_bank(job):
                n = x_at[job]
                if 4 <= n < 24:
                    pe.wait_ge(x_act.sem, n - 3)
                elif n >= 24:
                    pe.wait_ge(x_dve.sem, n - 23)
                return psum[4 + n % 4]

            def z_bank(job):
                n = z_at[job]
                if n >= 4:
                    pe.wait_ge(z_free.sem, n - 3)
                return psum[n % 4]

            def weight(n, width):
                slot = (MIX0 + n) % RING
                pe.wait_ge(w_ld[slot], 16 * ((MIX0 + n) // RING + 1))
                return w_slots[slot].rearrange("p (k n) -> p k n", k=2048 // width)

            def project(n):
                w = weight(n, 256)
                bank = x_bank(("in", n))
                for a in range(2):
                    for k in range(KD):
                        if 4 <= n < 6:
                            last = te.matmul(bank[:, a * 256:(a + 1) * 256], uT[:, k, a * P:(a + 1) * P], w[:, k], start=(k == 0), stop=(k == KD - 1))
                        else:
                            last = te.matmul(bank[:, a * SEQ:(a + 1) * SEQ], w[:, k, a * P:(a + 1) * P], uT[:, k], start=(k == 0), stop=(k == KD - 1))
                x_full.mark(last)

            def z_maps(r):
                for h in range(4):
                    bank = z_bank(("z", r, h))
                    pair, c = (4 * r + h) // 2, SD * (h % 2)
                    rows_ = slice(c, c + SD)
                    te.matmul(bank[:, 0:SEQ], skT[rows_, pair, 0:P], sqT[rows_, pair], start=True, stop=True)
                    z_full.mark(te.matmul(bank[:, SEQ:ZW], skT[rows_, pair, P:], sqT[rows_, pair, P:], start=True, stop=True))

            def remainders(r):
                pe.wait_ge(sp_ready.sem, r + 1)
                for h in range(4):
                    bank = z_bank(("rem", r, h))
                    te.matmul(bank[:, 0:SEQ], later, zsp[:, h, 0:SEQ], start=True, stop=False, skip_group_check=True)
                    te.matmul(bank[:, P:SEQ], ones, zsp[:, h, SEQ:ZW], start=False, stop=True, skip_group_check=True)
                    z_full.mark(te.matmul(bank[:, SEQ:ZW], later, zsp[:, h, SEQ:ZW], start=True, stop=True, skip_group_check=True))

            def attend(r):
                pe.wait_ge(masked.sem, r + 1)
                bank = z_bank(("o", r))
                for h in range(4):
                    c, at_ = SD * (h % 2), SEQ * (h // 2)
                    vc = slice((4 * r + h) * SD, (4 * r + h + 1) * SD)
                    te.matmul(bank[c:c + SD, at_:at_ + SEQ], sv_row[:, 0, vc], zx[:, h, 0:SEQ], start=True, stop=False, skip_group_check=True)
                    last = te.matmul(bank[c:c + SD, at_ + P:at_ + SEQ], sv_row[:, 1, vc], zx[:, h, SEQ:ZW], start=False, stop=True, skip_group_check=True)
                z_full.mark(last)

            for n in range(6):
                project(n)
            pe.wait_ge(x_act.sem, 6)
            z_maps(0)
            for n in range(6, 9):
                project(n)
            remainders(0)
            for n in range(9, 12):
                project(n)
            attend(0)
            z_maps(1)
            for n in range(12, 14):
                project(n)
            remainders(1)
            for n in range(14, 16):
                project(n)
            attend(1)
            for n in range(16, 20):
                project(n)
            for name, src, ready, kind in (("ya", convT, conv_ready, "conv"), ("yb", oT, z_free, "attn")):
                pe.wait_ge(ready.sem, 1 if name == "ya" else len(z_jobs))
                for n in range(4):
                    if n % 2 == 0:
                        w = weight(20 + (2 if name == "yb" else 0) + n // 2, 512)
                    bank = x_bank((name, n))
                    for a in range(2):
                        for k in range(4):
                            col = (n % 2) * 256 + a * P
                            last = te.matmul(bank[:, a * SEQ:(a + 1) * SEQ], w[:, k, col:col + P], src[:, k], start=(k == 0), stop=(k == 3))
                    x_full.mark(last)
            pe.wait_ge(merged_ready.sem, 4)
            for n in range(4):
                w = weight(24 + n, 256)
                bank = x_bank(("wo", n))
                for tt in range(QT):
                    for k in range(KD):
                        last = te.matmul(bank[:, tt * 256:(tt + 1) * 256], sgaT[:, k, tt * P:(tt + 1) * P], w[:, k], start=(k == 0), stop=(k == KD - 1))
                x_full.mark(last)
            transposed_norm(2)
            ffn(1)

        @block.vector
        def _(ve):
            v = nc.vector

            def take(job):
                return full_bank(ve, job, d_at, lane_d, d_full)

            def step(ins):
                dve.step(ve, ins)

            def sum_squares(name, src, rows=P):
                k, cols, width = norm_at[name]
                n = cols.stop - cols.start
                sq = tmp[0:rows, 0:n * width].rearrange("p (g w) -> p g w", g=n)
                step(v.tensor_tensor(sq, src, src, ALU.mult))
                assert sums.sent == k
                sums.step(ve, v.tensor_reduce(stats[0:rows, cols], sq, AX, ALU.add))

            def invert(name, rows=P):
                k, cols, width = norm_at[name]
                ve.wait_ge(roots.sem, k + 1)
                step(v.reciprocal(rstd[0:rows, cols], rstd[0:rows, cols]))
                return rstd[0:rows, cols]

            bank = take("gains")
            gains_ready.step(ve, v.tensor_copy(gains, bank[:, 0:P]))
            d_free.mark(v.tensor_copy(small[:, 0:1], bank[:, 0:1]))
            for n in range(2):
                w = (512, KEYS + SEQ - 512)[n]
                bank = take(("fill", n))
                last = v.tensor_copy(fill[:, n * 512:n * 512 + w], bank[0:4, 0:w])
                d_free.step(ve, last)
            fill_ready.step(ve, v.tensor_copy(small[:, 1:2], small[:, 0:1]))
            for tt in range(3):
                r = ROWS[tt]
                src = hx[:, tt] if tt < QT else hm
                ve.wait_ge(ld_x[tt], 16)
                sums.step(ve, v.tensor_tensor_reduce(out=tmp[0:r], in0=src[0:r], in1=src[0:r], scale=1.0, scalar=0.0,
                                                     op0=ALU.mult, op1=ALU.add, accum_out=stats[0:r, tt:tt + 1]))
            for tt in range(3):
                r = ROWS[tt]
                src = hx[:, tt] if tt < QT else hm
                inv = invert(("x", tt), r)
                xn_ready.mark(v.tensor_scalar(xn[0:r, tt], src[0:r], inv, None, ALU.mult))
            for tt in range(3):
                r = ROWS[tt]
                for b in range(2):
                    bank = take(("nT", tt, b))
                    g = GAIN["attn_norm"] + 4 * b
                    d_free.mark(v.tensor_tensor(nT[:, 4 * b:4 * b + 4, COL0[tt]:COL0[tt] + r],
                                                bank[:, 0:4 * r].rearrange("p (k n) -> p k n", k=4),
                                                spread(gains[:, g:g + 4], P, 4, r), ALU.mult))
            ve.wait_ge(ld_small, 16 * 9)
            pairs = lam_in.rearrange("p (a b) d -> p a b d", b=2)
            lam_sq = tmp[:, 0:2 * DD].rearrange("p (a d) -> p a d", a=2)
            step(v.tensor_tensor(lam_sq, pairs[:, :, 0], pairs[:, :, 1], ALU.mult))
            lam_sums.step(ve, v.tensor_reduce(lam[:, 0:2], lam_sq, AX, ALU.add))
            for tt in range(3):
                r = ROWS[tt]
                ve.wait_ge(a_free.sem, a_at["c", tt] + 1)
                src = pr[0:r, tt, 0:512].rearrange("p (g w) -> p g w", g=2)
                k, cols, _ = norm_at["c", tt]
                for j in range(2):
                    ins = v.tensor_tensor_reduce(out=tmp[0:r, 256 * j:256 * j + 256], in0=src[:, j], in1=src[:, j], scale=1.0, scalar=0.0,
                                                 op0=ALU.mult, op1=ALU.add, accum_out=stats[0:r, cols.start + j:cols.start + j + 1])
                    (step if j == 0 else lambda x: sums.step(ve, x))(ins)
            for tt in range(3):
                r = ROWS[tt]
                inv = invert(("c", tt), r)
                src = pr[0:r, tt, 0:512].rearrange("p (g w) -> p g w", g=2)
                c_row_ready.mark(v.tensor_tensor(src, src, spread(inv, r, 2, 256), ALU.mult))
            for tt in range(3):
                r = ROWS[tt]
                bank = take(("cT", tt))
                g = GAIN["mla_q_norm"]
                d_free.mark(v.tensor_tensor(cT[:, :, COL0[tt]:COL0[tt] + r], bank[:, 0:4 * r].rearrange("p (k n) -> p k n", k=4),
                                            spread(gains[:, g:g + 4], P, 4, r), ALU.mult))
            def half_heads(name, tt, c, ready):
                r = ROWS[tt]
                src = pr[0:r, tt, c:c + 512].rearrange("p (g w) -> p g w", w=DD)
                if ready is None:
                    sum_squares((name, tt), src, r)
                else:
                    ready.mark(v.tensor_tensor(src, src, spread(invert((name, tt), r), r, 8, DD), ALU.mult))
            for tt in range(3):
                ve.wait_ge(a_free.sem, a_at["dk", tt] + 1)
                half_heads("dk", tt, C_DK, None)
            for tt in range(3):
                half_heads("dk", tt, C_DK, dk_ready)
            for tt in range(QT):
                ve.wait_ge(a_free.sem, a_at["dq", tt] + 1)
                half_heads("dq", tt, C_DQ, None)
            for tt in range(QT):
                half_heads("dq", tt, C_DQ, dq_ready)
            order = [("q", 0), ("k", 0), ("q", 1), ("k", 1), ("k", 2)]
            def heads(which, tt):
                row = (q_row if which == "q" else k_row)[0:ROWS[tt], tt]
                return row.rearrange("p (h c) -> p h c", h=MH)
            for which, tt in order:
                r = ROWS[tt]
                ve.wait_ge(a_free.sem, a_at["q" if which == "q" else "kv", tt, 1] + 1)
                hd = heads(which, tt)
                if which == "k":
                    krope = pr[0:r, tt, C_ROPE:C_ROPE + ROPE].unsqueeze(1).to_broadcast([r, MH, ROPE])
                    step(v.tensor_copy(hd[:, :, NOPE:], krope))
                sum_squares((which, tt), hd, r)
            for which, tt in order:
                r = ROWS[tt]
                hd = heads(which, tt)
                step(v.tensor_tensor(hd, hd, spread(invert((which, tt), r), r, MH, QK), ALU.mult))
                a4, b4, g4 = (rot[0:r, s] for s in range(3))
                step(v.tensor_tensor(g4, hd[:, :, NOPE:], g_rope[0:r, 0 if which == "q" else 1].unsqueeze(1).to_broadcast([r, MH, ROPE]), ALU.mult))
                cs = rope[0:r, tt].rearrange("p (w c) -> p w c", w=2)
                halves = [x.rearrange("p h (w c) -> p h w c", w=2) for x in (a4, b4, g4)]
                for j in range(2):
                    tab = cs[:, j].unsqueeze(1).unsqueeze(1).to_broadcast([r, MH, 2, HALF])
                    step(v.tensor_tensor(halves[j], halves[2], tab, ALU.mult))
                step(v.tensor_tensor(hd[:, :, NOPE:NOPE + HALF], halves[0][:, :, 0], halves[1][:, :, 1], ALU.subtract))
                head_ready.mark(v.tensor_tensor(hd[:, :, NOPE + HALF:], halves[0][:, :, 1], halves[1][:, :, 0], ALU.add))
            ve.wait_ge(lam_exps.sem, 1)
            step(v.tensor_scalar(lam[:, 0:1], lam[:, 2:3], LAMBDA_INIT, lam[:, 3:4], ALU.add, ALU.subtract))
            ve.wait_ge(bias_ready.sem, 5)
            for i in range(len(STEPS) + 1):
                if i < len(STEPS):
                    tt, g = STEPS[i]
                    nk = META + P * (tt + 1)
                    if i >= 2:
                        ve.wait_ge(p_ready.sem, i - 1)
                    for m in range(4):
                        bank = take(("s", i, m))
                        add = mask[:, tt, 0:nk] if g < 2 else bias[:, 2 * (g - 2) + m // 2, tt, 0:nk]
                        d_free.mark(v.scalar_tensor_tensor(out=sc[i % 2][:, m, 0:nk], in0=bank[:, 0:nk],
                                                           scalar=float((QK if g < 2 else DD) ** -0.5), in1=add, op0=ALU.mult, op1=ALU.add))
                    ve.wait_ge(d_free.sem, d_free.sent)
                    step(v.tensor_reduce(small[:, 16 * i:16 * i + 4], sc[i % 2][:, :, 0:nk], AX, ALU.max))
                    m_ready.mark(v.tensor_scalar(small[:, 16 * i + 4:16 * i + 8], small[:, 16 * i:16 * i + 4], -1.0, None, ALU.mult))
                if i:
                    tt, g = STEPS[i - 1]
                    nk = META + P * (tt + 1)
                    z = small[:, 16 * i - 8:16 * i - 4]
                    rz = small[:, 16 * i - 4:16 * i]
                    ve.wait_ge(p_ready.sem, i)
                    step(v.reciprocal(rz, z))
                    if g >= 2:
                        p4 = pb[(i - 1) % 2]
                        step(v.tensor_scalar(z, rz, lam[:, 0:1], -1.0, ALU.mult, ALU.mult))
                        for m in maps(g):
                            step(v.tensor_scalar(p4[:, m, 0:nk], p4[:, m, 0:nk], rz[:, m:m + 1], None, ALU.mult))
                            ins = v.scalar_tensor_tensor(out=p4[:, m, 0:nk], in0=p4[:, m + 1, 0:nk], scalar=z[:, m + 1:m + 2],
                                                         in1=p4[:, m, 0:nk], op0=ALU.mult, op1=ALU.add)
                        a_ready.mark(ins)
                    bank = take(("o", i - 1))
                    dst = y[:, tt, 256 * g:256 * g + 256]
                    if g < 2:
                        d_free.mark(v.tensor_tensor(dst.rearrange("p (h c) -> p h c", h=4), bank[:, 0:256].rearrange("p (h c) -> p h c", h=4),
                                                    spread(rz, P, 4, MV), ALU.mult))
                    else:
                        d_free.mark(v.tensor_copy(dst, bank[:, 0:256]))
            ve.wait_ge(d_free.sem, d_free.sent)
            yd = y[:, :, 512:].rearrange("p t (h c) -> p t h c", h=DH)
            k, cols, _ = norm_at["subln"]
            sq4 = tmp[:, 0:QT * DH * DV].rearrange("p (t h c) -> p t h c", t=QT, h=DH)
            step(v.tensor_tensor(sq4, yd, yd, ALU.mult))
            sums.step(ve, v.tensor_reduce(stats[:, cols].rearrange("p (t h) -> p t h", t=QT), sq4, AX, ALU.add))
            inv = invert("subln").rearrange("p (t h) -> p t h", t=QT)
            y_ready.mark(v.tensor_tensor(yd, yd, spread(inv, P, QT, DH, DV), ALU.mult))
            for tt in range(QT):
                for b in range(2):
                    bank = take(("yT", tt, b))
                    dst = yT[:, 4 * b:4 * b + 4, P * tt:P * tt + P]
                    src = bank[:, :].rearrange("p (k n) -> p k n", k=4)
                    if b == 0:
                        d_free.mark(v.tensor_copy(dst, src))
                    else:
                        g = GAIN["diff_subln"]
                        d_free.mark(v.tensor_scalar(dst, src, gains[:, g:g + 1], 1.0 - LAMBDA_INIT, ALU.mult, ALU.mult))
            for n in range(2):
                for tt in range(QT):
                    bank = take(("wo", n, tt))
                    dst = hx[:, tt, n * 512:(n + 1) * 512]
                    d_free.mark(v.tensor_tensor(dst, dst, bank[:, :], ALU.add))
            ve.wait_ge(d_free.sem, d_free.sent)
            for tt in range(QT):
                k, cols, _ = norm_at["h1"]
                ins = v.tensor_tensor_reduce(out=tmp, in0=hx[:, tt], in1=hx[:, tt], scale=1.0, scalar=0.0, op0=ALU.mult,
                                             op1=ALU.add, accum_out=stats[:, cols.start + tt:cols.start + tt + 1])
                (step if tt == 0 else lambda x: sums.step(ve, x))(ins)
            inv = invert("h1")
            ve.wait_ge(ld_gffn, 16)
            for tt in range(QT):
                hn_ready.mark(v.scalar_tensor_tensor(out=hn[:, tt], in0=hx[:, tt], scalar=inv[:, tt:tt + 1], in1=g_ffn, op0=ALU.mult, op1=ALU.mult))
            for tt in range(QT):
                for b in range(2):
                    bank = take(("hnT", tt, b))
                    d_free.mark(v.tensor_copy(hnT[:, 4 * b:4 * b + 4, P * tt:P * tt + P], bank[:, :].rearrange("p (k n) -> p k n", k=4)))
            ve.wait_ge(a_free.sem, a_at["pq", 7] + 1)
            for j in range(TOPK):
                last = v.memset(iota16[:, j:j + 1], float(j))
            step(last)

            def top16(values, vals, idxs):
                for x, o in zip(values, vals):
                    last = v.max(out=o[:, 0:8], in_=x)
                step(last)
                for x, o, ix in zip(values, vals, idxs):
                    last = v.max_index(out=ix[:, 0:8], in_max=o[:, 0:8], in_values=x)
                step(last)
                for x, o in zip(values, vals):
                    last = v.match_replace(out=x, in_to_replace=o[:, 0:8], in_values=x, imm_value=-3e38)
                step(last)
                for x, o in zip(values, vals):
                    last = v.max(out=o[:, 8:16], in_=x)
                step(last)
                for x, o, ix in zip(values, vals, idxs):
                    last = v.max_index(out=ix[:, 8:16], in_max=o[:, 8:16], in_values=x)
                step(last)

            def per_head(tab):
                return tab.rearrange("p (h k) -> p h k", h=PH)

            for tt in range(QT):
                ve.wait_ge(a_free.sem, a_at["ps", tt, 3] + 1)
                n = 2 * PH
                top16([ps[tt][:, s] for s in range(n)], [top_v[:, s] for s in range(n)], [top_i[:, s] for s in range(n)])
                step(v.tensor_copy(top_f, top_i))
                pair = top_v.rearrange("p (h s) k -> p h s k", s=2)
                cand = wide[0]
                ve.wait_ge(a_full.sem, a_at["ps", 1, 3] + 1)
                step(v.tensor_tensor(cand, spread(pair[:, :, 0], P, PH, TOPK, TOPK),
                                     pair[:, :, 1].unsqueeze(2).to_broadcast([P, PH, TOPK, TOPK]), ALU.add))
                top16([cand[:, h].rearrange("p a b -> p (a b)") for h in range(PH)], [per_head(best)[:, h] for h in range(PH)],
                      [per_head(flat)[:, h] for h in range(PH)])
                bests.mark(v.tensor_tensor(per_head(gate[tt]), per_head(best), spread(per_head(best)[:, :, 0], P, PH, TOPK), ALU.subtract))
                idx_pair = top_f.rearrange("p (h s) k -> p h s k", s=2)
                for half, (op, arg, dst) in enumerate(((ALU.logical_shift_right, 4, e_hi), (ALU.bitwise_and, TOPK - 1, e_lo))):
                    step(v.tensor_scalar(half_i, flat, arg, None, op))
                    step(v.tensor_copy(half_f, half_i))
                    step(v.tensor_tensor(wide[1], spread(per_head(half_f), P, PH, TOPK, TOPK),
                                         iota16[:, 0:TOPK].unsqueeze(1).unsqueeze(1).to_broadcast([P, PH, TOPK, TOPK]), ALU.is_equal))
                    step(v.tensor_tensor(wide[1], wide[1], idx_pair[:, :, half].unsqueeze(2).to_broadcast([P, PH, TOPK, TOPK]), ALU.mult))
                    step(v.tensor_reduce(per_head(dst), wide[1], AX, ALU.add))
                step(v.scalar_tensor_tensor(out=e_hi, in0=e_hi, scalar=float(NK), in1=e_lo, op0=ALU.mult, op1=ALU.add))
                routed.step(ve, v.tensor_copy(expert[tt], e_hi))
                ve.wait_ge(softs.sem, tt + 1)
                z = slot8[:, 16:16 + PH]
                step(v.tensor_reduce(z, per_head(gate[tt]), AX, ALU.add))
                step(v.reciprocal(z, z))
                step(v.tensor_tensor(per_head(gate[tt]), per_head(gate[tt]), spread(z, P, PH, TOPK), ALU.mult))
                if tt == 0:
                    v.tensor_copy(slot8[:, 32:33], slot8[:, 16:17]).then_inc(rows_free, GB)
            base = dve.sent
            for tt in range(QT):
                with v.Fori(0, SLOTS // GB) as i:
                    for j in range(GB):
                        ve.wait_ge(rows_ld[j], (i + tt * (SLOTS // GB)) * 16 + 16)
                        if j >= 2:
                            ve.wait_ge(rows_free, (i + tt * (SLOTS // GB)) * GB + (GB + j - 1))
                        v.tensor_tensor_reduce(out=prod[:, j % 2], in0=rows[:, j], in1=hn[:, tt], scale=1.0, scalar=0.0, op0=ALU.mult,
                                               op1=ALU.add, accum_out=slot8[:, j:j + 1]).then_inc(rows_free, 1)
                    ve.wait_ge(rows_free, (i + tt * (SLOTS // GB)) * GB + 2 * GB)
                    v.tensor_copy(dots[tt][:, bass.ds(i * GB, GB)], slot8[:, 0:GB]).then_inc(dve.sem, 1)
                    ve.wait_ge(dve.sem, i + (base + tt * (SLOTS // GB) + 1))
                dve.sent += SLOTS // GB
                dots_ready.mark(v.tensor_copy(slot8[:, 32:33], slot8[:, 16:17]))
            base = dve.sent
            for tt in range(QT):
                ve.wait_ge(acts_ready.sem, tt + 1)
                step(v.tensor_tensor(gate[tt], gate[tt], dots[tt], ALU.mult))
                base = dve.sent
                at = (QT + tt) * (SLOTS // GB)
                with v.Fori(0, SLOTS // GB) as i:
                    ve.wait_ge(rows_free, (i + at) * GB + GB)
                    v.tensor_copy(slot8[:, 0:GB], gate[tt][:, bass.ds(i * GB, GB)]).then_inc(dve.sem, 1)
                    ve.wait_ge(dve.sem, i + (base + 1))
                    for j in range(GB):
                        ve.wait_ge(rows_ld[j], (i + at) * 16 + 16)
                        ve.wait_ge(rows_free, (i + at) * GB + (GB + j))
                        v.scalar_tensor_tensor(out=hx[:, tt], in0=rows[:, j], scalar=slot8[:, j:j + 1], in1=hx[:, tt],
                                               op0=ALU.mult, op1=ALU.add).then_inc(rows_free, 1)
                dve.sent += SLOTS // GB
            ve.wait_ge(rows_free, GB + 2 * QT * SLOTS)

            for s, name in enumerate(("norm1_g_2", "norm2_g_2", "norm3_g_2")):
                if s == 0:
                    ve.wait_ge(a_free.sem, len(a_jobs))
                g = GAIN[name]
                mod_ready.step(ve, v.scalar_tensor_tensor(out=mod[:, s, 1], in0=mod[:, s, 1], scalar=1.0, in1=gains[:, g:g + KD], op0=ALU.add, op1=ALU.mult))

            def norm_rows(s):
                for tt in range(QT):
                    ins = v.tensor_tensor_reduce(out=part, in0=hx[:, tt], in1=hx[:, tt], scale=1.0, scalar=0.0, op0=ALU.mult, op1=ALU.add,
                                                 accum_out=stats[:, 2 * s + tt:2 * s + tt + 1])
                    (step if tt == 0 else lambda x: b_sums.step(ve, x))(ins)
                ve.wait_ge(b_roots.sem, s + 1)
                b = rstd[:, 2 * s:2 * s + 2]
                step(v.reciprocal(b, b))
                if s == 3:
                    ve.wait_ge(ld_final, 16)
                    for tt in range(QT):
                        out_ready.mark(v.scalar_tensor_tensor(out=nrm[:, tt], in0=hx[:, tt], scalar=b[:, tt:tt + 1], in1=g_final, op0=ALU.mult, op1=ALU.mult))
                    return
                for tt in range(QT):
                    n_ready.mark(v.tensor_scalar(nrm[:, tt], hx[:, tt], b[:, tt:tt + 1], None, ALU.mult))
                for j in (0, 2):
                    ve.wait_ge(flipped.sem, 4 * s + j + 1)
                    for k in (2 * j, 2 * j + 1):
                        u_even.mark(v.tensor_scalar(uT[:, k], psum[j][:, (k % 2) * SEQ:(k % 2 + 1) * SEQ], mod[:, s, 1, k:k + 1],
                                                    mod[:, s, 0, k:k + 1], ALU.mult, ALU.add))

            def add_gated(bank, s, tt, cols):
                w = cols.stop - cols.start
                step(v.tensor_tensor(part[:, 0:w], bank, gates[:, s, cols], ALU.mult))
                return v.tensor_tensor(hx[:, tt, cols], hx[:, tt, cols], part[:, 0:w], ALU.add)

            def ffn_rows(f):
                def tile(j, c):
                    ve.wait_ge(silu_ready.sem, j + (f * FT + 1))
                    if f or not isinstance(j, int) or j >= 4:
                        ve.wait_ge(down_done.sem, j + (f * FT - 3))
                    v.tensor_tensor(hT[:, c], silu[:, c % 2], psum[c][:, SEQ:], ALU.mult).then_inc(h_ready.sem, 1)
                each_tile(v, tile)
                ve.wait_ge(down_done.sem, (f + 1) * FT)
                for tt in range(QT):
                    for n in range(2):
                        step(add_gated(psum[4 + 2 * tt + n][:, :], 2 * f, tt, slice(n * 512, (n + 1) * 512)))
                ffn_out.mark(v.tensor_copy(small[:, 0:1], small[:, 1:2]))

            norm_rows(0)
            ffn_rows(0)
            norm_rows(1)

            def scores_out(r):
                for h in range(4):
                    ve.wait_ge(z_full.sem, z_at["z", r, h] + 1)
                    bank = psum[z_at["z", r, h] % 4]
                    v.tensor_scalar(zlog[:, h], bank[:, 0:ZW], SD ** -0.5, 0.0, ALU.mult, ALU.min)
                    z_free.mark(v.tensor_scalar(zsp[:, h], bank[:, 0:ZW], SD ** -0.5, 0.0, ALU.mult, ALU.max))
                ve.wait_ge(z_free.sem, z_free.sent)
                min_ready.mark(v.tensor_tensor(zx, zlog, zsp, ALU.subtract))

            def seen_only(x):
                for c in (0, SEQ):
                    last = v.tensor_tensor(x[:, :, c:c + P], x[:, :, c:c + P], seen.unsqueeze(1).to_broadcast([P, 4, P]), ALU.mult)
                return last

            def softplus(r):
                ve.wait_ge(e_ready.sem, r + 1)
                v.tensor_tensor(zlog, zlog, zx, ALU.subtract)
                step(v.tensor_tensor(zsp, zsp, zx, ALU.add))
                sp_ready.mark(seen_only(zsp))

            def logs(r):
                for h in range(4):
                    ve.wait_ge(z_full.sem, z_at["rem", r, h] + 1)
                    bank = psum[z_at["rem", r, h] % 4]
                    z_free.mark(v.tensor_tensor(zlog[:, h], zlog[:, h], bank[:, 0:ZW], ALU.subtract))
                ve.wait_ge(z_free.sem, z_free.sent)
                log_ready.mark(v.tensor_copy(small[:, 0:1], small[:, 1:2]))
                ve.wait_ge(prob_ready.sem, r + 1)
                masked.mark(seen_only(zx))

            def heads_out(r):
                ve.wait_ge(z_full.sem, z_at["o", r] + 1)
                z_free.mark(v.tensor_copy(oT[:, 2 * r:2 * r + 2], psum[z_at["o", r] % 4][:, :].rearrange("p (a n) -> p a n", a=2)))

            last = v.memset(vT[:, :, 0:2], 0.0)
            step(last)
            scores_out(0)
            softplus(0)
            logs(0)
            heads_out(0)
            scores_out(1)
            softplus(1)
            ve.wait_ge(x_act.sem, 12)
            step(v.tensor_tensor(vT[:, :, 2:], ccT, cxT, ALU.mult))
            for k in range(4):
                tap = [gains[:, conv_row + 4 * a + k:conv_row + 4 * a + k + 1] for a in range(3)]
                step(v.tensor_scalar(convT[:, k], vT[:, k, 0:SEQ], tap[0], None, ALU.mult))
                for a in (1, 2):
                    step(v.scalar_tensor_tensor(out=convT[:, k], in0=vT[:, k, a:a + SEQ], scalar=tap[a], in1=convT[:, k], op0=ALU.mult, op1=ALU.add))
            conv_ready.mark(v.tensor_tensor(convT, convT, cbT, ALU.mult))
            logs(1)
            heads_out(1)
            ve.wait_ge(x_act.sem, 20)
            for name in ("ya", "yb"):
                for n in range(4):
                    ve.wait_ge(x_full.sem, x_at[name, n] + 1)
                    two = psum[4 + x_at[name, n] % 4][:, :].rearrange("p (a n) -> p a n", a=2)
                    gate_ = (sgaT if name == "ya" else sgbT)[:, 2 * n:2 * n + 2]
                    x_dve.step(ve, v.tensor_tensor(gate_, gate_, two, ALU.mult))
                    if name == "yb":
                        merged_ready.mark(v.tensor_tensor(sgaT[:, 2 * n:2 * n + 2], sgaT[:, 2 * n:2 * n + 2], gate_, ALU.add))
            for n in range(4):
                ve.wait_ge(x_full.sem, x_at["wo", n] + 1)
                bank = psum[4 + x_at["wo", n] % 4]
                for tt in range(QT):
                    ins = add_gated(bank[:, tt * 256:(tt + 1) * 256], 1, tt, slice(n * 256, (n + 1) * 256))
                    (step if tt == 0 else lambda x: x_dve.step(ve, x))(ins)
            norm_rows(2)
            ffn_rows(1)
            norm_rows(3)


_INS = ['x', 'meta_tokens', 'rel_bias', 'attn_norm', 'w_in', 'mla_q_norm', 'mla_w_uq', 'mla_kv_norm', 'mla_w_ukv',
        'mla_qk_norm_q', 'mla_qk_norm_k', 'diff_q_norm', 'diff_k_norm', 'diff_lambda_q1', 'diff_lambda_k1',
        'diff_lambda_q2', 'diff_lambda_k2', 'diff_subln', 'w_out', 'ffn_norm', 'peer_w_query', 'peer_sub_keys',
        'peer_u', 'peer_v', 'c_2', 'w_ada_2', 'b_ada_2', 'norm1_g_2', 'ffn1_w_gu_2', 'ffn1_w_down_2', 'norm2_g_2',
        'w_mix_in_2', 'b_merge_2', 'conv_w_2', 'w_conv_out_2', 'w_attn_out_2', 'w_out_2', 'norm3_g_2',
        'ffn2_w_gu_2', 'ffn2_w_down_2', 'final_g_2']


def kernel(**inputs):
    import numpy as _np
    import concourse.bacc as _bacc
    from concourse import mybir as _mybir
    from concourse.bass_utils import run_bass_kernel_spmd as _run

    nc = _bacc.Bacc("TRN2", target_bir_lowering=False, num_devices=1)
    arrays, tensors = {}, {}
    for name in _INS:
        a = _np.ascontiguousarray(inputs[name])
        arrays[f"in_{name}_dram"] = a
        tensors[name] = nc.dram_tensor(f"in_{name}_dram", a.shape, _mybir.dt.from_np(a.dtype), kind="ExternalInput").ap()
    out = nc.dram_tensor("out_0_dram", (1, SEQ, D), _mybir.dt.float32, kind="ExternalOutput").ap()
    program(nc, tensors, out)
    r = _run(nc, [arrays], core_ids=[0])
    return r.results[0]["out_0_dram"]
```

```python
import math
from contextlib import ExitStack

import numpy as np

import concourse.bass as bass
from concourse import mybir

F32 = mybir.dt.float32
F32R = mybir.dt.float32r
U32 = mybir.dt.uint32
ACT = mybir.ActivationFunctionType
ALU = mybir.AluOpType
AX = mybir.AxisListType.X

P = 128
D = 1024
KD = D // P
SEQ, META = 256, 16
KEYS = META + SEQ
ROWS = (P, P, META)
COL0 = (META, META + P, 0)
QT = 2
EPS = 1e-6
NEG = -1e30
MH, MQR, MKVR, NOPE, ROPE, MV = 8, 256, 256, 64, 32, 64
QK = NOPE + ROPE
HALF = ROPE // 2
DH, DD = 4, 64
DV = 2 * DD
LAMBDA_INIT = 0.8 - 0.6 * math.exp(0.0)
BUCKETS, MAX_DIST = 32, 128
C_C, C_ROPE = 0, MQR + MKVR
C_DQ = C_ROPE + ROPE
C_DK = C_DQ + DH * 2 * DD
C_DV = C_DK + DH * 2 * DD
IN_W = C_DV + DH * DV
PH, NK, TOPK, PQ = 8, 128, 16, 256
SLOTS = PH * TOPK
FF = 2816
FT = FF // P
SH, SD = 8, 64
CW = 512
ADA_W = 256


class Signal:

    def __init__(self, sem):
        self.sem, self.sent = sem, 0

    def mark(self, ins):
        self.sent += 1
        ins.then_inc(self.sem, 1)

    def step(self, eng, ins):
        self.mark(ins)
        eng.wait_ge(self.sem, self.sent)


def bucket_one_hot():
    dist = KEYS - 1 - np.arange(KEYS + SEQ)
    n = np.maximum(dist, 0)
    exact = BUCKETS // 2
    large = exact + (np.log(np.maximum(n, 1).astype(np.float32) / np.float32(exact))
                     / np.float32(math.log(MAX_DIST / exact)) * np.float32(BUCKETS - exact)).astype(np.int32)
    bucket = np.where(n < exact, n, np.minimum(large, BUCKETS - 1))
    return ((bucket[None] == np.arange(BUCKETS)[:, None]) & (dist >= 0)[None]).astype(np.float32)


def rope_table():
    inv = np.float32(10000.0) ** (-np.arange(HALF, dtype=np.float32) / np.float32(HALF))
    ang = np.arange(KEYS, dtype=np.float32)[:, None] * inv[None]
    return np.concatenate([np.cos(ang), np.sin(ang)], 1).astype(np.float32)


def spread(ap, *shape):
    while len(ap.shape) < len(shape):
        ap = ap.unsqueeze(len(ap.shape))
    return ap.to_broadcast(list(shape))


def program(nc, t, out):
    ctx = ExitStack()
    with ctx:
        def sb(name, cols, dt=F32, rows=P):
            return ctx.enter_context(nc.sbuf_tensor(name, [rows, cols], dt))

        def sem(name):
            return ctx.enter_context(nc.semaphore(name))

        def signal(name):
            return Signal(sem(name))

        RING, SLOT = 6, 2048
        hx = sb("hx", QT * D)[:].rearrange("p (t d) -> p t d", t=QT)
        ident = sb("ident", P)[:]
        ones = sb("ones", P)[:]
        eps = sb("eps", 1)[:]
        ring = sb("ring", RING * SLOT)
        ring_at = nc.sbuf_base - 4 * RING * SLOT
        arena = sb("arena", 34848)
        arena_at = nc.sbuf_base - 4 * 34848
        stats = sb("stats", 128)[:]
        rstd = sb("rstd", 128)[:]
        gain_rows = sb("gain_rows", P)[:]
        gains = sb("gains", P)[:]
        rope = sb("rope", 3 * ROPE)[:].rearrange("p (t c) -> p t c", t=3)
        lam_in = sb("lam_in", 4 * DD)[:].rearrange("p (v d) -> p v d", v=4)
        lam = sb("lam", 4)[:]
        rel = sb("rel", 4, rows=BUCKETS)[:]
        small = sb("small", 256)[:]

        def area(tensor, at, cols):
            assert at + cols <= tensor.shape[1]
            return tensor[:, at:at + cols]

        W0, W1, W2, WR = 0, 4096, 8192, 12288
        w_slot = [area(arena, o, 4096).rearrange("p (k n) -> p k n", k=KD) for o in (W0, W1, W2)]
        w_rope = area(arena, WR, KD * ROPE).rearrange("p (k n) -> p k n", k=KD)
        N0 = WR + KD * ROPE
        nT = area(arena, N0, KD * KEYS).rearrange("p (k n) -> p k n", k=KD)
        dqT = area(arena, N0, DH * SEQ).rearrange("p (h n) -> p h n", h=DH)
        dkT = area(arena, N0 + DH * SEQ, DH * KEYS).rearrange("p (h n) -> p h n", h=DH)
        R0 = N0 + KD * KEYS
        pr = area(arena, R0, 3 * IN_W).rearrange("p (t n) -> p t n", t=3)
        U0 = R0 + 3 * IN_W
        w_uq = area(arena, U0, 2 * MH * QK).rearrange("p (k n) -> p k n", k=2)
        w_ukv = area(arena, U0 + 2 * MH * QK, 2 * 1024).rearrange("p (k n) -> p k n", k=2)
        C0 = U0 + 2 * MH * QK + 2048
        hm = area(arena, C0, D)[0:META]
        cT = area(arena, C0, 4 * KEYS).rearrange("p (k n) -> p k n", k=4)
        B0 = C0 + 4 * KEYS
        bias = area(arena, B0, DH * QT * KEYS).rearrange("p (h t n) -> p h t n", h=DH, t=QT)
        mask = area(arena, B0 + DH * QT * KEYS, QT * KEYS).rearrange("p (t n) -> p t n", t=QT)
        G0 = B0 + (DH + 1) * QT * KEYS
        g_rope = area(arena, G0, 2 * ROPE).rearrange("p (w c) -> p w c", w=2)
        K0 = G0 + 2 * ROPE
        qT = area(arena, K0, MH * SEQ).rearrange("p (h n) -> p h n", h=MH)
        kT = area(arena, K0 + MH * SEQ, MH * KEYS).rearrange("p (h n) -> p h n", h=MH)
        q_row = area(arena, W1, 2 * MH * QK).rearrange("p (t n) -> p t n", t=2)
        k_row = area(arena, W1 + 2 * MH * QK, 3 * MH * QK).rearrange("p (t n) -> p t n", t=3)
        v_row = area(arena, W2, 3 * MH * MV).rearrange("p (t n) -> p t n", t=3)
        rot = area(arena, W2 + 3 * MH * MV, 3 * MH * ROPE).rearrange("p (s h c) -> p s h c", s=3, h=MH)
        wo_half = [w_slot[0], area(arena, U0, 4096).rearrange("p (k n) -> p k n", k=KD)]
        xn = area(ring, 0, 3 * D).rearrange("p (t d) -> p t d", t=3)
        fill = area(ring, 3072, KEYS + SEQ)[0:4]
        onehot = area(ring, 3616, KEYS + SEQ)[0:BUCKETS]
        tmp = area(ring, 4352, 1024)
        NM = 4
        sc = [area(ring, i * NM * KEYS, NM * KEYS).rearrange("p (m n) -> p m n", m=NM) for i in range(2)]
        pb = [area(ring, (2 + i) * NM * KEYS, NM * KEYS).rearrange("p (m n) -> p m n", m=NM) for i in range(2)]
        Y0 = 4 * NM * KEYS
        pT = area(ring, Y0, 4 * 3 * P).rearrange("p (s b n) -> p s b n", s=4, b=3)
        y = area(ring, Y0 + 1536, QT * D).rearrange("p (t d) -> p t d", t=QT)
        yT = area(ring, Y0 + 1536 + QT * D, KD * SEQ).rearrange("p (k n) -> p k n", k=KD)

        wq_chunk = [area(arena, o, 4096).rearrange("p (k n) -> p k n", k=KD) for o in (W1, W2, N0, N0 + 4096)]
        hn = area(arena, W0, QT * D).rearrange("p (t d) -> p t d", t=QT)
        hnT = area(arena, B0, KD * SEQ).rearrange("p (k n) -> p k n", k=KD)
        keysT = area(arena, B0 + 2048, 2 * PH * NK).rearrange("p (s n) -> p s n", s=2 * PH)
        keys = area(arena, B0 + 4096, 2 * PH * P).rearrange("p (s d) -> p s d", s=2 * PH)
        g_ffn = area(arena, B0 + 6144, D)
        pqT = area(arena, U0, 2 * PH * SEQ).rearrange("p (s n) -> p s n", s=2 * PH)
        ps = [area(arena, o, 2 * PH * NK).rearrange("p (s n) -> p s n", s=2 * PH) for o in (W0 + 2048, B0 + 4096)]
        wide = [area(ring, 8192 + 2048 * i, 2048).rearrange("p (h a b) -> p h a b", h=PH, a=TOPK) for i in range(2)]

        def table(n, dt=F32, cols=SLOTS):
            at = B0 + 7168 + P * n if n < 15 else C0 + 512 + P * (n - 15) if n < 19 else WR + P * (n - 19)
            tab = area(arena, at, cols)
            return tab if dt == F32 else tab.bitcast(dt)

        top_v, top_i, top_f = (table(2 * i, dt, 256).rearrange("p (s k) -> p s k", k=TOPK) for i, dt in enumerate((F32, U32, F32)))
        best, flat, half_i, half_f = table(6), table(7, U32), table(8, U32), table(9)
        e_hi, e_lo, iota16 = table(10), table(11), table(12)
        gate = [table(13), table(14)]
        expert = [table(15, U32), table(16, U32)]
        dots = [table(17), table(18)]
        slot8 = table(19)
        expert8 = table(20, U32)
        GB = 8
        rows = area(arena, N0, GB * D).rearrange("p (b d) -> p b d", b=GB)
        prod = area(arena, W2, 2 * D).rearrange("p (b d) -> p b d", b=2)
        gate1 = sb("gate1", D)[:]
        gates = [gate1, area(arena, B0, D), area(arena, B0 + D, D)]
        c_act = sb("c_act", KD)[:]
        mod = sb("mod", 3 * 2 * KD)[:].rearrange("p (s m k) -> p s m k", s=3, m=2)
        late = area(arena, B0 + 3 * D, 4 * D + D)
        ada_sum = [[area(arena, B0 + 7168, D), area(arena, B0 + 7168 + D, D), gate1]] + 2 * [[late[:, m * D:(m + 1) * D] for m in range(3)]]
        CHUNK = KD // 2 * ADA_W
        ada_chunk = [[(area(ring, Y0 + 1536 + QT * D + KD * SEQ + i * CHUNK, CHUNK) if s == 0 else late[:, 3 * D + i * CHUNK:3 * D + (i + 1) * CHUNK])
                      .rearrange("p (k n) -> p k n", k=KD // 2) for i in range(2)] for s in range(3)]

        uT = area(arena, 0, KD * SEQ).rearrange("p (k n) -> p k n", k=KD)
        nrm = area(arena, 2048, QT * D).rearrange("p (t d) -> p t d", t=QT)
        silu = area(arena, 4096, 2 * SEQ).rearrange("p (b n) -> p b n", b=2)
        hT = area(arena, 4608, 4 * SEQ).rearrange("p (b n) -> p b n", b=4)
        part = area(arena, 5632, D)
        g_final = area(arena, 6656, D)
        at = [7680]

        def mix(cols, *dims):
            piece = area(arena, at[0], cols)
            at[0] += cols
            return piece.rearrange("p (a n) -> p a n", a=dims[0]) if dims else piece

        PAD = SEQ + 2
        cbT, ccT, cxT, convT, vT = mix(4 * SEQ, 4), mix(4 * SEQ, 4), mix(4 * SEQ, 4), mix(4 * SEQ, 4), mix(4 * PAD, 4)
        sqT, skT, sv_row = mix(4 * SEQ, 4), mix(4 * SEQ, 4), mix(QT * CW, QT)
        sgaT, sgbT, oT = mix(KD * SEQ, KD), mix(KD * SEQ, KD), mix(4 * SEQ, 4)
        ZW = SEQ + P
        zx, zlog, zsp = (mix(4 * ZW, 4) for _ in range(3))
        assert at[0] <= B0

        def rounded(name, base, col, cols):
            return nc.alloc_sbuf_tensor_at(name, [P, cols], F32R, offset=base + 4 * col)[:]

        HI_AT = (7680, 9728, 11776, 13824, 17928, 19976)
        w_hi = [rounded(f"w_hi{i}", arena_at, HI_AT[i], SLOT) for i in range(RING)]
        w_lo = [rounded(f"w_lo{i}", ring_at, SLOT * i, SLOT) for i in range(RING)]
        mix_hi = {name: rounded(f"mix_hi_{name}", arena_at, col, SLOT) for name, col in
                  (("sga", 15880), ("sgb", 17928), ("conv", 8704), ("qk", 12808))}
        u_lo = rounded("u_lo", arena_at, 0, KD * SEQ).rearrange("p (k n) -> p k n", k=KD)
        u_hi = rounded("u_hi", arena_at, 2048, KD * SEQ).rearrange("p (k n) -> p k n", k=KD)
        h_lo = rounded("h_lo", arena_at, 4608, 4 * SEQ).rearrange("p (b n) -> p b n", b=4)
        h_hi = rounded("h_hi", arena_at, 5632, 4 * SEQ).rearrange("p (b n) -> p b n", b=4)
        later = sb("later", P)[:]
        seen = sb("seen", P)[:]
        w_slots = [ring[:, SLOT * i:SLOT * (i + 1)] for i in range(RING)]

        psum = [ctx.enter_context(nc.psum_tensor(f"bank{i}", [P, 512], F32)) for i in range(8)]
        LB = 4
        lane_d, lane_a = psum[:LB], psum[LB:]
        d_full, d_free = signal("d_full"), signal("d_free")
        a_full, a_free = signal("a_full"), signal("a_free")

        fill_dram = nc.dram_tensor("bias_by_distance", [4, KEYS + SEQ], F32, kind="Internal")
        SKEW = P * (KEYS + SEQ + 1)
        skew_dram = nc.dram_tensor("bias_by_distance_skewed", [DH, SKEW], F32, kind="Internal")
        onehot_dram = nc.inline_tensor(bucket_one_hot(), "bucket_one_hot")
        rope_dram = nc.inline_tensor(rope_table(), "rope_table")

        GAIN, n_gain = {}, 0
        gain_src = [("attn_norm", KD), ("mla_q_norm", 2), ("mla_kv_norm", 2), ("diff_subln", 1), ("norm1_g_2", KD),
                    ("norm2_g_2", KD), ("norm3_g_2", KD), ("b_merge_2", 2 * KD), ("c_2", KD)]
        for name, n in gain_src:
            GAIN[name], n_gain = n_gain, n_gain + n
        conv_row = n_gain
        n_gain += 12
        for name in ("diff_q_norm", "diff_k_norm", "mla_qk_norm_q", "mla_qk_norm_k"):
            GAIN[name], n_gain = n_gain, n_gain + 1
        assert n_gain <= P

        ld_x = [sem(f"ld_x{i}") for i in range(3)]
        ld_gain, ld_small, ld_rope_w = sem("ld_gain"), sem("ld_small"), sem("ld_rope_w")
        ld_c, ld_dk, ld_dq, ld_dv, ld_up, ld_wo = (sem(n) for n in ("ld_c", "ld_dk", "ld_dq", "ld_dv", "ld_up", "ld_wo"))
        ld_hot, st_fill, st_skew, ld_bias = (sem(n) for n in ("ld_hot", "st_fill", "st_skew", "ld_bias"))
        consts, bias_ready = signal("consts"), signal("bias_ready")
        sums, roots = signal("sums"), signal("roots")
        dve, act = signal("dve"), signal("act")
        gains_ready, fill_ready = signal("gains_ready"), signal("fill_ready")
        xn_ready, c_row_ready = signal("xn_ready"), signal("c_row_ready")
        m_ready, p_ready = signal("m_ready"), signal("p_ready")
        a_ready, y_ready = signal("a_ready"), signal("y_ready")
        dk_ready, dq_ready = signal("dk_ready"), signal("dq_ready")
        head_ready = signal("head_ready")
        lam_sums, lam_exps = signal("lam_sums"), signal("lam_exps")
        stored = sem("stored")
        ld_wq = [sem(f"ld_wq{i}") for i in range(4)]
        ld_keys, ld_gffn = sem("ld_keys"), sem("ld_gffn")
        hn_ready, c_ready = signal("hn_ready"), signal("c_ready")
        ld_ada, ld_ada_bias = [sem(f"ld_ada{i}") for i in range(2)], sem("ld_ada_bias")
        gps, gps_go = signal("gps"), sem("gps_go")
        ada_ready, ada_full, ada_free, mod_ready = (signal(n) for n in ("ada_ready", "ada_full", "ada_free", "mod_ready"))
        hi_ready, lo_ready = signal("hi_ready"), signal("lo_ready")
        mix_hi_ready, mix_lo_ready, conv_in = signal("mix_hi_ready"), signal("mix_lo_ready"), signal("conv_in")
        u_hi_ready, u_split, h_order = signal("u_hi_ready"), signal("u_split"), signal("h_order")
        bests, softs, routed = signal("bests"), signal("softs"), signal("routed")
        rows_ld = [sem(f"rows_ld{i}") for i in range(GB)]
        rows_free = sem("rows_free")
        gather_go = sem("gather_go")
        expert8_ready = signal("expert8_ready")
        n_ready = signal("n_ready")
        u_even, u_odd = signal("u_even"), signal("u_odd")
        flipped = signal("flipped")
        b_sums, b_roots = signal("b_sums"), signal("b_roots")
        w_ld = [sem(f"w_ld{i}") for i in range(RING)]
        gu_full, silu_ready, h_ready, down_done = (signal(n) for n in ("gu_full", "silu_ready", "h_ready", "down_done"))
        ffn_out = signal("ffn_out")
        x_full, x_act, x_dve = signal("x_full"), signal("x_act"), signal("x_dve")
        z_full, z_free, e_ready, sp_ready, prob_ready = (signal(n) for n in ("z_full", "z_free", "e_ready", "sp_ready", "prob_ready"))
        masked = signal("masked")
        log_ready, min_ready, conv_ready, merged_ready = (signal(n) for n in ("log_ready", "min_ready", "conv_ready", "merged_ready"))
        ld_final, out_ready = sem("ld_final"), signal("out_ready")
        dots_ready, acts_ready = signal("dots_ready"), signal("acts_ready")


        STEPS = [(tt, g) for tt in range(QT) for g in range(4)]
        def maps(g):
            return range(4) if g < 2 else range(0, 4, 2)

        d_jobs = ["gains"] + [("nT", tt, b) for tt in range(3) for b in range(2)] + [("fill", 0), ("fill", 1)] + [("cT", tt) for tt in range(3)]
        for i in range(len(STEPS) + 1):
            if i < len(STEPS):
                d_jobs += [("s", i, m) for m in range(4)]
            if i:
                d_jobs.append(("o", i - 1))
        d_jobs += [("yT", tt, b) for tt in range(QT) for b in range(2)]
        d_jobs += [("wo", n, tt) for n in range(2) for tt in range(QT)]
        a_jobs = [("c", tt) for tt in range(3)] + [("rope", tt) for tt in range(3)] + [("dk", tt) for tt in range(3)]
        a_jobs += [("dq", tt) for tt in range(QT)]
        for tt in range(3):
            a_jobs += [("q", tt, n) for n in range(2) if tt < QT] + [("kv", tt, n) for n in range(2)]
        a_jobs += [("dv", tt) for tt in range(3)] + [("dkT", tt) for tt in range(3)] + [("dqT", tt) for tt in range(QT)]
        for tt in range(3):
            a_jobs += [("qT", tt, n) for n in range(2) if tt < QT] + [("kT", tt, n) for n in range(2)]
        for i, (tt, g) in enumerate(STEPS):
            a_jobs += [("pT", i, m) for m in maps(g)]
        d_jobs += [("hnT", tt, b) for tt in range(QT) for b in range(2)]
        ADA_JOBS = ("columns", 0, 1)
        a_jobs += [("ada", job) for job in ADA_JOBS]
        a_jobs += [("keysT", n) for n in range(4)]
        QUARTERS = ((0, 1, 2, 3), (3, 2, 1, 0))
        q_jobs = []
        for tt in range(QT):
            for i in range(5):
                q_jobs += [("pq", tt, n) for n in QUARTERS[tt][i:i + 1]] + [("ps", tt, n) for n in QUARTERS[tt][i - 1:i] if i]
        a_jobs += q_jobs
        d_at = {job: n for n, job in enumerate(d_jobs)}
        a_at = {job: n for n, job in enumerate(a_jobs)}

        def bank_of(job, at, lane):
            return lane[at[job] % LB]

        def open_bank(pe, job, at, lane, free):
            if at[job] >= LB:
                pe.wait_ge(free.sem, at[job] - LB + 1)
            return bank_of(job, at, lane)

        def full_bank(eng, job, at, lane, full):
            eng.wait_ge(full.sem, at[job] + 1)
            return bank_of(job, at, lane)

        norms, col = [], 0
        for names, n, width in ([[("x", tt) for tt in range(3)], 1, D], [[("c", tt) for tt in range(3)], 2, 256],
                                [[("dk", tt) for tt in range(3)] + [("dq", tt) for tt in range(QT)], 8, DD],
                                [[("q", 0), ("k", 0), ("q", 1), ("k", 1), ("k", 2)], MH, QK],
                                [["subln"], QT * DH, DV], [["h1"], QT, D]):
            for name in names:
                norms.append((name, col, n, width))
                col += n
        norm_at = {name: (k, slice(c, c + n), width) for k, (name, c, n, width) in enumerate(norms)}
        ROWS_OF = {("x", 2): META, ("c", 2): META, ("dk", 2): META, ("k", 2): META}

        BLOCKS = FT // 2
        MIX = [("in", n) for n in range(20)] + [("conv", n) for n in range(2)] + [("attn", n) for n in range(2)] + [("out", n) for n in range(4)]
        FIRST = (0, 3 * BLOCKS + len(MIX))
        MIX0 = 3 * BLOCKS
        MIX_COLS = [256 * n for n in (*range(6, 12), *range(0, 6), *range(12, 20))]
        x_jobs = [("in", n) for n in range(20)] + [("ya", n) for n in range(4)] + [("yb", n) for n in range(4)] + [("wo", n) for n in range(4)]
        x_at = {job: n for n, job in enumerate(x_jobs)}
        z_jobs = []
        for r in range(2):
            z_jobs += [("z", r, h) for h in range(4)] + [("rem", r, h) for h in range(4)] + [("o", r)]
        z_at = {job: n for n, job in enumerate(z_jobs)}

        def ffn_slot(f, parity, c):
            return (FIRST[f] + 3 * parity + c) % RING

        def landed(f, i, parity, c):
            return i * 16 + 16 * ((FIRST[f] + 3 * parity + c) // RING + 1)

        def split_count(f, b, c):
            base = f * 3 * BLOCKS
            if isinstance(b, int) and (b == 0 and c < 2 or b == BLOCKS - 1 and c == 2):
                return base + (c + 1 if c < 2 else 3 * BLOCKS)
            return b * 3 + (base + (0, 1, 5)[c])

        IN = 20

        def mix_slot(n):
            return (MIX0 + n) % RING

        def mix_hi_of(n):
            if n < 14:
                return mix_hi[("sga", "sgb")[n % 2]]
            return mix_hi[{14: "conv", 15: "sgb"}.get(n, ("conv", "qk")[n % 2])]

        def each_block(eng, tile, split):
            def both(i, parity, last=False):
                b = i * 2 + parity
                tile(b * 2, 2 * parity)
                if not last:
                    for c in range(2):
                        split(i + 1 if parity else i, 1 - parity, c)
                tile(b * 2 + 1, 2 * parity + 1)
                split(i, parity, 2)
            for parity in range(2):
                both(0, parity)
            with eng.Fori(1, 5) as i:
                for parity in range(2):
                    both(i, parity)
            both(5, 0, last=True)

        block = ctx.enter_context(nc.Block())

        @block.sync
        def _(sp):
            for i, (dst, src) in enumerate(((hx[:, 0], t["x"][0, 0:P]), (hx[:, 1], t["x"][0, P:SEQ]), (hm, t["meta_tokens"]))):
                sp.dma_start(dst, src).then_inc(ld_x[i], 16)
            sp.wait_ge(consts.sem, 1)
            for name, n in gain_src:
                src = t[name].rearrange("a b -> (a b)") if len(t[name].shape) == 2 else t[name].rearrange("a b c -> (a b c)")
                sp.dma_start(gain_rows[GAIN[name]:GAIN[name] + n], src.rearrange("(k p) -> k p", p=P)).then_inc(ld_gain, 16)
            sp.dma_start(gain_rows[conv_row:conv_row + 12], t["conv_w_2"][0].rearrange("a (k p) -> (a k) p", p=P)).then_inc(ld_gain, 16)
            for name in ("diff_q_norm", "diff_k_norm"):
                for c in range(2):
                    sp.dma_start(gain_rows[GAIN[name]:GAIN[name] + 1, c * DD:(c + 1) * DD], t[name]).then_inc(ld_gain, 16)
            for name in ("mla_qk_norm_q", "mla_qk_norm_k"):
                sp.dma_start(gain_rows[GAIN[name]:GAIN[name] + 1, 0:NOPE], t[name][:, 0:NOPE]).then_inc(ld_gain, 16)
            sp.dma_start(onehot, onehot_dram.ap()).then_inc(ld_hot, 16)
            sp.dma_start(rel, t["rel_bias"]).then_inc(ld_hot, 16)
            for i in range(3):
                sp.dma_start(rope[0:ROWS[i], i], rope_dram.ap()[COL0[i]:COL0[i] + ROWS[i]]).then_inc(ld_small, 16)
            for i, name in enumerate(("diff_lambda_q1", "diff_lambda_k1", "diff_lambda_q2", "diff_lambda_k2")):
                sp.dma_start(lam_in[:, i], t[name].to_broadcast([P, DD])).then_inc(ld_small, 16)
            for i, name in enumerate(("mla_qk_norm_q", "mla_qk_norm_k")):
                sp.dma_start(g_rope[:, i], t[name][:, NOPE:QK].to_broadcast([P, ROPE])).then_inc(ld_small, 16)
            w_in = t["w_in"][0].rearrange("(k p) n -> p k n", p=P)
            sp.dma_start(w_rope, w_in[:, :, C_ROPE:C_ROPE + ROPE]).then_inc(ld_rope_w, 16)
            sp.dma_start(w_slot[1], w_in[:, :, C_DK:C_DK + 512]).then_inc(ld_dk, 16)
            sp.dma_start(w_slot[2], w_in[:, :, C_DQ:C_DQ + 512]).then_inc(ld_dq, 16)
            sp.dma_start(w_uq, t["mla_w_uq"][0].rearrange("(k p) n -> p k n", p=P)).then_inc(ld_up, 16)
            sp.dma_start(w_ukv, t["mla_w_ukv"][0].rearrange("(k p) n -> p k n", p=P)).then_inc(ld_up, 16)
            sp.wait_ge(a_full.sem, a_at["c", 2] + 1)
            sp.dma_start(w_slot[0], w_in[:, :, C_DV:C_DV + 512]).then_inc(ld_dv, 16)
            sp.wait_ge(fill_ready.sem, 1)
            sp.dma_start(fill_dram.ap(), fill).then_inc(st_fill, 16)
            sp.wait_ge(st_fill, 16)
            sp.dma_start(bass.AP(skew_dram, 0, [[KEYS + SEQ + 1, P], [SKEW, DH], [1, KEYS + SEQ]]),
                         bass.AP(fill_dram, 0, [[0, P], [KEYS + SEQ, DH], [1, KEYS + SEQ]])).then_inc(st_skew, 16)
            sp.wait_ge(st_skew, 16)
            for tt in range(QT):
                src = bass.AP(skew_dram, SEQ - 1 - P * tt, [[KEYS + SEQ, P], [SKEW, DH], [1, KEYS]])
                sp.dma_start(bias[:, :, tt], src).then_inc(ld_bias, 16)
            w_out = t["w_out"][0].rearrange("(k p) n -> p k n", p=P)
            sp.wait_ge(a_full.sem, a_at["dv", 2] + 1)
            for n in range(2):
                sp.dma_start(wo_half[n], w_out[:, :, n * 512:(n + 1) * 512]).then_inc(ld_wo, 16)
            sp.wait_ge(y_ready.sem, 1)
            w_query = t["peer_w_query"][0].rearrange("(k p) n -> p k n", p=P)
            sp.dma_start(g_ffn, t["ffn_norm"].to_broadcast([P, D])).then_inc(ld_gffn, 16)
            for n in range(4):
                sp.dma_start(wq_chunk[n], w_query[:, :, n * 512:(n + 1) * 512]).then_inc(ld_wq[n], 16)
                if n == 0:
                    sp.dma_start(keys, t["peer_sub_keys"][0].rearrange("h s n d -> n (h s) d")).then_inc(ld_keys, 16)
            def ffn_loads(f):
                w_gu = t[f"ffn{f + 1}_w_gu_2"][0].rearrange("(k p) n -> p k n", p=P)
                w_down = t[f"ffn{f + 1}_w_down_2"][0].rearrange("(j p) n -> p j n", p=P)

                def block_loads(b, parity, waits):
                    for c in range(3):
                        slot = (FIRST[f] + 3 * parity + c) % RING
                        waits(b, parity, c)
                        dst = w_slots[slot].rearrange("p (k n) -> p k n", k=KD if c < 2 else 2)
                        src = w_gu[:, :, bass.ds(b * 256 + c * FF, 256)] if c < 2 else w_down[:, bass.ds(b * 2, 2), :]
                        sp.dma_start(dst, src).then_inc(w_ld[slot], 16)

                def first(b, parity, c):
                    n = 3 * b + c
                    if f == 0 and n < 2:
                        sp.wait_ge(d_full.sem, d_at["yT", QT - 1, 1] + 1)
                    elif f == 0 and n < 4:
                        sp.wait_ge(hn_ready.sem, QT)
                    elif f == 0:
                        sp.wait_ge(routed.sem, QT)
                    else:
                        mix_slot_used(len(MIX) - RING + n)

                def steady(b, parity, c):
                    if c < 2:
                        sp.wait_ge(gu_full.sem, b * 2 + (f * FT - 2))
                    else:
                        sp.wait_ge(down_done.sem, b * 2 + (f * FT - 2))

                for b in range(2):
                    block_loads(b, b, first)
                with sp.Fori(1, 5) as i:
                    for c in range(2):
                        block_loads(i * 2 + c, c, steady)
                block_loads(10, 0, steady)

            def mix_slot_used(n):
                kind, m = MIX[n]
                job = {"in": ("in", m), "conv": ("ya", 2 * m + 1), "attn": ("yb", 2 * m + 1), "out": ("wo", m)}[kind]
                sp.wait_ge(x_full.sem, x_at[job] + 1)

            ffn_loads(0)
            w_mix = {"in": t["w_mix_in_2"], "conv": t["w_conv_out_2"], "attn": t["w_attn_out_2"], "out": t["w_out_2"]}
            for n, (kind, m) in enumerate(MIX):
                if n < RING:
                    k = 3 * BLOCKS - RING + n
                    done = (k // 3 + 1) * 2
                    sp.wait_ge((gu_full if k % 3 < 2 else down_done).sem, done)
                else:
                    mix_slot_used(n - RING)
                w = w_mix[kind][0].rearrange("(k p) n -> p k n", p=P)
                cols, width = (MIX_COLS[m], 256) if kind == "in" else (256 * m, 256) if kind == "out" else (512 * m, 512)
                slot = (MIX0 + n) % RING
                sp.dma_start(w_slots[slot].rearrange("p (k n) -> p k n", k=2048 // width), w[:, :, cols:cols + width]).then_inc(w_ld[slot], 16)
            ffn_loads(1)
            sp.dma_start(g_final, t["final_g_2"].unsqueeze(0).to_broadcast([P, D])).then_inc(ld_final, 16)
            for tt in range(QT):
                sp.wait_ge(out_ready.sem, tt + 1)
                sp.dma_start(out[0, tt * P:(tt + 1) * P], nrm[:, tt]).then_inc(stored, 16)
            sp.wait_ge(stored, 16 * QT)

        @block.gpsimd
        def _(pool):
            gp = nc.gpsimd
            consts.step(pool, gp.memset(gain_rows, 1.0))
            consts.step(pool, gp.memset(ident, 0.0))
            consts.step(pool, gp.affine_select(out=ident, in_=ident, compare_op=ALU.not_equal, fill=1.0, base=0,
                                               pattern=[[-1, P]], channel_multiplier=1))
            consts.step(pool, gp.memset(ones, 1.0))
            consts.step(pool, gp.memset(eps, EPS))
            consts.step(pool, gp.memset(later, 1.0))
            consts.step(pool, gp.affine_select(out=later, in_=later, compare_op=ALU.is_gt, fill=0.0, base=0,
                                               pattern=[[-1, P]], channel_multiplier=1))
            consts.step(pool, gp.memset(seen, 1.0))
            consts.step(pool, gp.affine_select(out=seen, in_=seen, compare_op=ALU.is_gt, fill=0.0, base=0,
                                               pattern=[[1, P]], channel_multiplier=-1))
            bias_ready.step(pool, gp.memset(mask, 0.0))
            for tt in range(QT):
                bias_ready.step(pool, gp.affine_select(out=mask[:, tt], in_=mask[:, tt], compare_op=ALU.is_ge, fill=NEG,
                                                       base=META + P * tt, pattern=[[-1, KEYS]], channel_multiplier=1))
            pool.wait_ge(ld_bias, 32)
            for tt in range(QT):
                bias_ready.step(pool, gp.affine_select(out=bias[:, :, tt], in_=bias[:, :, tt], compare_op=ALU.is_ge,
                                                       fill=NEG, base=META + P * tt, pattern=[[0, DH], [-1, KEYS]],
                                                       channel_multiplier=1))

            w_ada = t["w_ada_2"][0].rearrange("(k p) n -> p k n", p=P)
            ADA_OPS = 4
            CHUNKS = D // ADA_W

            def load_ada(s, m, i, half):
                ks = slice(half * KD // 2, (half + 1) * KD // 2)
                gp.dma_start(ada_chunk[s][half], w_ada[:, ks, bass.ds(i * ADA_W + (3 * s + m) * D, ADA_W)]).then_inc(ld_ada[half], 16)

            def sum_ada(s, m, i, half):
                pool.wait_ge(ld_ada[half], i * 16 + ((3 * s + m) * CHUNKS * 16 + 16))
                c = ada_chunk[s][half]
                dst = ada_sum[s][m][:, bass.ds(i * ADA_W, ADA_W)]
                ops = [(c, c, spread(c_act[:, half * KD // 2:(half + 1) * KD // 2], P, KD // 2, ADA_W), ALU.mult)]
                ops += [(c[:, 0:w], c[:, 0:w], c[:, w:2 * w], ALU.add) for w in (2, 1)]
                ops += [(dst, dst, c[:, 0], ALU.add)]
                for n, (o, x, y_, op) in enumerate(ops):
                    if n == ADA_OPS - 1:
                        pool.sem_inc(gps_go, 1)
                    gp.tensor_tensor(o, x, y_, op).then_inc(gps.sem, 1)
                    pool.wait_ge(gps.sem, i * (2 * ADA_OPS) + (gps.sent + half * ADA_OPS + n + 1))

            def modulation(s):
                for half in range(2):
                    load_ada(s, 0, 0, half)
                if s == 2:
                    pool.wait_ge(ada_full.sem, len(ADA_JOBS))
                for m in range(3):
                    gps.step(pool, gp.memset(ada_sum[s][m], 0.0))
                    gp.dma_start(ada_sum[s][m][0:1], t["b_ada_2"][:, (3 * s + m) * D:(3 * s + m + 1) * D]).then_inc(ld_ada_bias, 16)
                pool.wait_ge(ld_ada_bias, 16 * 3 * (s + 1))
                for m in range(3):
                    in_loop = CHUNKS if m < 2 else CHUNKS - 1
                    with gp.Fori(0, in_loop) as i:
                        for half in range(2):
                            sum_ada(s, m, i, half)
                            pool.sem_inc(gps_go, 1)
                            load_ada(s, m, i + 1, half)
                    if m == 2:
                        for half in range(2):
                            sum_ada(s, m, CHUNKS - 1, half)
                    gps.sent += 2 * CHUNKS * ADA_OPS
                ada_ready.mark(gp.tensor_copy(small[:, 255:256], ada_sum[s][2][:, 0:1]))

            def final_scale(s):
                if s == 0:
                    pool.wait_ge(a_free.sem, a_at["ada", "columns"] + 1)
                else:
                    pool.wait_ge(ada_free.sem, len(ADA_JOBS) * (s - 1) + 1)
                g = GAIN[f"norm{s + 1}_g_2"]
                gps.step(pool, gp.tensor_scalar(mod[:, s, 1], mod[:, s, 1], 1.0, None, ALU.add))
                mod_ready.mark(gp.tensor_tensor(mod[:, s, 1], mod[:, s, 1], gains[:, g:g + KD], ALU.mult))

            pool.wait_ge(c_ready.sem, 1)
            modulation(0)
            final_scale(0)

            pool.wait_ge(routed.sem, 1)
            for phase, (src, tt) in enumerate((("peer_u", 0), ("peer_u", 1), ("peer_v", 0), ("peer_v", 1))):
                if tt:
                    pool.wait_ge(routed.sem, 2)
                weights = t[src][0]
                with gp.Fori(0, SLOTS // (2 * GB)) as i:
                    for half in range(2):
                        first = (i * 2 + (phase * (SLOTS // GB) + half)) * GB
                        pool.wait_ge(rows_free, first + 1)
                        idx = expert8[:, half * GB:(half + 1) * GB]
                        gp.tensor_copy(idx, expert[tt][:, bass.ds((i * 2 + half) * GB, GB)]).then_inc(expert8_ready.sem, 1)
                        pool.wait_ge(expert8_ready.sem, i * 2 + (phase * (SLOTS // GB) + half + 1))
                        for j in range(GB):
                            pool.wait_ge(rows_free, first + (j + 1))
                            pool.sem_inc(gather_go, 1)
                            gp.indirect_dma_start(out=rows[:, j], out_offset=None, in_=weights,
                                                  in_offset=bass.IndirectOffsetOnAxis(ap=idx[:, j:j + 1], axis=0)).then_inc(rows_ld[j], 16)

            pool.wait_ge(rows_free, GB + 2 * QT * SLOTS)
            for s in (1, 2):
                modulation(s)
                final_scale(s)

        @block.scalar
        def _(sc_e):
            ac = nc.scalar

            def root(name, rows=P):
                k, cols, width = norm_at[name]
                sc_e.wait_ge(sums.sem, k + 1)
                roots.mark(ac.activation(rstd[0:rows, cols], stats[0:rows, cols], ACT.Sqrt, bias=eps[0:rows], scale=1.0 / width))

            def evac(job, pairs, scale=1.0):
                bank = full_bank(sc_e, job, a_at, lane_a, a_full)
                for dst, src in pairs(bank):
                    last = ac.activation(dst, src, ACT.Copy, scale=scale)
                a_free.mark(last)

            ac.dma_start(w_slot[0], t["w_in"][0].rearrange("(k p) n -> p k n", p=P)[:, :, C_C:C_C + 512]).then_inc(ld_c, 16)
            sc_e.wait_ge(consts.sem, 9)
            for tt in range(3):
                root(("x", tt), ROWS[tt])
            sc_e.wait_ge(gains_ready.sem, 1)
            c_ready.mark(ac.activation(c_act, gains[:, GAIN["c_2"]:GAIN["c_2"] + KD], ACT.Silu))
            for tt in range(3):
                evac(("c", tt), lambda b: [(pr[0:ROWS[tt], tt, C_C:C_C + 512], b[0:ROWS[tt], :])])
            for tt in range(3):
                evac(("rope", tt), lambda b: [(pr[0:ROWS[tt], tt, C_ROPE:C_ROPE + ROPE], b[0:ROWS[tt], 0:ROPE])])
            for tt in range(3):
                root(("c", tt), ROWS[tt])
            for tt in range(3):
                evac(("dk", tt), lambda b: [(pr[0:ROWS[tt], tt, C_DK:C_DK + 512], b[0:ROWS[tt], :])])
            for tt in range(QT):
                evac(("dq", tt), lambda b: [(pr[:, tt, C_DQ:C_DQ + 512], b[:, :])])
            for tt in range(3):
                root(("dk", tt), ROWS[tt])
            for tt in range(3):
                for n in range(2):
                    if tt < QT:
                        w = 512 if n == 0 else MH * QK - 512
                        evac(("q", tt, n), lambda b: [(q_row[:, tt, n * 512:n * 512 + w], b[:, 0:w])])
                for n in range(2):
                    def kv(b):
                        b = b[0:ROWS[tt], :].rearrange("p (h c) -> p h c", h=4)
                        k4 = k_row[0:ROWS[tt], tt].rearrange("p (h c) -> p h c", h=MH)[:, 4 * n:4 * n + 4, 0:NOPE]
                        v4 = v_row[0:ROWS[tt], tt].rearrange("p (h c) -> p h c", h=MH)[:, 4 * n:4 * n + 4]
                        return [(k4, b[:, :, 0:NOPE]), (v4, b[:, :, NOPE:])]
                    evac(("kv", tt, n), kv)
            for tt in range(QT):
                root(("dq", tt))
            for tt in range(3):
                evac(("dv", tt), lambda b: [(pr[0:ROWS[tt], tt, C_DV:C_DV + 512], b[0:ROWS[tt], :])])
            for tt in range(3):
                r = ROWS[tt]
                evac(("dkT", tt), lambda b: [(dkT[:, :, COL0[tt]:COL0[tt] + r], b[:, 0:4 * r].rearrange("p (h n) -> p h n", h=4))],
                     scale=gains[:, GAIN["diff_k_norm"]:GAIN["diff_k_norm"] + 1])
            for tt in range(QT):
                evac(("dqT", tt), lambda b: [(dqT[:, :, P * tt:P * tt + P], b[:, :].rearrange("p (h n) -> p h n", h=4))],
                     scale=gains[:, GAIN["diff_q_norm"]:GAIN["diff_q_norm"] + 1])
            for name in (("q", 0), ("k", 0), ("q", 1), ("k", 1), ("k", 2)):
                root(name, ROWS_OF.get(name, P))
            for tt in range(3):
                r = ROWS[tt]
                for n in range(2):
                    if tt < QT:
                        evac(("qT", tt, n), lambda b: [(qT[0:QK, 4 * n:4 * n + 4, P * tt:P * tt + P],
                                                        b[0:QK, :].rearrange("p (h n) -> p h n", h=4))],
                             scale=gains[0:QK, GAIN["mla_qk_norm_q"]:GAIN["mla_qk_norm_q"] + 1])
                for n in range(2):
                    evac(("kT", tt, n), lambda b: [(kT[0:QK, 4 * n:4 * n + 4, COL0[tt]:COL0[tt] + r],
                                                    b[0:QK, 0:4 * r].rearrange("p (h n) -> p h n", h=4))],
                         scale=gains[0:QK, GAIN["mla_qk_norm_k"]:GAIN["mla_qk_norm_k"] + 1])
            sc_e.wait_ge(lam_sums.sem, 1)
            lam_exps.mark(ac.activation(lam[:, 2:4], lam[:, 0:2], ACT.Exp))
            for i in range(len(STEPS) + 1):
                if i < len(STEPS):
                    tt, g = STEPS[i]
                    nk = META + P * (tt + 1)
                    sc_e.wait_ge(m_ready.sem, i + 1)
                    if i >= 2:
                        sc_e.wait_ge(a_full.sem, a_at["pT", i - 2, maps(STEPS[i - 2][1])[-1]] + 1)
                    for m in range(4):
                        last = ac.activation(pb[i % 2][:, m, 0:nk], sc[i % 2][:, m, 0:nk], ACT.Exp,
                                             bias=small[:, 16 * i + 4 + m:16 * i + 5 + m],
                                             accum_out=small[:, 16 * i + 8 + m:16 * i + 9 + m])
                    p_ready.mark(last)
                if i:
                    tt, g = STEPS[i - 1]
                    if i >= 2:
                        sc_e.wait_ge(d_full.sem, d_at["o", i - 2] + 1)
                    for m in maps(g):
                        s = m
                        evac(("pT", i - 1, m), lambda b: [(pT[0:META, s, 0], b[0:META, 0:P]),
                                                          (pT[:, s, 1:2 + tt], b[:, P:P * (2 + tt)].rearrange("p (k n) -> p k n", n=P))])
            root("subln")
            for job in ADA_JOBS:
                if job == "columns":
                    evac(("ada", job), lambda b: [(mod[:, 0, 0:2], b[:, 0:2 * KD].rearrange("p (m k) -> p m k", m=2))])
                else:
                    evac(("ada", job), lambda b: [(gates[0][:, job * 512:(job + 1) * 512], b[:, :])], scale=0.5)
            root("h1")
            for n in range(4):
                evac(("keysT", n), lambda b: [(keysT[:, 4 * n:4 * n + 4], b[:, :].rearrange("p (s n) -> p s n", s=4))])
            for job in q_jobs:
                what, tt, n = job
                dst = pqT[:, 4 * n:4 * n + 4, P * tt:P * tt + P] if what == "pq" else ps[tt][:, 4 * n:4 * n + 4]
                evac(job, lambda b: [(dst, b[:, :].rearrange("p (s n) -> p s n", s=4))])

            def soft(tt):
                sc_e.wait_ge(bests.sem, tt + 1)
                softs.mark(ac.activation(gate[tt], gate[tt], ACT.Exp))

            for tt in range(QT):
                soft(tt)
            for tt in range(QT):
                sc_e.wait_ge(dots_ready.sem, tt + 1)
                acts_ready.mark(ac.activation(dots[tt], dots[tt], ACT.Gelu))

            def round_slot(f):
                def split(i, parity, c):
                    slot = ffn_slot(f, parity, c)
                    sc_e.wait_ge(w_ld[slot], landed(f, i, parity, c))
                    ac.activation(w_hi[slot], w_slots[slot], ACT.Copy).then_inc(hi_ready.sem, 1)
                return split

            for c in range(2):
                round_slot(0)(0, 0, c)

            def norm_part(s):
                b = slice(2 * s, 2 * s + 2)
                sc_e.wait_ge(b_sums.sem, s + 1)
                b_roots.mark(ac.activation(rstd[:, b], stats[:, b], ACT.Sqrt, bias=eps, scale=1.0 / D))
                if s == 3:
                    return
                sc_e.wait_ge(mod_ready.sem, s + 1)
                for j in (1, 3):
                    sc_e.wait_ge(flipped.sem, 4 * s + j + 1)
                    for k in (2 * j, 2 * j + 1):
                        u_odd.mark(ac.activation(uT[:, k], psum[j][:, (k % 2) * SEQ:(k % 2 + 1) * SEQ], ACT.Identity,
                                                 scale=mod[:, s, 1, k:k + 1], bias=mod[:, s, 0, k:k + 1]))
                sc_e.wait_ge(u_odd.sem, u_odd.sent)
                for j in (1, 3):
                    last = ac.activation(u_hi[:, 2 * j:2 * j + 2], uT[:, 2 * j:2 * j + 2], ACT.Copy)
                u_hi_ready.mark(last)

            def silu_part(f):
                def tile(j, c):
                    sc_e.wait_ge(gu_full.sem, j + (f * FT + 1))
                    if f or not isinstance(j, int) or j >= 2:
                        sc_e.wait_ge(h_ready.sem, j + (f * FT - 1))
                    ac.activation(silu[:, c % 2], psum[c][:, 0:SEQ], ACT.Silu).then_inc(silu_ready.sem, 1)
                each_block(ac, tile, round_slot(f))

            def ada_out(s):
                for n, job in enumerate(ADA_JOBS):
                    sc_e.wait_ge(ada_full.sem, len(ADA_JOBS) * (s - 1) + n + 1)
                    if job == "columns":
                        ada_free.mark(ac.activation(mod[:, s, 0:2], psum[n][:, 0:2 * KD].rearrange("p (m k) -> p m k", m=2), ACT.Copy))
                    else:
                        ada_free.mark(ac.activation(gates[s][:, job * 512:(job + 1) * 512], psum[n][:, :], ACT.Copy, scale=(0.5, 1.0, 0.5)[s]))

            norm_part(0)
            silu_part(0)
            def round_mix(n):
                slot = mix_slot(n)
                sc_e.wait_ge(w_ld[slot], 16 * ((MIX0 + n) // RING + 1))
                if n == 14:
                    sc_e.wait_ge(conv_in.sem, 1)
                mix_hi_ready.mark(ac.activation(mix_hi_of(n), w_slots[slot], ACT.Copy))

            for n in range(2):
                round_mix(n)
            ada_out(1)
            norm_part(1)

            def x_out(n):
                sc_e.wait_ge(x_full.sem, n + 1)
                if n + 2 < IN:
                    round_mix(n + 2)
                bank = psum[4 + n % 4]
                two = bank[:, :].rearrange("p (a n) -> p a n", a=2)
                what, m = ("q", "k", "v", "cb", "cc", "cx", "ga", "ga", "gb", "gb")[n // 2], n % 2
                if what in ("q", "k"):
                    last = ac.activation((sqT if what == "q" else skT)[:, 2 * m:2 * m + 2], two, ACT.Copy)
                elif what == "v":
                    last = ac.activation(sv_row[:, :, 256 * m:256 * m + 256], two, ACT.Copy)
                elif what in ("cb", "cc", "cx"):
                    last = ac.activation({"cb": cbT, "cc": ccT, "cx": cxT}[what][:, 2 * m:2 * m + 2], two, ACT.Copy)
                else:
                    for j in range(2):
                        k = 2 * ((n - 12) % 4) + j
                        col = GAIN["b_merge_2"] + (0 if what == "ga" else KD) + k
                        last = ac.activation((sgaT if what == "ga" else sgbT)[:, k], two[:, j], ACT.Sigmoid, bias=gains[:, col:col + 1])
                x_act.mark(last)

            def soft_part(r):
                sc_e.wait_ge(min_ready.sem, r + 1)
                act.step(sc_e, ac.activation(zx, zx, ACT.Exp))
                e_ready.mark(ac.activation(zx, zx, ACT.Ln, bias=1.0))

            def prob_part(r):
                sc_e.wait_ge(log_ready.sem, r + 1)
                prob_ready.mark(ac.activation(zx, zlog, ACT.Exp))

            for n in range(6):
                x_out(n)
            soft_part(0)
            for n in range(6, 9):
                x_out(n)
            prob_part(0)
            for n in range(9, 12):
                x_out(n)
            soft_part(1)
            for n in range(12, 14):
                x_out(n)
            prob_part(1)
            for n in range(14, IN):
                x_out(n)
            sc_e.wait_ge(x_full.sem, x_at["wo", 0] + 1)
            for c in range(2):
                round_slot(1)(0, 0, c)
            ada_out(2)
            norm_part(2)
            silu_part(1)
            norm_part(3)

        @block.tensor
        def _(pe):
            te = nc.tensor

            def d_bank(job):
                return open_bank(pe, job, d_at, lane_d, d_free)

            def a_bank(job):
                return open_bank(pe, job, a_at, lane_a, a_free)

            def flip(bank, at, src, rows, cols):
                return te.transpose(bank[0:cols, at:at + rows], src, ident[0:rows, 0:rows])

            pe.wait_ge(consts.sem, 9)
            pe.wait_ge(ld_gain, 16 * (len(gain_src) + 7))
            bank = d_bank("gains")
            d_full.mark(flip(bank, 0, gain_rows, P, P))
            for tt in range(3):
                pe.wait_ge(xn_ready.sem, tt + 1)
                for b in range(2):
                    bank = d_bank(("nT", tt, b))
                    for j in range(4):
                        k = 4 * b + j
                        last = flip(bank, j * ROWS[tt], xn[0:ROWS[tt], tt, k * P:(k + 1) * P], ROWS[tt], P)
                    d_full.mark(last)

            def chunk(name, rhs, width, tiles):
                for tt in tiles:
                    bank = a_bank((name, tt))
                    pe.wait_ge(d_free.sem, d_at["nT", tt, 1] + 1)
                    for k in range(KD):
                        last = te.matmul(bank[0:ROWS[tt], 0:width], nT[:, k, COL0[tt]:COL0[tt] + ROWS[tt]], rhs[:, k],
                                         start=(k == 0), stop=(k == KD - 1))
                    a_full.mark(last)

            pe.wait_ge(ld_c, 16)
            chunk("c", w_slot[0], 512, range(3))
            pe.wait_ge(ld_hot, 32)
            for n in range(2):
                w = (512, KEYS + SEQ - 512)[n]
                bank = d_bank(("fill", n))
                d_full.mark(te.matmul(bank[0:4, 0:w], rel, onehot[:, n * 512:n * 512 + w], start=True, stop=True))
            pe.wait_ge(ld_rope_w, 16)
            chunk("rope", w_rope, ROPE, range(3))
            pe.wait_ge(ld_dk, 16)
            chunk("dk", w_slot[1], 512, range(3))
            for tt in range(3):
                pe.wait_ge(c_row_ready.sem, tt + 1)
                bank = d_bank(("cT", tt))
                for j in range(4):
                    last = flip(bank, j * ROWS[tt], pr[0:ROWS[tt], tt, j * P:(j + 1) * P], ROWS[tt], P)
                d_full.mark(last)
            pe.wait_ge(ld_dq, 16)
            chunk("dq", w_slot[2], 512, range(QT))
            pe.wait_ge(ld_up, 32)
            for tt in range(3):
                pe.wait_ge(d_free.sem, d_at["cT", tt] + 1)
                cols = slice(COL0[tt], COL0[tt] + ROWS[tt])
                for n in range(2):
                    if tt < QT:
                        w = 512 if n == 0 else MH * QK - 512
                        bank = a_bank(("q", tt, n))
                        for k in range(2):
                            last = te.matmul(bank[:, 0:w], cT[:, k, cols], w_uq[:, k, n * 512:n * 512 + w], start=(k == 0), stop=(k == 1))
                        a_full.mark(last)
                for n in range(2):
                    bank = a_bank(("kv", tt, n))
                    for k in range(2):
                        last = te.matmul(bank[0:ROWS[tt], :], cT[:, 2 + k, cols], w_ukv[:, k, n * 512:(n + 1) * 512],
                                         start=(k == 0), stop=(k == 1))
                    a_full.mark(last)
            pe.wait_ge(ld_dv, 16)
            chunk("dv", w_slot[0], 512, range(3))
            for tt in range(3):
                pe.wait_ge(dk_ready.sem, tt + 1)
                bank = a_bank(("dkT", tt))
                for h in range(DH):
                    last = flip(bank, h * ROWS[tt], pr[0:ROWS[tt], tt, C_DK + h * P:C_DK + (h + 1) * P], ROWS[tt], P)
                a_full.mark(last)
            for tt in range(QT):
                pe.wait_ge(dq_ready.sem, tt + 1)
                bank = a_bank(("dqT", tt))
                for h in range(DH):
                    last = flip(bank, h * P, pr[:, tt, C_DQ + h * P:C_DQ + (h + 1) * P], P, P)
                a_full.mark(last)
            for tt in range(3):
                for which, row in (("q", q_row), ("k", k_row)):
                    if which == "q" and tt == 2:
                        continue
                    pe.wait_ge(head_ready.sem, {("q", 0): 1, ("k", 0): 2, ("q", 1): 3, ("k", 1): 4, ("k", 2): 5}[which, tt])
                    for n in range(2):
                        bank = a_bank((which + "T", tt, n))
                        for j in range(4):
                            h = 4 * n + j
                            last = flip(bank, j * ROWS[tt], row[0:ROWS[tt], tt, h * QK:(h + 1) * QK], ROWS[tt], QK)
                        a_full.mark(last)
            for i in range(len(STEPS) + 1):
                if i < len(STEPS):
                    tt, g = STEPS[i]
                    nk = META + P * (tt + 1)
                    if i == 0:
                        pe.wait_ge(a_free.sem, a_at["kT", 2, 1] + 1)
                    for m in range(4):
                        bank = d_bank(("s", i, m))
                        if g < 2:
                            h = 4 * g + m
                            ins = te.matmul(bank[:, 0:nk], qT[0:QK, h, P * tt:P * tt + P], kT[0:QK, h, 0:nk], start=True, stop=True)
                        else:
                            h, c = 2 * (g - 2) + m // 2, DD * (m % 2)
                            ins = te.matmul(bank[:, 0:nk], dqT[c:c + DD, h, P * tt:P * tt + P], dkT[c:c + DD, h, 0:nk], start=True, stop=True)
                        d_full.mark(ins)
                if i:
                    tt, g = STEPS[i - 1]
                    if g < 2:
                        pe.wait_ge(p_ready.sem, i)
                    else:
                        pe.wait_ge(a_ready.sem, 2 * tt + g - 1)
                    for m in maps(g):
                        bank = a_bank(("pT", i - 1, m))
                        src = pb[(i - 1) % 2][:, m]
                        flip(bank, 0, src[:, 0:META], P, META)
                        for k in range(tt + 1):
                            last = flip(bank, P * (k + 1), src[:, META + P * k:META + P * (k + 1)], P, P)
                        a_full.mark(last)
                    bank = d_bank(("o", i - 1))
                    for m in maps(g):
                        pe.wait_ge(a_free.sem, a_at["pT", i - 1, m] + 1)
                        if g < 2:
                            h, w = 4 * g + m, MV
                            dst, v = bank[:, m * MV:(m + 1) * MV], v_row
                            vc = slice(h * MV, (h + 1) * MV)
                        else:
                            h = 2 * (g - 2) + m // 2
                            dst, v = bank[:, (m // 2) * DV:(m // 2 + 1) * DV], pr
                            vc = slice(C_DV + h * DV, C_DV + (h + 1) * DV)
                        s = m
                        te.matmul(dst, pT[0:META, s, 0], v[0:META, 2, vc], start=True, stop=False)
                        for k in range(tt + 1):
                            last = te.matmul(dst, pT[:, s, 1 + k], v[:, k, vc], start=False, stop=(k == tt))
                    d_full.mark(last)
            def over_partitions(bank, s, job):
                if job == "columns":
                    for col in range(2 * KD):
                        m, k = divmod(col, KD)
                        last = te.matmul(bank[:, col:col + 1], ada_sum[s][m][:, k * P:(k + 1) * P], ones[:, 0:1], start=True, stop=True)
                    return last
                return te.matmul(bank[:, :], ones, ada_sum[s][2][:, job * 512:(job + 1) * 512], start=True, stop=True)

            pe.wait_ge(ada_ready.sem, 1)
            for job in ADA_JOBS:
                bank = a_bank(("ada", job))
                a_full.mark(over_partitions(bank, 0, job))
            for tt in range(QT):
                pe.wait_ge(y_ready.sem, 1)
                for b in range(2):
                    bank = d_bank(("yT", tt, b))
                    for j in range(4):
                        last = flip(bank, j * P, y[:, tt, (4 * b + j) * P:(4 * b + j + 1) * P], P, P)
                    d_full.mark(last)
            pe.wait_ge(ld_wo, 32)
            pe.wait_ge(d_free.sem, d_at["yT", QT - 1, 1] + 1)
            for n in range(2):
                for tt in range(QT):
                    bank = d_bank(("wo", n, tt))
                    for k in range(KD):
                        last = te.matmul(bank[:, :], yT[:, k, P * tt:P * tt + P], wo_half[n][:, k], start=(k == 0), stop=(k == KD - 1))
                    d_full.mark(last)

            pe.wait_ge(ld_keys, 16)
            for n in range(4):
                bank = a_bank(("keysT", n))
                for j in range(4):
                    last = flip(bank, j * P, keys[:, 4 * n + j], P, P)
                a_full.mark(last)
            for tt in range(QT):
                pe.wait_ge(hn_ready.sem, tt + 1)
                for b in range(2):
                    bank = d_bank(("hnT", tt, b))
                    for j in range(4):
                        last = flip(bank, j * P, hn[:, tt, (4 * b + j) * P:(4 * b + j + 1) * P], P, P)
                    d_full.mark(last)
            pe.wait_ge(d_free.sem, d_at["hnT", QT - 1, 1] + 1)
            for job in q_jobs:
                what, tt, n = job
                if what == "pq":
                    pe.wait_ge(ld_wq[n], 16)
                else:
                    pe.wait_ge(a_free.sem, a_at["pq", tt, n] + 1)
                bank = a_bank(job)
                for j in range(4):
                    if what == "pq":
                        for k in range(KD):
                            last = te.matmul(bank[:, j * P:(j + 1) * P], wq_chunk[n][:, k, j * P:(j + 1) * P],
                                             hnT[:, k, P * tt:P * tt + P], start=(k == 0), stop=(k == KD - 1))
                    else:
                        last = te.matmul(bank[:, j * NK:(j + 1) * NK], pqT[:, 4 * n + j, P * tt:P * tt + P], keysT[:, 4 * n + j], start=True, stop=True)
                a_full.mark(last)
            def transposed_norm(s):
                for j in range(4):
                    for tt in range(QT):
                        if j == 0:
                            pe.wait_ge(n_ready.sem, QT * s + tt + 1)
                    for a in range(2):
                        for tt in range(QT):
                            last = flip(psum[j], a * SEQ + tt * P, nrm[:, tt, (2 * j + a) * P:(2 * j + a + 1) * P], P, P)
                    flipped.mark(last)
                pe.wait_ge(u_even.sem, 4 * (s + 1))
                pe.wait_ge(u_odd.sem, 4 * (s + 1))
                pe.wait_ge(u_split.sem, s + 1)

            THREE = ((0, 0), (0, 1), (1, 0))

            def ffn(f):
                def up(j, c, i):
                    if f or not isinstance(j, int) or j >= 4:
                        pe.wait_ge(h_ready.sem, j + (f * FT - 3))
                    parity = c // 2
                    for w in range(2):
                        if c % 2 == 0:
                            pe.wait_ge(lo_ready.sem, split_count(f, i * 2 + parity, w))
                        slot = ffn_slot(f, parity, w)
                        weight = [x.rearrange("p (k n) -> p k n", k=KD) for x in (w_hi[slot], w_lo[slot])]
                        for k in range(KD):
                            for n, (a, b) in enumerate(THREE):
                                last = te.matmul(psum[c][:, w * SEQ:(w + 1) * SEQ], weight[a][:, k, (c % 2) * P:(c % 2 + 1) * P], (u_hi, u_lo)[b][:, k],
                                                 start=(k == 0 and n == 0), stop=(k == KD - 1 and n == 2), skip_group_check=True)
                    last.then_inc(gu_full.sem, 1)

                def down(j, c, i, first=False, final=False):
                    pe.wait_ge(h_ready.sem, j + (f * FT + 1))
                    parity = c // 2
                    if c % 2 == 0:
                        pe.wait_ge(lo_ready.sem, split_count(f, i * 2 + parity, 2))
                    slot = ffn_slot(f, parity, 2)
                    weight = [x.rearrange("p (j n) -> p j n", j=2) for x in (w_hi[slot], w_lo[slot])]
                    for tt in range(QT):
                        for m, (a, b) in enumerate(THREE):
                            for n in range(2):
                                last = te.matmul(psum[4 + 2 * tt + n][:, :], (h_hi, h_lo)[a][:, c, tt * P:(tt + 1) * P],
                                                 weight[b][:, c % 2, n * 512:(n + 1) * 512],
                                                 start=first and m == 0, stop=final and m == 2, skip_group_check=True)
                    last.then_inc(down_done.sem, 1)

                for j in range(4):
                    up(j, j, 0)
                    if j >= 2:
                        down(j - 2, j - 2, 0, first=(j == 2))
                with te.Fori(1, 5) as i:
                    for c in range(4):
                        up(i * 4 + c, c, i)
                        if c >= 2:
                            down(i * 4 + (c - 2), c - 2, i)
                        else:
                            down(i * 4 + (c - 2), c + 2, i - 1)
                for j in (20, 21):
                    up(j, j % 4, 5)
                    down(j - 2, (j - 2) % 4, 4)
                down(20, 0, 5)
                down(21, 1, 5, final=True)

            def modulation(s):
                pe.wait_ge(ada_ready.sem, s + 1)
                for n, job in enumerate(ADA_JOBS):
                    ada_full.mark(over_partitions(psum[n], s, job))
                pe.wait_ge(ada_free.sem, len(ADA_JOBS) * s)

            transposed_norm(0)
            ffn(0)
            modulation(1)
            pe.wait_ge(ffn_out.sem, 1)
            transposed_norm(1)

            def x_bank(job):
                n = x_at[job]
                if 4 <= n < 24:
                    pe.wait_ge(x_act.sem, n - 3)
                elif n >= 24:
                    pe.wait_ge(x_dve.sem, n - 23)
                return psum[4 + n % 4]

            def z_bank(job):
                n = z_at[job]
                if n >= 4:
                    pe.wait_ge(z_free.sem, n - 3)
                return psum[n % 4]

            def weight(n, width):
                slot = (MIX0 + n) % RING
                pe.wait_ge(w_ld[slot], 16 * ((MIX0 + n) // RING + 1))
                return w_slots[slot].rearrange("p (k n) -> p k n", k=2048 // width)

            def project(n):
                pe.wait_ge(mix_lo_ready.sem, n + 1)
                w = [x.rearrange("p (k n) -> p k n", k=KD) for x in (mix_hi_of(n), w_lo[mix_slot(n)])]
                u = (u_hi, u_lo)
                bank = x_bank(("in", n))
                for a in range(2):
                    cols = slice(a * P, (a + 1) * P)
                    for k in range(KD):
                        for m, (i, j) in enumerate(THREE):
                            start, stop = k == 0 and m == 0, k == KD - 1 and m == 2
                            if 4 <= n < 6:
                                last = te.matmul(bank[:, a * 256:(a + 1) * 256], u[i][:, k, cols], w[j][:, k], start=start, stop=stop)
                            else:
                                last = te.matmul(bank[:, a * SEQ:(a + 1) * SEQ], w[i][:, k, cols], u[j][:, k], start=start, stop=stop)
                x_full.mark(last)

            def z_maps(r):
                for h in range(4):
                    bank = z_bank(("z", r, h))
                    pair, c = (4 * r + h) // 2, SD * (h % 2)
                    rows_ = slice(c, c + SD)
                    te.matmul(bank[:, 0:SEQ], skT[rows_, pair, 0:P], sqT[rows_, pair], start=True, stop=True)
                    z_full.mark(te.matmul(bank[:, SEQ:ZW], skT[rows_, pair, P:], sqT[rows_, pair, P:], start=True, stop=True))

            def remainders(r):
                pe.wait_ge(sp_ready.sem, r + 1)
                for h in range(4):
                    bank = z_bank(("rem", r, h))
                    te.matmul(bank[:, 0:SEQ], later, zsp[:, h, 0:SEQ], start=True, stop=False, skip_group_check=True)
                    te.matmul(bank[:, P:SEQ], ones, zsp[:, h, SEQ:ZW], start=False, stop=True, skip_group_check=True)
                    z_full.mark(te.matmul(bank[:, SEQ:ZW], later, zsp[:, h, SEQ:ZW], start=True, stop=True, skip_group_check=True))

            def attend(r):
                pe.wait_ge(masked.sem, r + 1)
                bank = z_bank(("o", r))
                for h in range(4):
                    c, at_ = SD * (h % 2), SEQ * (h // 2)
                    vc = slice((4 * r + h) * SD, (4 * r + h + 1) * SD)
                    te.matmul(bank[c:c + SD, at_:at_ + SEQ], sv_row[:, 0, vc], zx[:, h, 0:SEQ], start=True, stop=False, skip_group_check=True)
                    last = te.matmul(bank[c:c + SD, at_ + P:at_ + SEQ], sv_row[:, 1, vc], zx[:, h, SEQ:ZW], start=False, stop=True, skip_group_check=True)
                z_full.mark(last)

            for n in range(6):
                project(n)
            pe.wait_ge(x_act.sem, 6)
            z_maps(0)
            for n in range(6, 9):
                project(n)
            remainders(0)
            for n in range(9, 12):
                project(n)
            attend(0)
            z_maps(1)
            for n in range(12, 14):
                project(n)
            remainders(1)
            for n in range(14, 16):
                project(n)
            attend(1)
            for n in range(16, 20):
                project(n)
            for name, src, ready, kind in (("ya", convT, conv_ready, "conv"), ("yb", oT, z_free, "attn")):
                pe.wait_ge(ready.sem, 1 if name == "ya" else len(z_jobs))
                for n in range(4):
                    if n % 2 == 0:
                        w = weight(20 + (2 if name == "yb" else 0) + n // 2, 512)
                    bank = x_bank((name, n))
                    for a in range(2):
                        for k in range(4):
                            col = (n % 2) * 256 + a * P
                            last = te.matmul(bank[:, a * SEQ:(a + 1) * SEQ], w[:, k, col:col + P], src[:, k], start=(k == 0), stop=(k == 3))
                    x_full.mark(last)
            pe.wait_ge(merged_ready.sem, 4)
            for n in range(4):
                w = weight(24 + n, 256)
                bank = x_bank(("wo", n))
                for tt in range(QT):
                    for k in range(KD):
                        last = te.matmul(bank[:, tt * 256:(tt + 1) * 256], sgaT[:, k, tt * P:(tt + 1) * P], w[:, k], start=(k == 0), stop=(k == KD - 1))
                x_full.mark(last)
            pe.wait_ge(z_free.sem, len(z_jobs))
            modulation(2)
            transposed_norm(2)
            ffn(1)

        @block.vector
        def _(ve):
            v = nc.vector

            def take(job):
                return full_bank(ve, job, d_at, lane_d, d_full)

            def step(ins):
                dve.step(ve, ins)

            def sum_squares(name, src, rows=P):
                k, cols, width = norm_at[name]
                n = cols.stop - cols.start
                sq = tmp[0:rows, 0:n * width].rearrange("p (g w) -> p g w", g=n)
                step(v.tensor_tensor(sq, src, src, ALU.mult))
                assert sums.sent == k
                sums.step(ve, v.tensor_reduce(stats[0:rows, cols], sq, AX, ALU.add))

            def invert(name, rows=P):
                k, cols, width = norm_at[name]
                ve.wait_ge(roots.sem, k + 1)
                step(v.reciprocal(rstd[0:rows, cols], rstd[0:rows, cols]))
                return rstd[0:rows, cols]

            for tt in range(3):
                r = ROWS[tt]
                src = hx[:, tt] if tt < QT else hm
                ve.wait_ge(ld_x[tt], 16)
                sums.step(ve, v.tensor_tensor_reduce(out=tmp[0:r], in0=src[0:r], in1=src[0:r], scale=1.0, scalar=0.0,
                                                     op0=ALU.mult, op1=ALU.add, accum_out=stats[0:r, tt:tt + 1]))
            for tt in range(3):
                r = ROWS[tt]
                src = hx[:, tt] if tt < QT else hm
                inv = invert(("x", tt), r)
                xn_ready.mark(v.tensor_scalar(xn[0:r, tt], src[0:r], inv, None, ALU.mult))
            bank = take("gains")
            gains_ready.step(ve, v.tensor_copy(gains, bank[:, 0:P]))
            d_free.mark(v.tensor_copy(small[:, 0:1], bank[:, 0:1]))
            for tt in range(3):
                r = ROWS[tt]
                for b in range(2):
                    bank = take(("nT", tt, b))
                    g = GAIN["attn_norm"] + 4 * b
                    d_free.mark(v.tensor_tensor(nT[:, 4 * b:4 * b + 4, COL0[tt]:COL0[tt] + r],
                                                bank[:, 0:4 * r].rearrange("p (k n) -> p k n", k=4),
                                                spread(gains[:, g:g + 4], P, 4, r), ALU.mult))
            for n in range(2):
                w = (512, KEYS + SEQ - 512)[n]
                bank = take(("fill", n))
                last = v.tensor_copy(fill[:, n * 512:n * 512 + w], bank[0:4, 0:w])
                d_free.step(ve, last)
            fill_ready.step(ve, v.tensor_copy(small[:, 1:2], small[:, 0:1]))
            ve.wait_ge(ld_small, 16 * 9)
            pairs = lam_in.rearrange("p (a b) d -> p a b d", b=2)
            lam_sq = tmp[:, 0:2 * DD].rearrange("p (a d) -> p a d", a=2)
            step(v.tensor_tensor(lam_sq, pairs[:, :, 0], pairs[:, :, 1], ALU.mult))
            lam_sums.step(ve, v.tensor_reduce(lam[:, 0:2], lam_sq, AX, ALU.add))
            for tt in range(3):
                r = ROWS[tt]
                ve.wait_ge(a_free.sem, a_at["c", tt] + 1)
                src = pr[0:r, tt, 0:512].rearrange("p (g w) -> p g w", g=2)
                k, cols, _ = norm_at["c", tt]
                for j in range(2):
                    ins = v.tensor_tensor_reduce(out=tmp[0:r, 256 * j:256 * j + 256], in0=src[:, j], in1=src[:, j], scale=1.0, scalar=0.0,
                                                 op0=ALU.mult, op1=ALU.add, accum_out=stats[0:r, cols.start + j:cols.start + j + 1])
                    (step if j == 0 else lambda x: sums.step(ve, x))(ins)
            for tt in range(3):
                r = ROWS[tt]
                inv = invert(("c", tt), r)
                src = pr[0:r, tt, 0:512].rearrange("p (g w) -> p g w", g=2)
                c_row_ready.mark(v.tensor_tensor(src, src, spread(inv, r, 2, 256), ALU.mult))
            for tt in range(3):
                r = ROWS[tt]
                bank = take(("cT", tt))
                g = GAIN["mla_q_norm"]
                d_free.mark(v.tensor_tensor(cT[:, :, COL0[tt]:COL0[tt] + r], bank[:, 0:4 * r].rearrange("p (k n) -> p k n", k=4),
                                            spread(gains[:, g:g + 4], P, 4, r), ALU.mult))
            def half_heads(name, tt, c, ready):
                r = ROWS[tt]
                src = pr[0:r, tt, c:c + 512].rearrange("p (g w) -> p g w", w=DD)
                if ready is None:
                    sum_squares((name, tt), src, r)
                else:
                    ready.mark(v.tensor_tensor(src, src, spread(invert((name, tt), r), r, 8, DD), ALU.mult))
            for tt in range(3):
                ve.wait_ge(a_free.sem, a_at["dk", tt] + 1)
                half_heads("dk", tt, C_DK, None)
            for tt in range(3):
                half_heads("dk", tt, C_DK, dk_ready)
            for tt in range(QT):
                ve.wait_ge(a_free.sem, a_at["dq", tt] + 1)
                half_heads("dq", tt, C_DQ, None)
            for tt in range(QT):
                half_heads("dq", tt, C_DQ, dq_ready)
            order = [("q", 0), ("k", 0), ("q", 1), ("k", 1), ("k", 2)]
            def heads(which, tt):
                row = (q_row if which == "q" else k_row)[0:ROWS[tt], tt]
                return row.rearrange("p (h c) -> p h c", h=MH)
            for which, tt in order:
                r = ROWS[tt]
                ve.wait_ge(a_free.sem, a_at["q" if which == "q" else "kv", tt, 1] + 1)
                hd = heads(which, tt)
                if which == "k":
                    krope = pr[0:r, tt, C_ROPE:C_ROPE + ROPE].unsqueeze(1).to_broadcast([r, MH, ROPE])
                    step(v.tensor_copy(hd[:, :, NOPE:], krope))
                sum_squares((which, tt), hd, r)
            for which, tt in order:
                r = ROWS[tt]
                hd = heads(which, tt)
                step(v.tensor_tensor(hd, hd, spread(invert((which, tt), r), r, MH, QK), ALU.mult))
                a4, b4, g4 = (rot[0:r, s] for s in range(3))
                step(v.tensor_tensor(g4, hd[:, :, NOPE:], g_rope[0:r, 0 if which == "q" else 1].unsqueeze(1).to_broadcast([r, MH, ROPE]), ALU.mult))
                cs = rope[0:r, tt].rearrange("p (w c) -> p w c", w=2)
                halves = [x.rearrange("p h (w c) -> p h w c", w=2) for x in (a4, b4, g4)]
                for j in range(2):
                    tab = cs[:, j].unsqueeze(1).unsqueeze(1).to_broadcast([r, MH, 2, HALF])
                    step(v.tensor_tensor(halves[j], halves[2], tab, ALU.mult))
                step(v.tensor_tensor(hd[:, :, NOPE:NOPE + HALF], halves[0][:, :, 0], halves[1][:, :, 1], ALU.subtract))
                head_ready.mark(v.tensor_tensor(hd[:, :, NOPE + HALF:], halves[0][:, :, 1], halves[1][:, :, 0], ALU.add))
            ve.wait_ge(lam_exps.sem, 1)
            step(v.tensor_scalar(lam[:, 0:1], lam[:, 2:3], LAMBDA_INIT, lam[:, 3:4], ALU.add, ALU.subtract))
            ve.wait_ge(bias_ready.sem, 5)
            for i in range(len(STEPS) + 1):
                if i < len(STEPS):
                    tt, g = STEPS[i]
                    nk = META + P * (tt + 1)
                    if i >= 2:
                        ve.wait_ge(p_ready.sem, i - 1)
                    for m in range(4):
                        bank = take(("s", i, m))
                        add = mask[:, tt, 0:nk] if g < 2 else bias[:, 2 * (g - 2) + m // 2, tt, 0:nk]
                        d_free.mark(v.scalar_tensor_tensor(out=sc[i % 2][:, m, 0:nk], in0=bank[:, 0:nk],
                                                           scalar=float((QK if g < 2 else DD) ** -0.5), in1=add, op0=ALU.mult, op1=ALU.add))
                    ve.wait_ge(d_free.sem, d_free.sent)
                    step(v.tensor_reduce(small[:, 16 * i:16 * i + 4], sc[i % 2][:, :, 0:nk], AX, ALU.max))
                    m_ready.mark(v.tensor_scalar(small[:, 16 * i + 4:16 * i + 8], small[:, 16 * i:16 * i + 4], -1.0, None, ALU.mult))
                if i:
                    tt, g = STEPS[i - 1]
                    nk = META + P * (tt + 1)
                    z = small[:, 16 * i - 8:16 * i - 4]
                    rz = small[:, 16 * i - 4:16 * i]
                    ve.wait_ge(p_ready.sem, i)
                    step(v.reciprocal(rz, z))
                    if g >= 2:
                        p4 = pb[(i - 1) % 2]
                        step(v.tensor_scalar(z, rz, lam[:, 0:1], -1.0, ALU.mult, ALU.mult))
                        for m in maps(g):
                            step(v.tensor_scalar(p4[:, m, 0:nk], p4[:, m, 0:nk], rz[:, m:m + 1], None, ALU.mult))
                            ins = v.scalar_tensor_tensor(out=p4[:, m, 0:nk], in0=p4[:, m + 1, 0:nk], scalar=z[:, m + 1:m + 2],
                                                         in1=p4[:, m, 0:nk], op0=ALU.mult, op1=ALU.add)
                        a_ready.mark(ins)
                    bank = take(("o", i - 1))
                    dst = y[:, tt, 256 * g:256 * g + 256]
                    if g < 2:
                        d_free.mark(v.tensor_tensor(dst.rearrange("p (h c) -> p h c", h=4), bank[:, 0:256].rearrange("p (h c) -> p h c", h=4),
                                                    spread(rz, P, 4, MV), ALU.mult))
                    else:
                        d_free.mark(v.tensor_copy(dst, bank[:, 0:256]))
            ve.wait_ge(d_free.sem, d_free.sent)
            yd = y[:, :, 512:].rearrange("p t (h c) -> p t h c", h=DH)
            k, cols, _ = norm_at["subln"]
            sq4 = tmp[:, 0:QT * DH * DV].rearrange("p (t h c) -> p t h c", t=QT, h=DH)
            step(v.tensor_tensor(sq4, yd, yd, ALU.mult))
            sums.step(ve, v.tensor_reduce(stats[:, cols].rearrange("p (t h) -> p t h", t=QT), sq4, AX, ALU.add))
            inv = invert("subln").rearrange("p (t h) -> p t h", t=QT)
            y_ready.mark(v.tensor_tensor(yd, yd, spread(inv, P, QT, DH, DV), ALU.mult))
            for tt in range(QT):
                for b in range(2):
                    bank = take(("yT", tt, b))
                    dst = yT[:, 4 * b:4 * b + 4, P * tt:P * tt + P]
                    src = bank[:, :].rearrange("p (k n) -> p k n", k=4)
                    if b == 0:
                        d_free.mark(v.tensor_copy(dst, src))
                    else:
                        g = GAIN["diff_subln"]
                        d_free.mark(v.tensor_scalar(dst, src, gains[:, g:g + 1], 1.0 - LAMBDA_INIT, ALU.mult, ALU.mult))
            for n in range(2):
                for tt in range(QT):
                    bank = take(("wo", n, tt))
                    dst = hx[:, tt, n * 512:(n + 1) * 512]
                    d_free.mark(v.tensor_tensor(dst, dst, bank[:, :], ALU.add))
            ve.wait_ge(d_free.sem, d_free.sent)
            for tt in range(QT):
                k, cols, _ = norm_at["h1"]
                ins = v.tensor_tensor_reduce(out=tmp, in0=hx[:, tt], in1=hx[:, tt], scale=1.0, scalar=0.0, op0=ALU.mult,
                                             op1=ALU.add, accum_out=stats[:, cols.start + tt:cols.start + tt + 1])
                (step if tt == 0 else lambda x: sums.step(ve, x))(ins)
            inv = invert("h1")
            ve.wait_ge(ld_gffn, 16)
            for tt in range(QT):
                hn_ready.mark(v.scalar_tensor_tensor(out=hn[:, tt], in0=hx[:, tt], scalar=inv[:, tt:tt + 1], in1=g_ffn, op0=ALU.mult, op1=ALU.mult))
            for tt in range(QT):
                for b in range(2):
                    bank = take(("hnT", tt, b))
                    d_free.mark(v.tensor_copy(hnT[:, 4 * b:4 * b + 4, P * tt:P * tt + P], bank[:, :].rearrange("p (k n) -> p k n", k=4)))
            for j in range(TOPK):
                last = v.memset(iota16[:, j:j + 1], float(j))
            step(last)

            def top16(values, vals, idxs):
                for x, o in zip(values, vals):
                    last = v.max(out=o[:, 0:8], in_=x)
                step(last)
                for x, o, ix in zip(values, vals, idxs):
                    last = v.max_index(out=ix[:, 0:8], in_max=o[:, 0:8], in_values=x)
                step(last)
                for x, o in zip(values, vals):
                    last = v.match_replace(out=x, in_to_replace=o[:, 0:8], in_values=x, imm_value=-3e38)
                step(last)
                for x, o in zip(values, vals):
                    last = v.max(out=o[:, 8:16], in_=x)
                step(last)
                for x, o, ix in zip(values, vals, idxs):
                    last = v.max_index(out=ix[:, 8:16], in_max=o[:, 8:16], in_values=x)
                step(last)

            def per_head(tab):
                return tab.rearrange("p (h k) -> p h k", h=PH)

            def top_keys(tt, part):
                segs = range(4 * part, 4 * part + 4)
                ve.wait_ge(a_free.sem, a_at["ps", tt, part] + 1)
                top16([ps[tt][:, s] for s in segs], [top_v[:, s] for s in segs], [top_i[:, s] for s in segs])

            def top_pairs(tt, part):
                pair = top_v.rearrange("p (h s) k -> p h s k", s=2)
                cand = wide[0]
                if part == 0:
                    step(v.tensor_copy(top_f, top_i))
                    step(v.tensor_tensor(cand, spread(pair[:, :, 0], P, PH, TOPK, TOPK),
                                         pair[:, :, 1].unsqueeze(2).to_broadcast([P, PH, TOPK, TOPK]), ALU.add))
                heads = range(4 * part, 4 * part + 4)
                top16([cand[:, h].rearrange("p a b -> p (a b)") for h in heads], [per_head(best)[:, h] for h in heads],
                      [per_head(flat)[:, h] for h in heads])
                if part == 1:
                    bests.mark(v.tensor_tensor(per_head(gate[tt]), per_head(best), spread(per_head(best)[:, :, 0], P, PH, TOPK), ALU.subtract))

            def pick(tt, half):
                idx_pair = top_f.rearrange("p (h s) k -> p h s k", s=2)
                op, arg, dst = ((ALU.logical_shift_right, 4, e_hi), (ALU.bitwise_and, TOPK - 1, e_lo))[half]
                step(v.tensor_scalar(half_i, flat, arg, None, op))
                step(v.tensor_copy(half_f, half_i))
                step(v.tensor_tensor(wide[1], spread(per_head(half_f), P, PH, TOPK, TOPK),
                                     iota16[:, 0:TOPK].unsqueeze(1).unsqueeze(1).to_broadcast([P, PH, TOPK, TOPK]), ALU.is_equal))
                step(v.tensor_tensor(wide[1], wide[1], idx_pair[:, :, half].unsqueeze(2).to_broadcast([P, PH, TOPK, TOPK]), ALU.mult))
                step(v.tensor_reduce(per_head(dst), wide[1], AX, ALU.add))
                if half == 1:
                    step(v.scalar_tensor_tensor(out=e_hi, in0=e_hi, scalar=float(NK), in1=e_lo, op0=ALU.mult, op1=ALU.add))
                    routed.step(ve, v.tensor_copy(expert[tt], e_hi))

            def normalize(tt):
                ve.wait_ge(softs.sem, tt + 1)
                z = slot8[:, 16:16 + PH]
                step(v.tensor_reduce(z, per_head(gate[tt]), AX, ALU.add))
                step(v.reciprocal(z, z))
                step(v.tensor_tensor(per_head(gate[tt]), per_head(gate[tt]), spread(z, P, PH, TOPK), ALU.mult))

            def dot_groups(tt, first, count):
                base = dve.sent
                with v.Fori(0, count) as i:
                    at = i + (tt * GROUPS + first)
                    for j in range(GB):
                        ve.wait_ge(rows_ld[j], at * 16 + 16)
                        if j >= 2:
                            ve.wait_ge(rows_free, at * GB + (GB + j - 1))
                        v.tensor_tensor_reduce(out=prod[:, j % 2], in0=rows[:, j], in1=hn[:, tt], scale=1.0, scalar=0.0, op0=ALU.mult,
                                               op1=ALU.add, accum_out=slot8[:, j:j + 1]).then_inc(rows_free, 1)
                    ve.wait_ge(rows_free, at * GB + 2 * GB)
                    v.tensor_copy(dots[tt][:, bass.ds((i + first) * GB, GB)], slot8[:, 0:GB]).then_inc(dve.sem, 1)
                    ve.wait_ge(dve.sem, i + (base + 1))
                dve.sent += count

            GROUPS = SLOTS // GB
            for q in range(4):
                top_keys(0, q)
            for half in range(2):
                top_pairs(0, half)
            for half in range(2):
                pick(0, half)
            ve.wait_ge(a_full.sem, max(a_at["pq", 1, n] for n in (2, 3)) + 1)
            v.tensor_copy(slot8[:, 32:33], iota16[:, 0:1]).then_inc(rows_free, GB)
            for i, q in enumerate(QUARTERS[1]):
                top_keys(1, q)
                if i == 0:
                    ve.wait_ge(a_full.sem, a_at["pq", 1, 1] + 1)
                dot_groups(0, 2 * i, 2)
            for half in range(2):
                top_pairs(1, half)
                dot_groups(0, 8 + 2 * half, 2)
            for half in range(2):
                pick(1, half)
                dot_groups(0, 12 + 2 * half, 2)
            dots_ready.mark(v.tensor_copy(slot8[:, 32:33], iota16[:, 0:1]))
            dot_groups(1, 0, GROUPS)
            dots_ready.mark(v.tensor_copy(slot8[:, 32:33], iota16[:, 0:1]))
            def lo_slot(f):
                def split(i, parity, c):
                    slot = ffn_slot(f, parity, c)
                    ve.wait_ge(hi_ready.sem, split_count(f, i * 2 + parity, c))
                    v.tensor_tensor(w_lo[slot], w_slots[slot], w_hi[slot].bitcast(F32), ALU.subtract).then_inc(lo_ready.sem, 1)
                return split

            base = dve.sent
            for tt in range(QT):
                ve.wait_ge(acts_ready.sem, tt + 1)
                if tt == 1:
                    for c in range(2):
                        lo_slot(0)(0, 0, c)
                normalize(tt)
                step(v.tensor_tensor(gate[tt], gate[tt], dots[tt], ALU.mult))
                base = dve.sent
                at = (QT + tt) * (SLOTS // GB)
                with v.Fori(0, SLOTS // GB) as i:
                    ve.wait_ge(rows_free, (i + at) * GB + GB)
                    v.tensor_copy(slot8[:, 0:GB], gate[tt][:, bass.ds(i * GB, GB)]).then_inc(dve.sem, 1)
                    ve.wait_ge(dve.sem, i + (base + 1))
                    for j in range(GB):
                        ve.wait_ge(rows_ld[j], (i + at) * 16 + 16)
                        ve.wait_ge(rows_free, (i + at) * GB + (GB + j))
                        v.scalar_tensor_tensor(out=hx[:, tt], in0=rows[:, j], scalar=slot8[:, j:j + 1], in1=hx[:, tt],
                                               op0=ALU.mult, op1=ALU.add).then_inc(rows_free, 1)
                dve.sent += SLOTS // GB
            ve.wait_ge(rows_free, GB + 2 * QT * SLOTS)

            def split_mix(*slots):
                for n in slots:
                    ve.wait_ge(mix_hi_ready.sem, n + 1)
                    slot = mix_slot(n)
                    mix_lo_ready.mark(v.tensor_tensor(w_lo[slot], w_slots[slot], mix_hi_of(n).bitcast(F32), ALU.subtract))

            def norm_rows(s):
                for tt in range(QT):
                    ins = v.tensor_tensor_reduce(out=part, in0=hx[:, tt], in1=hx[:, tt], scale=1.0, scalar=0.0, op0=ALU.mult, op1=ALU.add,
                                                 accum_out=stats[:, 2 * s + tt:2 * s + tt + 1])
                    (step if tt == 0 else lambda x: b_sums.step(ve, x))(ins)
                ve.wait_ge(b_roots.sem, s + 1)
                b = rstd[:, 2 * s:2 * s + 2]
                step(v.reciprocal(b, b))
                if s == 3:
                    ve.wait_ge(ld_final, 16)
                    for tt in range(QT):
                        out_ready.mark(v.scalar_tensor_tensor(out=nrm[:, tt], in0=hx[:, tt], scalar=b[:, tt:tt + 1], in1=g_final, op0=ALU.mult, op1=ALU.mult))
                    return
                for tt in range(QT):
                    n_ready.mark(v.tensor_scalar(nrm[:, tt], hx[:, tt], b[:, tt:tt + 1], None, ALU.mult))
                if s == 1:
                    split_mix(0, 1)
                ve.wait_ge(mod_ready.sem, s + 1)
                if s:
                    ve.wait_ge(ada_free.sem, len(ADA_JOBS) * s)
                for j in (0, 2):
                    ve.wait_ge(flipped.sem, 4 * s + j + 1)
                    for k in (2 * j, 2 * j + 1):
                        u_even.mark(v.tensor_scalar(uT[:, k], psum[j][:, (k % 2) * SEQ:(k % 2 + 1) * SEQ], mod[:, s, 1, k:k + 1],
                                                    mod[:, s, 0, k:k + 1], ALU.mult, ALU.add))
                ve.wait_ge(u_even.sem, u_even.sent)
                ve.wait_ge(flipped.sem, 4 * s + 4)
                for j in (0, 2):
                    last = v.tensor_copy(u_hi[:, 2 * j:2 * j + 2], uT[:, 2 * j:2 * j + 2])
                step(last)
                ve.wait_ge(u_hi_ready.sem, s + 1)
                u_split.mark(v.tensor_tensor(u_lo, uT, u_hi.bitcast(F32), ALU.subtract))

            def add_gated(bank, s, tt, cols):
                w = cols.stop - cols.start
                step(v.tensor_tensor(part[:, 0:w], bank, gates[s][:, cols], ALU.mult))
                return v.tensor_tensor(hx[:, tt, cols], hx[:, tt, cols], part[:, 0:w], ALU.add)

            def ffn_rows(f):
                def tile(j, c):
                    ve.wait_ge(silu_ready.sem, j + (f * FT + 1))
                    if f or not isinstance(j, int) or j >= 4:
                        ve.wait_ge(down_done.sem, j + (f * FT - 3))
                    order = j * 2 + (2 * f * FT)
                    v.tensor_tensor(hT[:, c], silu[:, c % 2], psum[c][:, SEQ:], ALU.mult).then_inc(h_order.sem, 1)
                    ve.wait_ge(h_order.sem, order + 1)
                    v.tensor_copy(h_hi[:, c], hT[:, c]).then_inc(h_order.sem, 1)
                    ve.wait_ge(h_order.sem, order + 2)
                    v.tensor_tensor(h_lo[:, c], hT[:, c], h_hi[:, c].bitcast(F32), ALU.subtract).then_inc(h_ready.sem, 1)
                each_block(v, tile, lo_slot(f))
                ve.wait_ge(down_done.sem, (f + 1) * FT)
                for tt in range(QT):
                    for n in range(2):
                        step(add_gated(psum[4 + 2 * tt + n][:, :], 2 * f, tt, slice(n * 512, (n + 1) * 512)))
                ffn_out.mark(v.tensor_copy(small[:, 0:1], small[:, 1:2]))

            norm_rows(0)
            ffn_rows(0)
            norm_rows(1)

            def scores_out(r):
                for h in range(4):
                    ve.wait_ge(z_full.sem, z_at["z", r, h] + 1)
                    bank = psum[z_at["z", r, h] % 4]
                    v.tensor_scalar(zlog[:, h], bank[:, 0:ZW], SD ** -0.5, 0.0, ALU.mult, ALU.min)
                    z_free.mark(v.tensor_scalar(zsp[:, h], bank[:, 0:ZW], SD ** -0.5, 0.0, ALU.mult, ALU.max))
                ve.wait_ge(z_free.sem, z_free.sent)
                min_ready.mark(v.tensor_tensor(zx, zlog, zsp, ALU.subtract))

            def seen_only(x):
                for c in (0, SEQ):
                    last = v.tensor_tensor(x[:, :, c:c + P], x[:, :, c:c + P], seen.unsqueeze(1).to_broadcast([P, 4, P]), ALU.mult)
                return last

            def softplus(r):
                ve.wait_ge(e_ready.sem, r + 1)
                v.tensor_tensor(zlog, zlog, zx, ALU.subtract)
                step(v.tensor_tensor(zsp, zsp, zx, ALU.add))
                sp_ready.mark(seen_only(zsp))

            def logs(r):
                for h in range(4):
                    ve.wait_ge(z_full.sem, z_at["rem", r, h] + 1)
                    bank = psum[z_at["rem", r, h] % 4]
                    z_free.mark(v.tensor_tensor(zlog[:, h], zlog[:, h], bank[:, 0:ZW], ALU.subtract))
                ve.wait_ge(z_free.sem, z_free.sent)
                log_ready.mark(v.tensor_copy(small[:, 0:1], small[:, 1:2]))
                ve.wait_ge(prob_ready.sem, r + 1)
                masked.mark(seen_only(zx))

            def heads_out(r):
                ve.wait_ge(z_full.sem, z_at["o", r] + 1)
                z_free.mark(v.tensor_copy(oT[:, 2 * r:2 * r + 2], psum[z_at["o", r] % 4][:, :].rearrange("p (a n) -> p a n", a=2)))

            last = v.memset(vT[:, :, 0:2], 0.0)
            step(last)
            split_mix(*range(2, 8))
            scores_out(0)
            softplus(0)
            split_mix(8, 9, 10)
            logs(0)
            split_mix(11, 12)
            heads_out(0)
            ve.wait_ge(x_act.sem, 12)
            conv_in.step(ve, v.tensor_tensor(vT[:, :, 2:], ccT, cxT, ALU.mult))
            split_mix(13)
            scores_out(1)
            softplus(1)
            split_mix(14, 15)
            logs(1)
            split_mix(16, 17)
            heads_out(1)
            split_mix(18, 19)
            for k in range(4):
                tap = [gains[:, conv_row + 4 * a + k:conv_row + 4 * a + k + 1] for a in range(3)]
                step(v.tensor_scalar(convT[:, k], vT[:, k, 0:SEQ], tap[0], None, ALU.mult))
                for a in (1, 2):
                    step(v.scalar_tensor_tensor(out=convT[:, k], in0=vT[:, k, a:a + SEQ], scalar=tap[a], in1=convT[:, k], op0=ALU.mult, op1=ALU.add))
            conv_ready.mark(v.tensor_tensor(convT, convT, cbT, ALU.mult))
            ve.wait_ge(x_act.sem, IN)
            for name in ("ya", "yb"):
                for n in range(4):
                    ve.wait_ge(x_full.sem, x_at[name, n] + 1)
                    two = psum[4 + x_at[name, n] % 4][:, :].rearrange("p (a n) -> p a n", a=2)
                    gate_ = (sgaT if name == "ya" else sgbT)[:, 2 * n:2 * n + 2]
                    x_dve.step(ve, v.tensor_tensor(gate_, gate_, two, ALU.mult))
                    if name == "yb":
                        merged_ready.mark(v.tensor_tensor(sgaT[:, 2 * n:2 * n + 2], sgaT[:, 2 * n:2 * n + 2], gate_, ALU.add))
            for c in range(2):
                lo_slot(1)(0, 0, c)
            for n in range(4):
                ve.wait_ge(x_full.sem, x_at["wo", n] + 1)
                bank = psum[4 + x_at["wo", n] % 4]
                for tt in range(QT):
                    ins = add_gated(bank[:, tt * 256:(tt + 1) * 256], 1, tt, slice(n * 256, (n + 1) * 256))
                    (step if tt == 0 else lambda x: x_dve.step(ve, x))(ins)
            norm_rows(2)
            ffn_rows(1)
            norm_rows(3)


_INS = ['x', 'meta_tokens', 'rel_bias', 'attn_norm', 'w_in', 'mla_q_norm', 'mla_w_uq', 'mla_kv_norm', 'mla_w_ukv',
        'mla_qk_norm_q', 'mla_qk_norm_k', 'diff_q_norm', 'diff_k_norm', 'diff_lambda_q1', 'diff_lambda_k1',
        'diff_lambda_q2', 'diff_lambda_k2', 'diff_subln', 'w_out', 'ffn_norm', 'peer_w_query', 'peer_sub_keys',
        'peer_u', 'peer_v', 'c_2', 'w_ada_2', 'b_ada_2', 'norm1_g_2', 'ffn1_w_gu_2', 'ffn1_w_down_2', 'norm2_g_2',
        'w_mix_in_2', 'b_merge_2', 'conv_w_2', 'w_conv_out_2', 'w_attn_out_2', 'w_out_2', 'norm3_g_2',
        'ffn2_w_gu_2', 'ffn2_w_down_2', 'final_g_2']


def kernel(**inputs):
    import numpy as _np
    import concourse.bacc as _bacc
    from concourse import mybir as _mybir
    from concourse.bass_utils import run_bass_kernel_spmd as _run

    nc = _bacc.Bacc("TRN2", target_bir_lowering=False, num_devices=1)
    arrays, tensors = {}, {}
    for name in _INS:
        a = _np.ascontiguousarray(inputs[name])
        arrays[f"in_{name}_dram"] = a
        tensors[name] = nc.dram_tensor(f"in_{name}_dram", a.shape, _mybir.dt.from_np(a.dtype), kind="ExternalInput").ap()
    out = nc.dram_tensor("out_0_dram", (1, SEQ, D), _mybir.dt.float32, kind="ExternalOutput").ap()
    program(nc, tensors, out)
    r = _run(nc, [arrays], core_ids=[0])
    return r.results[0]["out_0_dram"]
```
